# Optimizing a Trainium2 kernel written in Bass

```python
import jax, jax.numpy as jnp
from jax import lax
import numpy as np

D_MODEL = 1024
BATCH = 1
SEQ = 1024
DEPTH = 1

FFN_HIDDEN = 2816
H_A = 4
DK_A = 128
DV_A = 256
CONV_W = 4
CHUNK = 64
H_B = 8
DH_B = 128
SB_BLOCK = 128
PLE_DIM = 256
LN_EPS = 1e-5
DEEPNORM_ALPHA = (2 * DEPTH) ** 0.25
DEEPNORM_BETA = (8 * DEPTH) ** -0.25

A_QK_W = 2 * H_A * DK_A
A_V_W = H_A * DV_A
A_O_W = H_A * DV_A
B_QKV_W = 3 * H_B * DH_B
GATE_W = 2 * D_MODEL
SPLIT_IDX = list(np.cumsum([A_QK_W, A_V_W, A_O_W, H_A, H_A, B_QKV_W]))
N_IN = A_QK_W + A_V_W + A_O_W + 2 * H_A + B_QKV_W + GATE_W

kernel_name = "hybrid_mlstm_stickbreaking_macaron_deepnorm"

def layer_norm(x, g, b):
    xf = x.astype(jnp.float32)
    mu = jnp.mean(xf, axis=-1, keepdims=True)
    var = jnp.mean(jnp.square(xf - mu), axis=-1, keepdims=True)
    y = (xf - mu) * lax.rsqrt(var + LN_EPS) * g.astype(jnp.float32) + b.astype(jnp.float32)
    return y.astype(x.dtype)

def swiglu(x, wg, wu, wd):
    return (jax.nn.silu(x @ wg) * (x @ wu)) @ wd

def causal_conv(u, w, b):
    c = u.shape[-1]
    y = lax.conv_general_dilated(u, w[:, None, :], window_strides=(1,), padding=((CONV_W - 1, 0),),
                                 dimension_numbers=("NWC", "WIO", "NWC"), feature_group_count=c)
    return y + b

def head_norm(h, g):
    mu = jnp.mean(h, axis=-1, keepdims=True)
    var = jnp.mean(jnp.square(h - mu), axis=-1, keepdims=True)
    return (h - mu) * lax.rsqrt(var + LN_EPS) * g.astype(jnp.float32)

def mlstm_chunkwise(q, k, v, i_pre, log_f):
    bsz, s, h, dk = q.shape
    dv = v.shape[-1]
    nc = s // CHUNK
    f32 = jnp.float32
    qc = q.astype(f32).reshape(bsz, nc, CHUNK, h, dk).transpose(1, 0, 3, 2, 4)
    kc = k.astype(f32).reshape(bsz, nc, CHUNK, h, dk).transpose(1, 0, 3, 2, 4)
    vc = v.astype(f32).reshape(bsz, nc, CHUNK, h, dv).transpose(1, 0, 3, 2, 4)
    ic = i_pre.astype(f32).reshape(bsz, nc, CHUNK, h).transpose(1, 0, 3, 2)
    fc = log_f.astype(f32).reshape(bsz, nc, CHUNK, h).transpose(1, 0, 3, 2)
    tril = jnp.tril(jnp.ones((CHUNK, CHUNK), dtype=bool))

    def step(carry, inp):
        c_st, n_st, m_st = carry
        qb, kb, vb, ib, fb = inp
        bcum = jnp.cumsum(fb, axis=-1)
        dmat = jnp.where(tril, bcum[..., :, None] - bcum[..., None, :] + ib[..., None, :], -jnp.inf)
        inter = bcum + m_st[..., None]
        m_t = jnp.maximum(inter, jnp.max(dmat, axis=-1))
        w_inter = jnp.exp(inter - m_t)
        scores = jnp.einsum("bhtd,bhsd->bhts", qb, kb) * jnp.exp(dmat - m_t[..., None])
        num = w_inter[..., None] * jnp.einsum("bhtd,bhde->bhte", qb, c_st) + jnp.einsum("bhts,bhse->bhte", scores, vb)
        den = w_inter * jnp.einsum("bhtd,bhd->bht", qb, n_st) + jnp.sum(scores, axis=-1)
        h_out = num / jnp.maximum(jnp.abs(den), jnp.exp(-m_t))[..., None]
        b_last = bcum[..., -1]
        g = b_last[..., None] - bcum + ib
        m_new = jnp.maximum(b_last + m_st, jnp.max(g, axis=-1))
        a_prev = jnp.exp(b_last + m_st - m_new)
        w_in = jnp.exp(g - m_new[..., None])
        c_new = a_prev[..., None, None] * c_st + jnp.einsum("bhs,bhsd,bhse->bhde", w_in, kb, vb)
        n_new = a_prev[..., None] * n_st + jnp.einsum("bhs,bhsd->bhd", w_in, kb)
        return (c_new, n_new, m_new), h_out

    init = (jnp.zeros((bsz, h, dk, dv), f32), jnp.zeros((bsz, h, dk), f32), jnp.zeros((bsz, h), f32))
    _, hs = lax.scan(step, init, (qc, kc, vc, ic, fc))
    return hs.transpose(1, 0, 3, 2, 4).reshape(bsz, s, h, dv)

def stick_breaking_attention(q, k, v):
    bsz, s, h, dh = q.shape
    nq = s // SB_BLOCK
    scale = DH_B ** -0.5
    kt = k.transpose(0, 2, 1, 3)
    vt = v.transpose(0, 2, 1, 3)
    qblocks = q.transpose(0, 2, 1, 3).reshape(bsz, h, nq, SB_BLOCK, dh).transpose(2, 0, 1, 3, 4)
    s_pos = jnp.arange(s)

    def block(args):
        qb, bi = args
        z = jnp.einsum("bhtd,bhsd->bhts", qb, kt).astype(jnp.float32) * scale
        t_pos = bi * SB_BLOCK + jnp.arange(SB_BLOCK)
        mask = s_pos[None, :] < t_pos[:, None]
        log_keep = jnp.where(mask, -jax.nn.softplus(z), 0.0)
        later = lax.cumsum(log_keep, axis=3, reverse=True) - log_keep
        weights = jnp.where(mask, jnp.exp(jax.nn.log_sigmoid(z) + later), 0.0)
        return jnp.einsum("bhts,bhsd->bhtd", weights.astype(vt.dtype), vt)

    out = lax.map(block, (qblocks, jnp.arange(nq)))
    return out.transpose(1, 0, 3, 2, 4).reshape(bsz, s, h * dh)

def token_mix(x, w_in, b_in, b_forget, conv_w, conv_b, mh_norm_g, w_branch_a, w_branch_b, w_mix_out):
    bsz, s, _ = x.shape
    proj = x @ w_in + b_in
    qk_a, v_a, o_a, i_a, f_a, qkv_b, gates = jnp.split(proj, SPLIT_IDX, axis=-1)
    qk_a = jax.nn.silu(causal_conv(qk_a, conv_w, conv_b))
    q_a = qk_a[..., : A_QK_W // 2].reshape(bsz, s, H_A, DK_A)
    k_a = qk_a[..., A_QK_W // 2:].reshape(bsz, s, H_A, DK_A) * (DK_A ** -0.5)
    v_a = v_a.reshape(bsz, s, H_A, DV_A)
    log_f = jax.nn.log_sigmoid((f_a + b_forget).astype(jnp.float32))
    h_a = mlstm_chunkwise(q_a, k_a, v_a, i_a, log_f)
    y_a = (head_norm(h_a, mh_norm_g).reshape(bsz, s, A_V_W) * jax.nn.sigmoid(o_a.astype(jnp.float32))).astype(x.dtype)
    q_b, k_b, v_b = jnp.split(qkv_b, 3, axis=-1)
    y_b = stick_breaking_attention(q_b.reshape(bsz, s, H_B, DH_B), k_b.reshape(bsz, s, H_B, DH_B),
                                   v_b.reshape(bsz, s, H_B, DH_B)).astype(x.dtype)
    g_a, g_b = jnp.split(gates, 2, axis=-1)
    merged = jax.nn.sigmoid(g_a) * (y_a @ w_branch_a) + jax.nn.sigmoid(g_b) * (y_b @ w_branch_b)
    return merged @ w_mix_out

def setup_inputs(seed: int = 0) -> dict:
    key = jax.random.key(seed)
    ks = jax.random.split(key, 20)
    f32 = jnp.float32

    def dense(k, shape, fan_in, scale=1.0):
        return jax.random.normal(k, shape, f32) * (scale * fan_in ** -0.5)

    x = jax.random.normal(ks[0], (BATCH, SEQ, D_MODEL), f32)
    p = jax.random.normal(ks[1], (DEPTH, BATCH, SEQ, PLE_DIM), f32)
    ln_g = 1.0 + 0.02 * jax.random.normal(ks[2], (DEPTH, 4, D_MODEL), f32)
    ln_b = 0.02 * jax.random.normal(ks[3], (DEPTH, 4, D_MODEL), f32)
    ffn_wg = dense(ks[4], (DEPTH, 2, D_MODEL, FFN_HIDDEN), D_MODEL)
    ffn_wu = dense(ks[5], (DEPTH, 2, D_MODEL, FFN_HIDDEN), D_MODEL)
    ffn_wd = dense(ks[6], (DEPTH, 2, FFN_HIDDEN, D_MODEL), FFN_HIDDEN, DEEPNORM_BETA)
    w_in = dense(ks[7], (DEPTH, D_MODEL, N_IN), D_MODEL)
    b_in = 0.01 * jax.random.normal(ks[8], (DEPTH, N_IN), f32)
    b_forget = jnp.linspace(3.0, 6.0, H_A, dtype=f32)[None, :] + 0.1 * jax.random.normal(ks[9], (DEPTH, H_A), f32)
    conv_w = dense(ks[10], (DEPTH, CONV_W, A_QK_W), CONV_W)
    conv_b = 0.01 * jax.random.normal(ks[11], (DEPTH, A_QK_W), f32)
    mh_norm_g = 1.0 + 0.02 * jax.random.normal(ks[12], (DEPTH, H_A, DV_A), f32)
    w_branch_a = dense(ks[13], (DEPTH, A_V_W, D_MODEL), A_V_W)
    w_branch_b = dense(ks[14], (DEPTH, H_B * DH_B, D_MODEL), H_B * DH_B)
    w_mix_out = dense(ks[15], (DEPTH, D_MODEL, D_MODEL), D_MODEL, DEEPNORM_BETA)
    w_ple = dense(ks[16], (DEPTH, PLE_DIM, D_MODEL), PLE_DIM, DEEPNORM_BETA)
    w_ple_gate = dense(ks[17], (DEPTH, D_MODEL, D_MODEL), D_MODEL)
    b_ple_gate = 0.01 * jax.random.normal(ks[18], (DEPTH, D_MODEL), f32)
    return {"x": x, "p": p, "ln_g": ln_g, "ln_b": ln_b, "ffn_wg": ffn_wg, "ffn_wu": ffn_wu,
            "ffn_wd": ffn_wd, "w_in": w_in, "b_in": b_in, "b_forget": b_forget, "conv_w": conv_w,
            "conv_b": conv_b, "mh_norm_g": mh_norm_g, "w_branch_a": w_branch_a,
            "w_branch_b": w_branch_b, "w_mix_out": w_mix_out, "w_ple": w_ple,
            "w_ple_gate": w_ple_gate, "b_ple_gate": b_ple_gate}

def reference(x, p, ln_g, ln_b, ffn_wg, ffn_wu, ffn_wd, w_in, b_in, b_forget, conv_w, conv_b,
              mh_norm_g, w_branch_a, w_branch_b, w_mix_out, w_ple, w_ple_gate, b_ple_gate):
    for i in range(DEPTH):
        x = layer_norm(DEEPNORM_ALPHA * x + 0.5 * swiglu(x, ffn_wg[i, 0], ffn_wu[i, 0], ffn_wd[i, 0]),
                       ln_g[i, 0], ln_b[i, 0])
        mix = token_mix(x, w_in[i], b_in[i], b_forget[i], conv_w[i], conv_b[i], mh_norm_g[i],
                        w_branch_a[i], w_branch_b[i], w_mix_out[i])
        x = layer_norm(DEEPNORM_ALPHA * x + mix, ln_g[i, 1], ln_b[i, 1])
        x = layer_norm(DEEPNORM_ALPHA * x + 0.5 * swiglu(x, ffn_wg[i, 1], ffn_wu[i, 1], ffn_wd[i, 1]),
                       ln_g[i, 2], ln_b[i, 2])
        gate = jax.nn.sigmoid(x @ w_ple_gate[i] + b_ple_gate[i])
        x = layer_norm(DEEPNORM_ALPHA * x + gate * (p[i] @ w_ple[i]), ln_g[i, 3], ln_b[i, 3])
    return x


_drawn_inputs = setup_inputs


def setup_inputs(seed=0):
    import zlib

    import numpy as np

    out = dict(_drawn_inputs(seed))
    spreads = {}
    factors = {'b_in': 6.098, 'conv_b': 8.0, 'mh_norm_g': 31.255, 'b_ple_gate': 57.248}
    for name, (base, spread) in spreads.items():
        noise = np.random.default_rng([zlib.crc32(name.encode()), seed]).standard_normal(out[name].shape)
        drawn = base * np.exp(spread * noise) if base else spread * noise
        out[name] = __import__('jax').numpy.asarray(drawn.astype(out[name].dtype))
    for name, factor in factors.items():
        out[name] = (out[name] * factor).astype(out[name].dtype)
    return out
```

```python
import concourse.bass as bass
from concourse import mybir
from contextlib import ExitStack

F32 = mybir.dt.float32
F32R = mybir.dt.float32r
ACT = mybir.ActivationFunctionType
ALU = mybir.AluOpType

P = 128
D = 1024
T = 1024
KC = D // P
TT = T // P
PC = 1024
FFN_F = 2816
FC = FFN_F // P
FI = FC // 2
H_A, DK_A, DV_A, CONV_W = 4, 128, 256, 4
H_B, DH_B = 8, 128
NAT = 3072
NG = NAT // 512
NQA = 2 * H_A
NTC = 34
TC_Q, TC_K, TC_GA, TC_GB, TC_I, TC_F = 0, 8, 16, 24, 32, 33
EPS = 1e-5
ALPHA = 2.0 ** 0.25

N_START = 2 + 2 + KC
B_FFN1 = N_START
B_NAT = B_FFN1 + 6 * FI
B_QA = B_NAT + 4 * NG
B_TC = B_QA + NQA
B_BR = B_TC + NTC
B_MIX = B_BR + 2 * 2 * KC
B_FFN2 = B_MIX + KC
B_PLE = B_FFN2 + 6 * FI
N_PIECES = B_PLE + KC


def triangle_units(descending, strict):
    out = []
    for half in range(2):
        blocks = range(4 * half + 4)
        for sb in (reversed(blocks) if descending else blocks):
            t0 = max(sb * P, 512 * half)
            out.append((half, sb, t0, 512 * (half + 1) - t0, sb >= 4 * half))
    return out


def build(nc, w_all, x_nat, b_t, b_qa, b_nat, b_if, conv_w, conv_b, mh_g, ln_g, ln_b, b_ple, out,
          s_ple, s_x, s_nat, s_qa, s_t, s_m, s_h, s_ya, s_yb):
    ctx = ExitStack()
    with ctx:
        FP = ctx.enter_context(nc.sbuf_tensor("fp", [P, 15900], F32))
        RP = ctx.enter_context(nc.sbuf_tensor("rp", [P, 37120], F32R))
        PS = [ctx.enter_context(nc.psum_tensor(f"bank{b}", [P, 512], F32)) for b in range(8)]
        made = {}

        def sem(name):
            if name not in made:
                made[name] = ctx.enter_context(nc.semaphore(name))
            return made[name]

        def fv(base, n, **kw):
            return FP[:, base:base + n]

        def rv(base, n):
            return RP[:, base:base + n]

        raw = [fv(0, PC), fv(PC, PC)]
        ident = fv(2048, P)
        stats = FP[:, 2176:2176 + 96].rearrange("p (t s) -> p t s", t=TT)
        mv = FP[:, 2272:2288].rearrange("p (t s) -> p t s", t=TT)
        rstd = fv(2288, TT)
        bt_col = fv(2296, NTC)
        bqa_col = fv(2330, NQA)
        cw_col = FP[:, 2338:2338 + 4 * NQA].rearrange("p (c j) -> p c j", j=CONV_W)
        cb_col = fv(2370, NQA)
        a_col = FP[:, 2378:2378 + 32].rearrange("p (h t) -> p h t", h=H_A)
        e_col = FP[:, 2410:2410 + 32].rearrange("p (h t) -> p h t", h=H_A)
        a_head = fv(2442, TT)
        e_head = fv(2450, TT)
        small = fv(2458, 64)
        bf_col = fv(2522, 1)
        ve = fv(2524, TT)
        X0 = 2688
        X = FP[:, X0:X0 + 8192].rearrange("p (t n) -> p t n", t=TT)
        G0 = X0 + 8192
        lng_t, lnb_t = fv(G0, D), fv(G0 + D, D)
        T0 = G0 + 2048
        W0 = X0

        XH = RP[:, 0:8192].rearrange("p (k n) -> p k n", k=KC)
        XL = RP[:, 8192:16384].rearrange("p (k n) -> p k n", k=KC)
        R2 = 16384
        R3 = 32768
        TRI = rv(36864, P)
        TRIC = rv(36992, P)

        def seg(base):
            return rv(base, PC), rv(base + PC, PC)

        raw_in = [sem("raw_in0"), sem("raw_in1")]
        w_hi = sem("w_hi")
        w_split = sem("w_split")

        block = ctx.enter_context(nc.Block())

        def apart(eng):
            eng.sem_inc(sem("passed"), 1)

        def load_pair(sp, j):
            for s in range(2):
                sp.wait_ge(w_split, 2 * j + s - 1)
                sp.dma_start(raw[s], w_all[2 * j + s]).then_inc(raw_in[s], 16)

        def split_piece(pool, n, s, count, hi, lo):
            pool.wait_ge(raw_in[s], 16 * count + 16)
            apart(pool)
            nc.gpsimd.tensor_copy(hi, raw[s]).then_inc(w_hi, 1)
            pool.wait_ge(w_hi, n + 1)
            nc.gpsimd.tensor_tensor(lo, raw[s], hi, ALU.subtract).then_inc(w_split, 1)

        def three(pe, ps, lh, ll, rh, rl, start, stop, skip=False):
            nc.tensor.matmul(ps, lh, rh, start=start, stop=False, skip_group_check=skip)
            nc.tensor.matmul(ps, lh, rl, start=False, stop=False, skip_group_check=skip)
            return nc.tensor.matmul(ps, ll, rh, start=False, stop=stop, skip_group_check=skip)

        PTH = RP[:, R3:R3 + 2048].rearrange("p (k n) -> p k n", k=2)
        PTL = RP[:, R3 + 2048:R3 + 4096].rearrange("p (k n) -> p k n", k=2)
        WPH = RP[:, R2:R2 + 2048].rearrange("p (k n) -> p k n", k=2)
        WPL = RP[:, R2 + 2048:R2 + 4096].rearrange("p (k n) -> p k n", k=2)
        stage4 = [fv(T0 + 512 * i, 512) for i in range(4)]

        def start_pool(pool):
            nc.gpsimd.memset(ident, 0.0).then_inc(sem("const"), 1)
            nc.gpsimd.memset(fv(G0, P), 1.0).then_inc(sem("const"), 1)
            pool.wait_ge(sem("const"), 2)
            nc.gpsimd.affine_select(out=ident, in_=ident, compare_op=ALU.not_equal, fill=1.0, base=0,
                                    pattern=[[-1, P]], channel_multiplier=1).then_inc(sem("const"), 1)
            nc.gpsimd.affine_select(out=TRI, in_=fv(G0, P), compare_op=ALU.is_ge, fill=0.0, base=0,
                                    pattern=[[-1, P]], channel_multiplier=1).then_inc(sem("const"), 1)
            nc.gpsimd.affine_select(out=TRIC, in_=fv(G0, P), compare_op=ALU.is_gt, fill=0.0, base=0,
                                    pattern=[[1, P]], channel_multiplier=-1).then_inc(sem("const"), 1)
            pool.wait_ge(sem("const"), 5)
            for n in range(N_START):
                if n < 4:
                    hi, lo = ((PTH, PTL) if n < 2 else (WPH, WPL))
                    hi, lo = hi[:, n % 2, :], lo[:, n % 2, :]
                else:
                    hi, lo = XH[:, n - 4, :], XL[:, n - 4, :]
                split_piece(pool, n, n % 2, n // 2, hi, lo)

        def start_tensor(pe):
            pe.wait_ge(w_split, 4)
            for o in range(16):
                tt, dh = o // 2, o % 2
                if o >= 8:
                    pe.wait_ge(sem("st_evac"), o - 7)
                for k in range(2):
                    l, r = slice(tt * P, tt * P + P), slice(dh * 512, dh * 512 + 512)
                    last = three(pe, PS[o % 8][:, :], PTH[:, k, l], PTL[:, k, l],
                                 WPH[:, k, r], WPL[:, k, r], k == 0, k == 1)
                last.then_inc(sem("st_done"), 1)

        def start_scalar(act):
            act.dma_start(X, x_nat).then_inc(sem("x_in"), 16)
            small_loads = [(bt_col, b_t), (bqa_col, b_qa), (cw_col, conv_w), (cb_col, conv_b),
                           (FP[0:H_A, 2522:2523], b_if)]
            for dst, src in small_loads:
                act.dma_start(dst, src).then_inc(sem("small_in"), 16)
            for o in range(16):
                act.wait_ge(sem("st_done"), o + 1)
                if o >= 4:
                    act.wait_ge(sem(f"st_out{o % 4}"), 16 * (o // 4))
                nc.scalar.copy(stage4[o % 4], PS[o % 8][:, :]).then_inc(sem("st_evac"), 1)
                act.wait_ge(sem("st_evac"), o + 1)
                act.dma_start(s_ple[o // 2 * P:o // 2 * P + P, o % 2 * 512:o % 2 * 512 + 512],
                              stage4[o % 4]).then_inc(sem(f"st_out{o % 4}"), 16)
            act.wait_ge(sem("x_in"), 16)
            scale_x(act)
            for n in range(4):
                act.wait_ge(sem(f"st_out{n}"), 64)

        def scale_x(act):
            for tt in range(TT):
                nc.scalar.mul(X[:, tt, :], X[:, tt, :], ALPHA).then_inc(sem("x_scaled"), 1)

        fseg = [seg(R2 + 2048 * s) for s in range(6)]
        HH = RP[:, R2 + 12288:R2 + 14336].rearrange("p (f h n) -> p f h n", f=2, h=2)
        HL = RP[:, R2 + 14336:R2 + 16384].rearrange("p (f h n) -> p f h n", f=2, h=2)
        silu_t = [fv(T0 + 512 * i, 512) for i in range(2)]
        prod_t = [fv(T0 + 1024 + 512 * i, 512) for i in range(2)]
        UNITS = [(0, 0), (1, 0), (0, 1), (1, 1)]

        def ffn_pool(pool, r, base, free):
            u4, u16 = 4 * FI * r, 16 * FI * r
            for s, v in free:
                pool.wait_ge(s, v)
            with pool.Fori(0, FI) as i:
                for s in range(6):
                    if s < 4:
                        pool.wait_ge(sem("f_unit_done"), u4 + 4 * i + 3 + s // 2)
                    else:
                        pool.wait_ge(sem("f_down_done"), u16 + 16 * i + 16)
                    split_piece(pool, base + 6 * i + s, s % 2, base // 2 + 3 * i + s // 2, *fseg[s])

        def ffn_tensor(pe, r, base, ready):
            u4, u16 = 4 * FI * r, 16 * FI * r
            for s, v in ready:
                pe.wait_ge(s, v)
            if r == 0:
                pe.sem_inc(sem("f_unit_done"), 4)
                pe.sem_inc(sem("f_down_done"), 16)
            with pe.Fori(0, FI) as i:
                for u, (f, h) in enumerate(UNITS):
                    if h == 0:
                        pe.wait_ge(w_split, base + 6 * i + 2 * f + 2)
                    pe.wait_ge(sem("f_prod"), u4 + 4 * i + u + 1)
                    for g in range(2):
                        wh, wl = fseg[2 * f + g]
                        for k in range(KC):
                            c = slice(k * P, k * P + P)
                            t = slice(h * 512, h * 512 + 512)
                            last = three(pe, PS[2 * (u % 2) + g][:, :], wh[:, c], wl[:, c],
                                         XH[:, k, t], XL[:, k, t], k == 0, k == KC - 1)
                    last.then_inc(sem("f_unit_done"), 1)
                pe.wait_ge(w_split, base + 6 * i + 6)
                for o in range(16):
                    h, tl, dh = o // 8, o // 2 % 4, o % 2
                    if o % 8 == 0:
                        pe.wait_ge(sem("f_h_lo"), u4 + 4 * i + 2 + 2 * h)
                    pe.wait_ge(sem("f_down_evac"), u16 + 16 * i + o + 1)
                    for f in range(2):
                        t = slice(tl * P, tl * P + P)
                        c = slice(dh * 512, dh * 512 + 512)
                        wh, wl = fseg[4 + f]
                        last = three(pe, PS[4 + o % 4][:, :], HH[:, f, h, t], HL[:, f, h, t],
                                     wh[:, c], wl[:, c], f == 0, f == 1)
                    last.then_inc(sem("f_down_done"), 1)

        def ffn_scalar(act, r):
            u4, u16 = 4 * FI * r, 16 * FI * r
            with act.Fori(0, FI) as i:
                for u, (f, h) in enumerate(UNITS):
                    act.wait_ge(sem("f_unit_done"), u4 + 4 * i + u + 5)
                    act.wait_ge(sem("f_prod"), u4 + 4 * i + u + 1)
                    nc.scalar.activation(silu_t[u % 2], PS[2 * (u % 2)][:, :], ACT.Silu)\
                        .then_inc(sem("f_silu"), 1)
                    act.wait_ge(sem("f_prod"), u4 + 4 * i + u + 3)
                    act.wait_ge(sem("f_down_done"), u16 + 16 * i + 8 + 8 * h)
                    nc.scalar.copy(HH[:, f, h, :], prod_t[u % 2]).then_inc(sem("f_h_hi"), 1)

        def ffn_vector(dve, r, x_ready):
            u4, u16 = 4 * FI * r, 16 * FI * r
            if r == 0:
                dve.sem_inc(sem("f_prod"), 2)
                dve.sem_inc(sem("f_down_evac"), 4)
            for s, v in x_ready:
                dve.wait_ge(s, v)
            with dve.Fori(0, FI) as i:
                for u, (f, h) in enumerate(UNITS):
                    dve.wait_ge(sem("f_silu"), u4 + 4 * i + u + 1)
                    nc.vector.tensor_tensor(prod_t[u % 2], silu_t[u % 2], PS[2 * (u % 2) + 1][:, :], ALU.mult)\
                        .then_inc(sem("f_prod"), 1)
                    dve.wait_ge(sem("f_h_hi"), u4 + 4 * i + u + 1)
                    nc.vector.tensor_tensor(HL[:, f, h, :], prod_t[u % 2], HH[:, f, h, :], ALU.subtract)\
                        .then_inc(sem("f_h_lo"), 1)
                for o in range(16):
                    h, tl, dh = o // 8, o // 2 % 4, o % 2
                    xs = X[:, 4 * h + tl, dh * 512:dh * 512 + 512]
                    dve.wait_ge(sem("f_down_done"), u16 + 16 * i + o + 17)
                    nc.vector.scalar_tensor_tensor(out=xs, in0=PS[4 + o % 4][:, :], scalar=0.5, in1=xs,
                                                   op0=ALU.mult, op1=ALU.add).then_inc(sem("f_down_evac"), 1)

        def ln_vector(dve, r, ready, transposed=True):
            for s, v in ready:
                dve.wait_ge(s, v)
            for tt in range(TT):
                for h in range(2):
                    nc.vector.bn_stats(stats[:, tt, 6 * h:6 * h + 6], X[:, tt, 512 * h:512 * h + 512])\
                        .then_inc(sem("ln_st"), 1)
            for tt in range(TT):
                dve.wait_ge(sem("ln_st"), 16 * r + 2 * tt + 2)
                nc.vector.bn_aggr(mv[:, tt, :], stats[:, tt, :]).then_inc(sem("ln_mv"), 1)
            dve.wait_ge(sem("ln_mv"), 8 * r + TT)
            nc.vector.tensor_scalar(ve, mv[:, :, 1], EPS, None, ALU.add).then_inc(sem("ln_ve"), 1)
            dve.wait_ge(sem("ln_sd"), 1 * r + 1)
            nc.vector.reciprocal(rstd, ve).then_inc(sem("ln_rstd"), 1)
            dve.wait_ge(sem("ln_rstd"), 1 * r + 1)
            dve.wait_ge(sem("ln_gb_in"), 32 * r + 32)

            def centre(tt):
                nc.vector.scalar_tensor_tensor(out=X[:, tt, :], in0=X[:, tt, :], scalar=mv[:, tt, 0:1], in1=lng_t,
                                               op0=ALU.subtract, op1=ALU.mult).then_inc(sem("ln_ctr"), 1)

            def low(g):
                tt, j = g // 2, g % 2
                dve.wait_ge(sem("ln_tr_hi"), 16 * r + g + 1)
                k = slice(4 * j, 4 * j + 4)
                nc.vector.tensor_tensor(XL[:, k, tt * P:tt * P + P],
                                        PS[g % 4][:, :].rearrange("p (k n) -> p k n", k=4),
                                        XH[:, k, tt * P:tt * P + P], ALU.subtract).then_inc(sem("ln_tr_lo"), 1)

            centre(0)
            for tt in range(TT):
                if tt + 1 < TT:
                    centre(tt + 1)
                dve.wait_ge(sem("ln_ctr"), 8 * r + tt + 1)
                nc.vector.scalar_tensor_tensor(out=X[:, tt, :], in0=X[:, tt, :], scalar=rstd[:, tt:tt + 1], in1=lnb_t,
                                               op0=ALU.mult, op1=ALU.add).then_inc(sem("ln_y"), 1)
                if transposed and tt >= 1:
                    low(2 * tt - 2)
                    low(2 * tt - 1)
            if transposed:
                low(2 * TT - 2)
                low(2 * TT - 1)

        def ln_tensor(pe, r, banks_free):
            for s, v in banks_free:
                pe.wait_ge(s, v)
            for g in range(2 * TT):
                tt, j = g // 2, g % 2
                pe.wait_ge(sem("ln_y"), 8 * r + tt + 1)
                if g >= 4:
                    pe.wait_ge(sem("ln_tr_lo"), 16 * r + g - 3)
                for k in range(4):
                    last = nc.tensor.transpose(PS[g % 4][:, k * P:k * P + P],
                                               X[:, tt, (4 * j + k) * P:(4 * j + k) * P + P], ident)
                last.then_inc(sem("ln_tr"), 1)

        def ln_loads(act, r, free):
            for s, v in free:
                act.wait_ge(s, v)
            act.dma_start(lng_t, ln_g[r].partition_broadcast(P)).then_inc(sem("ln_gb_in"), 16)
            act.dma_start(lnb_t, ln_b[r].partition_broadcast(P)).then_inc(sem("ln_gb_in"), 16)

        def ln_scalar(act, r, rx_free, transposed=True):
            act.wait_ge(sem("ln_ve"), 1 * r + 1)
            nc.scalar.sqrt(ve, ve).then_inc(sem("ln_sd"), 1)
            for s, v in rx_free:
                act.wait_ge(s, v)
            if transposed:
                for g in range(2 * TT):
                    tt, j = g // 2, g % 2
                    act.wait_ge(sem("ln_tr"), 16 * r + g + 1)
                    nc.scalar.copy(XH[:, 4 * j:4 * j + 4, tt * P:tt * P + P],
                                   PS[g % 4][:, :].rearrange("p (k n) -> p k n", k=4)).then_inc(sem("ln_tr_hi"), 1)

        def nseg(kh):
            b = R2 + 4096 * kh
            return (RP[:, b:b + 2048].rearrange("p (k n) -> p k n", k=4),
                    RP[:, b + 2048:b + 4096].rearrange("p (k n) -> p k n", k=4))
        bias_nat = fv(X0, NAT)

        def nat_pool(pool, free):
            for s, v in free:
                pool.wait_ge(s, v)
            with pool.Fori(0, NG) as i:
                for s in range(4):
                    hi, lo = nseg(s // 2)
                    k = 2 * (s % 2)
                    if s % 2 == 0:
                        pool.wait_ge(sem("n_half"), 2 * i + 1 + s // 2)
                    split_piece(pool, B_NAT + 4 * i + s, s % 2, B_NAT // 2 + 2 * i + s // 2,
                                hi[:, k:k + 2, :].rearrange("p k n -> p (k n)"),
                                lo[:, k:k + 2, :].rearrange("p k n -> p (k n)"))

        def nat_tensor(pe, ready):
            for s, v in ready:
                pe.wait_ge(s, v)
            pe.sem_inc(sem("n_half"), 2)
            with pe.Fori(0, NG) as i:
                for kh in range(2):
                    pe.wait_ge(w_split, B_NAT + 4 * i + 2 + 2 * kh)
                    wh, wl = nseg(kh)
                    for tt in range(TT):
                        if kh == 0:
                            pe.wait_ge(sem("n_evac"), 8 * i + tt + 1)
                        for k in range(4):
                            t = slice(tt * P, tt * P + P)
                            last = three(pe, PS[tt][:, :], XH[:, 4 * kh + k, t], XL[:, 4 * kh + k, t],
                                         wh[:, k, :], wl[:, k, :], kh == 0 and k == 0, kh == 1 and k == 3)
                        if kh == 1:
                            last.then_inc(sem("n_done"), 1)
                    if kh == 0:
                        last.then_inc(sem("n_half"), 1)
                    else:
                        pe.wait_ge(sem("n_done"), 8 * i + 8)
                        pe.sem_inc(sem("n_half"), 1)

        def nat_vector(dve):
            dve.sem_inc(sem("n_evac"), 8)
            dve.wait_ge(sem("bnat_in"), 16)
            with dve.Fori(0, NG) as i:
                for tt in range(TT):
                    dve.wait_ge(sem("n_done"), 8 * i + tt + 1)
                    dve.wait_ge(sem(f"n_out{tt % 4}"), 32 * i + 16 * (tt // 4))
                    nc.vector.tensor_tensor(stage4[tt % 4], PS[tt][:, :], bias_nat[:, bass.ts(i, 512)], ALU.add)\
                        .then_inc(sem("n_evac"), 1)

        def nat_scalar(act):
            act.wait_ge(sem("ln_y"), TT)
            act.dma_start(s_x, X).then_inc(sem("x_out"), 16)
            act.wait_ge(sem("x_out"), 16)
            act.wait_ge(sem("ln_tr"), 2 * TT)
            act.dma_start(bias_nat, b_nat.partition_broadcast(P)).then_inc(sem("bnat_in"), 16)
            with act.Fori(0, NG) as i:
                for tt in range(TT):
                    act.wait_ge(sem("n_evac"), 8 * i + tt + 9)
                    act.dma_start(s_nat[tt * P:tt * P + P, bass.ts(i, 512)], stage4[tt % 4])\
                        .then_inc(sem(f"n_out{tt % 4}"), 16)

        cseg = [seg(R3 + 2048 * j) for j in range(2)]
        UP = W0 + 3072
        u_pad = [fv(UP + 1028 * j, 1027) for j in range(2)]
        conv_t = [fv(UP + 2056 + 1024 * j, 1024) for j in range(2)]
        conv_o = [fv(UP + 4104 + 1024 * j, 1024) for j in range(2)]

        def chunk_pool(pool, q, base, n, free):
            for s, v in free:
                pool.wait_ge(s, v)
            with pool.Fori(0, n // 2) as i:
                for j in range(2):
                    pool.wait_ge(sem(q + "done"), 4 * i + 2 * j + 2)
                    split_piece(pool, base + 2 * i + j, j, base // 2 + i, *cseg[j])

        def chunk_tensor(pe, q, base, n, ready):
            for s, v in ready:
                pe.wait_ge(s, v)
            pe.sem_inc(sem(q + "done"), 4)
            with pe.Fori(0, n // 2) as i:
                for j in range(2):
                    wh, wl = cseg[j]
                    pe.wait_ge(w_split, base + 2 * i + j + 1)
                    for h in range(2):
                        pe.wait_ge(sem(q + f"evac{h}"), 2 * i + j + 1)
                        for k in range(KC):
                            c, t = slice(k * P, k * P + P), slice(h * 512, h * 512 + 512)
                            last = three(pe, PS[2 * j + h][:, :], wh[:, c], wl[:, c], XH[:, k, t], XL[:, k, t],
                                         k == 0, k == KC - 1)
                        last.then_inc(sem(q + "done"), 1)

        def qa_vector(dve):
            dve.wait_ge(sem("n_out3"), 16 * 2 * NG)
            for j in range(2):
                nc.vector.memset(u_pad[j][:, 0:3], 0.0).then_inc(sem("qa_zero"), 1)
            dve.wait_ge(sem("qa_zero"), 2)
            dve.wait_ge(sem("small_in"), 80)
            with dve.Fori(0, NQA // 2) as i:
                for j in range(2):
                    dve.wait_ge(sem("qa_evac0"), 2 * i + j + 3)
                    dve.wait_ge(sem("qa_evac1"), 2 * i + j + 3)
                    dve.wait_ge(sem("qa_silu"), 2 * i + j + 1)
                    nc.vector.tensor_scalar(conv_t[j], u_pad[j][:, 0:T], cw_col[:, 2 * i + j, 0:1],
                                            cb_col[:, bass.ds(2 * i + j, 1)], ALU.mult, ALU.add)\
                        .then_inc(sem("qa_conv"), 1)
                    for w in range(1, CONV_W):
                        dve.wait_ge(sem("qa_conv"), 8 * i + 4 * j + w)
                        nc.vector.scalar_tensor_tensor(out=conv_t[j], in0=u_pad[j][:, w:w + T],
                                                       scalar=cw_col[:, 2 * i + j, w:w + 1], in1=conv_t[j],
                                                       op0=ALU.mult, op1=ALU.add).then_inc(sem("qa_conv"), 1)

        def qa_scalar(act):
            act.sem_inc(sem("qa_evac0"), 2)
            act.sem_inc(sem("qa_evac1"), 2)
            act.sem_inc(sem("qa_silu"), 2)
            act.wait_ge(sem("small_in"), 80)
            with act.Fori(0, NQA // 2) as i:
                for j in range(2):
                    for h in range(2):
                        act.wait_ge(sem("qa_done"), 4 * i + 2 * j + h + 5)
                        if h == 0:
                            act.wait_ge(sem("qa_conv"), 8 * i)
                        apart(act)
                        nc.scalar.activation(u_pad[j][:, 3 + 512 * h:515 + 512 * h], PS[2 * j + h][:, :],
                                             ACT.Identity, bias=bqa_col[:, bass.ds(2 * i + j, 1)])\
                            .then_inc(sem(f"qa_evac{h}"), 1)
                for j in range(2):
                    act.wait_ge(sem("qa_conv"), 8 * i + 4 * j + 4)
                    act.wait_ge(sem(f"qa_out{j}"), 16 * i)
                    nc.scalar.activation(conv_o[j], conv_t[j], ACT.Silu).then_inc(sem("qa_silu"), 1)
                    act.wait_ge(sem("qa_silu"), 2 * i + j + 3)
                    act.dma_start(s_qa[2 * i + j], conv_o[j]).then_inc(sem(f"qa_out{j}"), 16)

        TS0 = UP + 6152
        t_stage = [fv(TS0 + 1024 * j, 1024) for j in range(2)]

        def tc_vector(dve):
            dve.sem_inc(sem("tc_evac1"), 2)
            for s in range(4):
                dve.wait_ge(sem(f"n_out{s}"), 16 * 2 * NG)
            with dve.Fori(0, NTC // 2) as i:
                for j in range(2):
                    dve.wait_ge(sem("tc_done"), 4 * i + 2 * j + 6)
                    dve.wait_ge(sem(f"tc_out{j}"), 16 * i)
                    nc.vector.tensor_scalar(t_stage[j][:, 512:1024], PS[2 * j + 1][:, :],
                                            bt_col[:, bass.ds(2 * i + j, 1)], None, ALU.add)\
                        .then_inc(sem("tc_evac1"), 1)

        def tc_scalar(act):
            act.sem_inc(sem("tc_evac0"), 2)
            for s in range(4):
                act.wait_ge(sem(f"n_out{s}"), 16 * 2 * NG)
            with act.Fori(0, NTC // 2) as i:
                for j in range(2):
                    act.wait_ge(sem("tc_done"), 4 * i + 2 * j + 5)
                    act.wait_ge(sem(f"tc_out{j}"), 16 * i)
                    apart(act)
                    nc.scalar.activation(t_stage[j][:, 0:512], PS[2 * j][:, :], ACT.Identity,
                                         bias=bt_col[:, bass.ds(2 * i + j, 1)]).then_inc(sem("tc_evac0"), 1)
                    act.wait_ge(sem("tc_evac0"), 2 * i + j + 3)
                    act.wait_ge(sem("tc_evac1"), 2 * i + j + 3)
                    act.dma_start(s_t[2 * i + j], t_stage[j]).then_inc(sem(f"tc_out{j}"), 16)

        GR = W0
        gate = [FP[0:H_A, GR + 1024 * n:GR + 1024 * n + 1024] for n in range(8)]
        g_i, g_f, g_t, g_u, g_F, g_a, g_M, g_e = gate

        def gates_sync(sp):
            for j in range(2):
                sp.wait_ge(sem(f"tc_out{j}"), 16 * (NTC // 2))
            sp.wait_ge(sem("qa_out0"), 16 * (NQA // 2))
            sp.wait_ge(sem("qa_out1"), 16 * (NQA // 2))
            sp.dma_start(g_i, s_t[TC_I][0:H_A, :]).then_inc(sem("g_in"), 16)
            sp.dma_start(g_f, s_t[TC_F][0:H_A, :]).then_inc(sem("g_in"), 16)

        def gates_vector(dve):
            n = [0]

            def link(ins):
                n[0] += 1
                ins.then_inc(sem("g_v"), 1)
                dve.wait_ge(sem("g_v"), n[0])
            dve.wait_ge(sem("g_in"), 32)
            dve.wait_ge(sem("small_in"), 80)
            link(nc.vector.tensor_scalar(g_f, g_f, bf_col[0:H_A, :], None, ALU.add))
            dve.wait_ge(sem("g_act"), 3)
            link(nc.vector.scalar_tensor_tensor(out=g_u, in0=g_f, scalar=0.0, in1=g_t, op0=ALU.min,
                                                op1=ALU.subtract))
            link(nc.vector.memset(g_t, 0.0))
            link(nc.vector.tensor_tensor_scan(out=g_F, data0=g_u, data1=g_t, initial=0.0, op0=ALU.add, op1=ALU.add))
            link(nc.vector.tensor_tensor(g_a, g_i, g_F, ALU.subtract))
            link(nc.vector.tensor_tensor_scan(out=g_M, data0=g_a, data1=g_a, initial=0.0, op0=ALU.max, op1=ALU.max))
            link(nc.vector.tensor_tensor(g_u, g_F, g_M, ALU.add))
            dve.wait_ge(sem("g_tr"), 1)
            nc.vector.tensor_copy(a_col.rearrange("p h t -> p t h"),
                                  PS[0][:, 0:32].rearrange("p (t h) -> p t h", h=H_A)).then_inc(sem("g_col"), 1)
            nc.vector.tensor_copy(e_col.rearrange("p h t -> p t h"),
                                  PS[0][:, 32:64].rearrange("p (t h) -> p t h", h=H_A)).then_inc(sem("g_col"), 1)

        def gates_scalar(act):
            act.wait_ge(sem("g_v"), 1)
            nc.scalar.activation(g_t, g_f, ACT.Abs).then_inc(sem("g_act"), 1)
            act.wait_ge(sem("g_act"), 1)
            nc.scalar.activation(g_u, g_t, ACT.Exp, scale=-1.0).then_inc(sem("g_act"), 1)
            act.wait_ge(sem("g_act"), 2)
            nc.scalar.activation(g_t, g_u, ACT.Ln, bias=1.0).then_inc(sem("g_act"), 1)
            act.wait_ge(sem("g_v"), 7)
            nc.scalar.activation(g_e, g_u, ACT.Exp, scale=-1.0).then_inc(sem("g_act"), 1)
            act.dma_start(s_m, g_M).then_inc(sem("m_out"), 16)

        def gates_tensor(pe):
            pe.wait_ge(sem("g_act"), 4)
            pe.wait_ge(sem("tc_evac0"), NTC + 2)
            pe.wait_ge(sem("tc_evac1"), NTC + 2)
            for n, src in enumerate((g_a, g_e)):
                for tt in range(TT):
                    last = nc.tensor.transpose(PS[0][:, 32 * n + 4 * tt:32 * n + 4 * tt + 4],
                                               src[:, tt * P:tt * P + P], ident[0:H_A, 0:H_A])
            last.then_inc(sem("g_tr"), 1)

        MU = triangle_units(False, False)
        NMU = len(MU)
        MQ = W0 + 8192
        m_q, m_k = fv(W0, 1024), fv(W0 + 1024, 1024)
        m_v = FP[:, W0 + 2048:W0 + 4096].rearrange("p (s n) -> p s n", s=TT)
        m_M = fv(W0 + 4096, 1024)
        m_D = [fv(W0 + 5120 + 512 * j, 512) for j in range(2)]
        m_P = [fv(W0 + 6144 + 512 * j, 512) for j in range(2)]
        m_H = [fv(W0 + 8192 + 256 * j, 256) for j in range(4)]
        QH, QL, KH, KL = (rv(R2 + 1024 * n, 1024) for n in range(4))
        VW = DV_A + 2
        VH = RP[:, R2 + 4096:R2 + 4096 + TT * VW].rearrange("p (s n) -> p s n", s=TT)
        VL = RP[:, R2 + 4096 + TT * VW:R2 + 4096 + 2 * TT * VW].rearrange("p (s n) -> p s n", s=TT)
        PB = R2 + 4096 + 2 * TT * VW
        PHt = [rv(PB + 512 * j, 512) for j in range(2)]
        PLt = [rv(PB + 1024 + 512 * j, 512) for j in range(2)]

        def ml_sync(sp):
            sp.wait_ge(sem("g_v"), 7)
            sp.wait_ge(sem("g_act"), 4)
            sp.wait_ge(sem("g_tr"), 1)
            sp.wait_ge(sem("m_out"), 16)
            for s in range(4):
                sp.wait_ge(sem(f"n_out{s}"), 16 * 2 * NG)
            with sp.Fori(0, H_A) as i:
                sp.wait_ge(sem("ml_split"), 3 * i)
                sp.dma_start(m_q, s_qa[i]).then_inc(sem("ml_in"), 16)
                sp.dma_start(m_k, s_qa[i + H_A]).then_inc(sem("ml_in"), 16)
                sp.dma_start(m_v, s_nat[:, bass.ts(i, DV_A)].rearrange("(s p) n -> p s n", p=P))\
                    .then_inc(sem("ml_in"), 16)
                sp.wait_ge(sem("ml_d"), NMU * i)
                sp.dma_start(m_M, s_m[i].partition_broadcast(P)).then_inc(sem("ml_M_in"), 16)

        def ml_pool(pool):
            pool.wait_ge(sem("tc_done"), 2 * NTC + 4)
            nc.gpsimd.memset(VL[:, :, DV_A:VW].bitcast(F32), 0.0).then_inc(sem("ml_one"), 1)
            nc.gpsimd.memset(VH[:, :, DV_A + 1:VW].bitcast(F32), 0.0).then_inc(sem("ml_one"), 1)
            nc.gpsimd.memset(VH[:, :, DV_A:DV_A + 1].bitcast(F32), 1.0).then_inc(sem("ml_one"), 1)
            with pool.Fori(0, H_A) as i:
                pool.wait_ge(sem("ml_in"), 48 * i + 48)
                pool.wait_ge(sem("ml_pv"), NMU * i + 2)
                for n, (src, hi, lo) in enumerate([(m_q, QH, QL), (m_k, KH, KL),
                                                   (m_v, VH[:, :, 0:DV_A], VL[:, :, 0:DV_A])]):
                    apart(pool)
                    nc.gpsimd.tensor_copy(hi, src).then_inc(sem("ml_hi"), 1)
                    pool.wait_ge(sem("ml_hi"), 3 * i + n + 1)
                    nc.gpsimd.tensor_tensor(lo, src, hi, ALU.subtract).then_inc(sem("ml_split"), 1)
                dg = 0
                for u, (h, sb, t0, n, diag) in enumerate(MU):
                    if diag:
                        pool.wait_ge(sem("ml_d"), NMU * i + u + 1)
                        apart(pool)
                        nc.gpsimd.affine_select(out=m_D[u % 2][:, 0:P], in_=m_D[u % 2][:, 0:P],
                                                compare_op=ALU.is_ge, fill=0.0, base=0, pattern=[[1, P]],
                                                channel_multiplier=-1).then_inc(sem("ml_mask"), 1)

        def ml_tensor(pe):
            pe.sem_inc(sem("ml_pv"), 2)
            pe.wait_ge(sem("g_col"), 2)
            pe.wait_ge(sem("ml_one"), 3)
            with pe.Fori(0, H_A) as i:
                def score(u):
                    h, sb, t0, n, diag = MU[u]
                    pe.wait_ge(sem("ml_p"), NMU * i + u + 1)
                    s, t = slice(sb * P, sb * P + P), slice(t0, t0 + n)
                    three(pe, PS[u % 2][:, 0:n], KH[:, s], KL[:, s], QH[:, t], QL[:, t], True, True)\
                        .then_inc(sem("ml_s"), 1)
                pe.wait_ge(sem("ml_split"), 3 * i + 3)
                score(0)
                for u, (h, sb, t0, n, diag) in enumerate(MU):
                    if u + 1 < NMU:
                        score(u + 1)
                    pe.wait_ge(sem("ml_pl"), NMU * i + u + 1)
                    for tl in range((t0 - 512 * h) // P, 4):
                        if sb == 0:
                            pe.wait_ge(sem("ml_nev"), 8 * i + 4 * h + tl + 1)
                        t = slice(512 * h + tl * P - t0, 512 * h + tl * P - t0 + P)
                        last = three(pe, PS[2 + tl][:, 0:VW], PHt[u % 2][:, t], PLt[u % 2][:, t],
                                     VH[:, sb, :], VL[:, sb, :], sb == 0, sb == 4 * h + tl)
                    last.then_inc(sem("ml_pv"), 1)

        def ml_scalar(act):
            act.wait_ge(sem("g_col"), 2)
            with act.Fori(0, H_A) as i:
                act.wait_ge(sem("ml_M_in"), 16 * i + 16)
                act.wait_ge(sem("ml_head"), 2 * i + 2)

                def decay(u):
                    h, sb, t0, n, diag = MU[u]
                    act.wait_ge(sem("ml_p"), NMU * i + u + 1)
                    nc.scalar.activation(m_D[u % 2][:, 0:n], m_M[:, t0:t0 + n], ACT.Exp,
                                         bias=a_head[:, sb:sb + 1], scale=-1.0).then_inc(sem("ml_d"), 1)
                decay(0)
                for u, (h, sb, t0, n, diag) in enumerate(MU):
                    if u + 1 < NMU:
                        decay(u + 1)
                    act.wait_ge(sem("ml_p"), NMU * i + u + 3)
                    act.wait_ge(sem("ml_pv"), NMU * i + u + 1)
                    nc.scalar.copy(PHt[u % 2][:, 0:n], m_P[u % 2][:, 0:n]).then_inc(sem("ml_ph"), 1)
                    if diag and u > 0:
                        tl = sb - 4 * h
                        e = 4 * h + tl
                        act.wait_ge(sem("ml_h"), 8 * i + e + 1)
                        act.dma_start(s_h[e * P:e * P + P, bass.ts(i, DV_A)], m_H[tl])\
                            .then_inc(sem(f"ml_out{tl}"), 16)
                    elif diag:
                        act.wait_ge(sem("ml_h"), 8 * i + 1)
                        act.dma_start(s_h[0:P, bass.ts(i, DV_A)], m_H[0]).then_inc(sem("ml_out0"), 16)

        def ml_vector(dve):
            dve.sem_inc(sem("ml_p"), 2)
            dve.sem_inc(sem("ml_nev"), 4)
            dve.wait_ge(sem("g_col"), 2)
            with dve.Fori(0, H_A) as i:
                dve.wait_ge(sem("ml_d"), NMU * i)
                dve.wait_ge(sem("ml_h"), 8 * i)
                nc.vector.tensor_copy(a_head, a_col[:, i, :]).then_inc(sem("ml_head"), 1)
                nc.vector.tensor_copy(e_head, e_col[:, i, :]).then_inc(sem("ml_head"), 1)
                dve.wait_ge(sem("ml_head"), 2 * i + 2)
                dg = 0
                for u, (h, sb, t0, n, diag) in enumerate(MU):
                    dve.wait_ge(sem("ml_s"), NMU * i + u + 1)
                    dve.wait_ge(sem("ml_d"), NMU * i + u + 1)
                    if diag:
                        dg += 1
                        dve.wait_ge(sem("ml_mask"), 8 * i + dg)
                    nc.vector.scalar_tensor_tensor(out=m_P[u % 2][:, 0:n], in0=PS[u % 2][:, 0:n],
                                                   scalar=DK_A ** -0.5, in1=m_D[u % 2][:, 0:n],
                                                   op0=ALU.mult, op1=ALU.mult).then_inc(sem("ml_p"), 1)
                    dve.wait_ge(sem("ml_ph"), NMU * i + u + 1)
                    nc.vector.tensor_tensor(PLt[u % 2][:, 0:n], m_P[u % 2][:, 0:n], PHt[u % 2][:, 0:n],
                                            ALU.subtract).then_inc(sem("ml_pl"), 1)
                    if diag:
                        tl = sb - 4 * h
                        e = 4 * h + tl
                        dve.wait_ge(sem("ml_pv"), NMU * i + u + 3)
                        bank = PS[2 + tl]
                        nc.vector.tensor_scalar(small[:, 0:1], bank[:, DV_A:DV_A + 1], -1.0, e_head[:, e:e + 1],
                                                ALU.mult, ALU.max).then_inc(sem("ml_den"), 1)
                        dve.wait_ge(sem("ml_den"), 24 * i + 3 * e + 1)
                        nc.vector.tensor_tensor(small[:, 0:1], bank[:, DV_A:DV_A + 1], small[:, 0:1], ALU.max)\
                            .then_inc(sem("ml_den"), 1)
                        dve.wait_ge(sem("ml_den"), 24 * i + 3 * e + 2)
                        nc.vector.reciprocal(small[:, 1:2], small[:, 0:1]).then_inc(sem("ml_den"), 1)
                        dve.wait_ge(sem("ml_den"), 24 * i + 3 * e + 3)
                        dve.wait_ge(sem(f"ml_out{tl}"), 32 * i + 16 * h)
                        nc.vector.tensor_scalar(m_H[tl], bank[:, 0:DV_A], small[:, 1:2], None, ALU.mult)\
                            .then_inc(sem("ml_h"), 1)
                        dve.wait_ge(sem("ml_h"), 8 * i + e + 1)
                        dve.sem_inc(sem("ml_nev"), 1)

        h_in = [fv(W0 + 1024 * j, 1024) for j in range(2)]
        o_in = [fv(W0 + 2048 + 1024 * j, 1024) for j in range(2)]
        y_t = [fv(W0 + 4096 + 1024 * j, 1024) for j in range(2)]
        y_s = [FP[:, W0 + 6144 + 1024 * j:W0 + 7168 + 1024 * j].rearrange("p (k n) -> p k n", k=KC) for j in range(2)]
        mhg_t = fv(W0 + 9216, 1024)

        def hn_sync(sp):
            for tl in range(4):
                sp.wait_ge(sem(f"ml_out{tl}"), 16 * 2 * H_A)
            sp.wait_ge(sem("ml_pl"), NMU * H_A)
            sp.dma_start(mhg_t, mh_g.partition_broadcast(P)).then_inc(sem("hn_g"), 16)
            with sp.Fori(0, TT // 2) as i:
                for j in range(2):
                    sp.wait_ge(sem("hn_y"), 8 * i + 4 * j + 4)
                    sp.dma_start(h_in[j], s_h[bass.ts(2 * i + j, P), :]).then_inc(sem(f"hn_in{j}"), 16)
                    sp.dma_start(o_in[j], s_nat[bass.ts(2 * i + j, P), 1024:2048]).then_inc(sem(f"hn_in{j}"), 16)

        def hn_vector(dve):
            dve.sem_inc(sem("hn_y"), 8)
            dve.sem_inc(sem("hn_ev"), 4)
            dve.wait_ge(sem("hn_g"), 16)
            with dve.Fori(0, TT // 2) as i:
                for j in range(2):
                    st = small[:, 24 * j:24 * j + 24].rearrange("p (h s) -> p h s", h=H_A)
                    m = stats[:, j, 0:8].rearrange("p (h s) -> p h s", h=H_A)
                    v = ve[:, 4 * j:4 * j + 4]
                    r = rstd[:, 4 * j:4 * j + 4]
                    dve.wait_ge(sem(f"hn_in{j}"), 32 * i + 32)
                    for h in range(H_A):
                        nc.vector.bn_stats(st[:, h, :], h_in[j][:, h * DV_A:(h + 1) * DV_A]).then_inc(sem("hn_st"), 1)
                    for h in range(H_A):
                        dve.wait_ge(sem("hn_st"), 8 * i + 4 * j + h + 1)
                        apart(dve)
                        nc.vector.bn_aggr(m[:, h, :], st[:, h, :]).then_inc(sem("hn_mv"), 1)
                    dve.wait_ge(sem("hn_mv"), 8 * i + 4 * j + 4)
                    nc.vector.tensor_scalar(v, m[:, :, 1], EPS, None, ALU.add).then_inc(sem("hn_ve"), 1)
                    dve.wait_ge(sem("hn_sd"), 4 * i + 2 * j + 2)
                    nc.vector.reciprocal(r, v).then_inc(sem("hn_r"), 1)
                    for h in range(H_A):
                        c = slice(h * DV_A, (h + 1) * DV_A)
                        nc.vector.scalar_tensor_tensor(out=h_in[j][:, c], in0=h_in[j][:, c], scalar=m[:, h, 0:1],
                                                       in1=mhg_t[:, c], op0=ALU.subtract, op1=ALU.mult)\
                            .then_inc(sem("hn_c"), 1)
                    dve.wait_ge(sem("hn_r"), 2 * i + j + 1)
                    dve.wait_ge(sem("hn_tr"), 4 * i + 2 * j + 2)
                    for h in range(H_A):
                        c = slice(h * DV_A, (h + 1) * DV_A)
                        dve.wait_ge(sem("hn_c"), 8 * i + 4 * j + h + 1)
                        nc.vector.scalar_tensor_tensor(out=y_t[j][:, c], in0=h_in[j][:, c], scalar=r[:, h:h + 1],
                                                       in1=o_in[j][:, c], op0=ALU.mult, op1=ALU.mult)\
                            .then_inc(sem("hn_y"), 1)
                    for b in range(2):
                        dve.wait_ge(sem("hn_tr"), 4 * i + 2 * j + b + 5)
                        dve.wait_ge(sem(f"hn_out{j}"), 16 * i)
                        nc.vector.tensor_copy(y_s[j][:, 4 * b:4 * b + 4, :],
                                              PS[2 * j + b][:, :].rearrange("p (k n) -> p k n", k=4))\
                            .then_inc(sem("hn_ev"), 1)

        def hn_scalar(act):
            with act.Fori(0, TT // 2) as i:
                for j in range(2):
                    act.wait_ge(sem(f"hn_in{j}"), 32 * i + 32)
                    nc.scalar.activation(o_in[j], o_in[j], ACT.Sigmoid).then_inc(sem("hn_sd"), 1)
                    act.wait_ge(sem("hn_ve"), 2 * i + j + 1)
                    v = ve[:, 4 * j:4 * j + 4]
                    nc.scalar.sqrt(v, v).then_inc(sem("hn_sd"), 1)
                    act.wait_ge(sem("hn_ev"), 4 * i + 2 * j + 6)
                    act.dma_start(s_ya[:, :, bass.ts(2 * i + j, P)].rearrange("k p n -> p k n"), y_s[j])\
                        .then_inc(sem(f"hn_out{j}"), 16)

        def hn_tensor(pe):
            pe.wait_ge(sem("ml_nev"), 8 * H_A + 4)
            pe.sem_inc(sem("hn_tr"), 4)
            with pe.Fori(0, TT // 2) as i:
                for j in range(2):
                    for b in range(2):
                        pe.wait_ge(sem("hn_y"), 8 * i + 4 * j + 2 * b + 10)
                        pe.wait_ge(sem("hn_ev"), 4 * i + 2 * j + b + 1)
                        for k in range(4):
                            c = (4 * b + k) * P
                            last = nc.tensor.transpose(PS[2 * j + b][:, k * P:k * P + P], y_t[j][:, c:c + P], ident)
                        last.then_inc(sem("hn_tr"), 1)

        AU = triangle_units(True, True)
        NAU = len(AU)
        SB_SCALE = DH_B ** -0.5
        A0 = W0
        b_q, b_k, b_v = fv(A0, 1024), fv(A0 + 1024, 1024), FP[:, A0 + 2048:A0 + 3072].rearrange("p (s n) -> p s n", s=TT)
        z_t = [fv(A0 + 3072 + 512 * j, 512) for j in range(2)]
        ab_t = [fv(A0 + 4096 + 512 * j, 512) for j in range(2)]
        sp_t = [fv(A0 + 5120 + 512 * j, 512) for j in range(2)]
        ag_t = [fv(A0 + 6144 + 512 * j, 512) for j in range(2)]
        yo_t = [fv(A0 + 7168 + 512 * j, 512) for j in range(2)]
        BQH, BQL, BKH, BKL, BVH, BVL = (rv(R2 + 1024 * n, 1024) for n in range(6))
        SPH = [rv(R2 + 6144 + 512 * j, 512) for j in range(2)]
        SPL = [rv(R2 + 7168 + 512 * j, 512) for j in range(2)]
        WH = [rv(R2 + 8192 + 512 * j, 512) for j in range(2)]
        WL = [rv(R2 + 9216 + 512 * j, 512) for j in range(2)]

        def at_sync(sp):
            for j in range(2):
                sp.wait_ge(sem(f"hn_out{j}"), 16 * (TT // 2))
            sp.wait_ge(sem("hn_tr"), 2 * TT + 4)
            with sp.Fori(0, H_B) as i:
                sp.wait_ge(sem("at_split"), 3 * i)
                sp.dma_start(b_q, s_t[i + TC_Q]).then_inc(sem("at_in"), 16)
                sp.dma_start(b_k, s_t[i + TC_K]).then_inc(sem("at_in"), 16)
                sp.dma_start(b_v, s_nat[:, bass.ds(i * DH_B + 2048, DH_B)].rearrange("(s p) n -> p s n", p=P))\
                    .then_inc(sem("at_in"), 16)

        def at_pool(pool):
            with pool.Fori(0, H_B) as i:
                pool.wait_ge(sem("at_in"), 48 * i + 48)
                pool.wait_ge(sem("at_pv"), NAU * i + 2)
                for n, (src, hi, lo) in enumerate([
                        (b_q, BQH, BQL), (b_k, BKH, BKL),
                        (b_v, BVH.rearrange("p (s n) -> p s n", s=TT), BVL.rearrange("p (s n) -> p s n", s=TT))]):
                    apart(pool)
                    nc.gpsimd.tensor_copy(hi, src).then_inc(sem("at_hi"), 1)
                    pool.wait_ge(sem("at_hi"), 3 * i + n + 1)
                    nc.gpsimd.tensor_tensor(lo, src, hi, ALU.subtract).then_inc(sem("at_split"), 1)

                def soft(u):
                    h, sb, t0, n, diag = AU[u]
                    j = u % 2
                    pool.wait_ge(sem("at_sp"), NAU * i + u + 1)
                    if diag:
                        apart(pool)
                        nc.gpsimd.affine_select(out=sp_t[j][:, 0:P], in_=sp_t[j][:, 0:P], compare_op=ALU.is_gt,
                                                fill=0.0, base=0, pattern=[[1, P]], channel_multiplier=-1)\
                            .then_inc(sem("at_smask"), 1)
                        pool.wait_ge(sem("at_smask"), 8 * i + ndiag(u + 1))
                    pool.wait_ge(sem("at_tric"), NAU * i + u + 1)
                    apart(pool)
                    nc.gpsimd.tensor_copy(SPH[j][:, 0:n], sp_t[j][:, 0:n]).then_inc(sem("at_sph"), 1)
                    pool.wait_ge(sem("at_sph"), NAU * i + u + 1)
                    nc.gpsimd.tensor_tensor(SPL[j][:, 0:n], sp_t[j][:, 0:n], SPH[j][:, 0:n], ALU.subtract)\
                        .then_inc(sem("at_spl"), 1)

                def wmask(u):
                    h, sb, t0, n, diag = AU[u]
                    j = u % 2
                    if diag:
                        pool.wait_ge(sem("at_w"), NAU * i + u + 1)
                        apart(pool)
                        nc.gpsimd.affine_select(out=ag_t[j][:, 0:P], in_=ag_t[j][:, 0:P], compare_op=ALU.is_gt,
                                                fill=0.0, base=0, pattern=[[1, P]], channel_multiplier=-1)\
                            .then_inc(sem("at_wmask"), 1)
                soft(0)
                for u in range(NAU):
                    if u + 1 < NAU:
                        soft(u + 1)
                    wmask(u)

        def ndiag(n):
            return sum(1 for a in AU[:n] if a[4])

        def at_tensor(pe):
            pe.sem_inc(sem("at_pv"), 2)
            pe.sem_inc(sem("at_tric"), 2)
            pe.wait_ge(sem("hn_ev"), 2 * TT + 4)
            with pe.Fori(0, H_B) as i:
                def score(u):
                    h, sb, t0, n, diag = AU[u]
                    pe.wait_ge(sem("at_z"), NAU * i + u + 1)
                    s, t = slice(sb * P, sb * P + P), slice(t0, t0 + n)
                    three(pe, PS[u % 2][:, 0:n], BKH[:, s], BKL[:, s], BQH[:, t], BQL[:, t], True, True)\
                        .then_inc(sem("at_s"), 1)

                def weigh(u):
                    h, sb, t0, n, diag = AU[u]
                    pe.wait_ge(sem("at_wl"), NAU * i + u + 1)
                    first = sb == 4 * h + 3
                    if first:
                        pe.wait_ge(sem("at_yev"), 2 * i + h + 1)
                    v = slice(sb * P, sb * P + P)
                    c = slice(t0 - 512 * h, 512)
                    three(pe, PS[4 + h][:, c], BVH[:, v], BVL[:, v], WH[u % 2][:, 0:n], WL[u % 2][:, 0:n],
                          first, sb == 0, skip=True).then_inc(sem("at_pv"), 1)

                pe.wait_ge(sem("at_split"), 3 * i + 3)
                score(0)
                for u, (h, sb, t0, n, diag) in enumerate(AU):
                    if u + 1 < NAU:
                        score(u + 1)
                    first = sb == 4 * h + 3
                    c = slice(t0 - 512 * h, 512)
                    pe.wait_ge(sem("at_spl"), NAU * i + u + 1)
                    nc.tensor.matmul(PS[2 + h][:, c], TRI, SPH[u % 2][:, 0:n], start=first, stop=False,
                                     skip_group_check=True)
                    nc.tensor.matmul(PS[2 + h][:, c], TRI, SPL[u % 2][:, 0:n], start=False, stop=True,
                                     skip_group_check=True).then_inc(sem("at_tri"), 1)
                    if u >= 1:
                        weigh(u - 1)
                    pe.wait_ge(sem("at_arg"), NAU * i + u + 1)
                    nc.tensor.matmul(PS[2 + h][:, c], TRIC, SPH[u % 2][:, 0:n], start=False, stop=False,
                                     skip_group_check=True)
                    nc.tensor.matmul(PS[2 + h][:, c], TRIC, SPL[u % 2][:, 0:n], start=False, stop=True,
                                     skip_group_check=True).then_inc(sem("at_tric"), 1)
                weigh(NAU - 1)

        def at_scalar(act):
            act.sem_inc(sem("at_z"), 2)
            with act.Fori(0, H_B) as i:
                def front(u):
                    h, sb, t0, n, diag = AU[u]
                    j = u % 2
                    act.wait_ge(sem("at_s"), NAU * i + u + 1)
                    act.wait_ge(sem("at_arg"), NAU * i + u - 1) if u >= 2 else act.wait_ge(sem("at_arg"), NAU * i)
                    nc.scalar.activation(z_t[j][:, 0:n], PS[j][:, 0:n], ACT.Copy, scale=SB_SCALE)\
                        .then_inc(sem("at_z"), 1)
                    act.wait_ge(sem("at_ab"), NAU * i + u + 1)
                    nc.scalar.activation(ab_t[j][:, 0:n], ab_t[j][:, 0:n], ACT.Exp).then_inc(sem("at_ex"), 1)
                    act.wait_ge(sem("at_ex"), NAU * i + u + 1)
                    nc.scalar.activation(ab_t[j][:, 0:n], ab_t[j][:, 0:n], ACT.Ln, bias=1.0).then_inc(sem("at_ln"), 1)

                def back(u):
                    h, sb, t0, n, diag = AU[u]
                    j = u % 2
                    act.wait_ge(sem("at_arg"), NAU * i + u + 1)
                    nc.scalar.activation(ag_t[j][:, 0:n], ag_t[j][:, 0:n], ACT.Exp).then_inc(sem("at_w"), 1)
                    if diag:
                        act.wait_ge(sem("at_wmask"), 8 * i + ndiag(u + 1))
                    act.wait_ge(sem("at_w"), NAU * i + u + 1)
                    act.wait_ge(sem("at_pv"), NAU * i + u + 1)
                    nc.scalar.copy(WH[j][:, 0:n], ag_t[j][:, 0:n]).then_inc(sem("at_wh"), 1)

                front(0)
                for u in range(NAU):
                    if u + 1 < NAU:
                        front(u + 1)
                    back(u)
                for h in range(2):
                    act.wait_ge(sem("at_yev"), 2 * i + h + 3)
                    act.dma_start(s_yb[i][:, 512 * h:512 * h + 512], yo_t[h]).then_inc(sem(f"at_out{h}"), 16)

        def at_vector(dve):
            dve.sem_inc(sem("at_yev"), 2)
            with dve.Fori(0, H_B) as i:
                def front(u):
                    h, sb, t0, n, diag = AU[u]
                    j = u % 2
                    dve.wait_ge(sem("at_z"), NAU * i + u + 3)
                    nc.vector.scalar_tensor_tensor(out=ab_t[j][:, 0:n], in0=z_t[j][:, 0:n], scalar=-1.0,
                                                   in1=z_t[j][:, 0:n], op0=ALU.mult, op1=ALU.min)\
                        .then_inc(sem("at_ab"), 1)
                    dve.wait_ge(sem("at_ln"), NAU * i + u + 1)
                    dve.wait_ge(sem("at_spl"), NAU * i + max(u - 1, 0))
                    nc.vector.scalar_tensor_tensor(out=sp_t[j][:, 0:n], in0=z_t[j][:, 0:n], scalar=0.0,
                                                   in1=ab_t[j][:, 0:n], op0=ALU.max, op1=ALU.add)\
                        .then_inc(sem("at_sp"), 1)

                def back(u):
                    h, sb, t0, n, diag = AU[u]
                    j = u % 2
                    c = slice(t0 - 512 * h, 512)
                    dve.wait_ge(sem("at_tri"), NAU * i + u + 1)
                    dve.wait_ge(sem("at_wl"), NAU * i + max(u - 1, 0))
                    nc.vector.tensor_tensor(ag_t[j][:, 0:n], z_t[j][:, 0:n], PS[2 + h][:, c], ALU.subtract)\
                        .then_inc(sem("at_arg"), 1)

                def low(u):
                    h, sb, t0, n, diag = AU[u]
                    j = u % 2
                    dve.wait_ge(sem("at_wh"), NAU * i + u + 1)
                    nc.vector.tensor_tensor(WL[j][:, 0:n], ag_t[j][:, 0:n], WH[j][:, 0:n], ALU.subtract)\
                        .then_inc(sem("at_wl"), 1)

                front(0)
                for u in range(NAU):
                    if u + 1 < NAU:
                        front(u + 1)
                    back(u)
                    low(u)
                for h in range(2):
                    dve.wait_ge(sem("at_pv"), NAU * i + 2 + (4 if h == 0 else NAU))
                    dve.wait_ge(sem(f"at_out{h}"), 16 * i)
                    nc.vector.tensor_copy(yo_t[h], PS[4 + h][:, :]).then_inc(sem("at_yev"), 1)

        YH = RP[:, 0:8192].rearrange("p (a k n) -> p a k n", a=2, k=KC)
        YL = RP[:, 8192:16384].rearrange("p (a k n) -> p a k n", a=2, k=KC)
        MH = RP[:, R2:R2 + 8192].rearrange("p (k n) -> p k n", k=KC)
        ML = RP[:, R2 + 8192:R2 + 16384].rearrange("p (k n) -> p k n", k=KC)
        BR0 = W0
        y_raw = FP[:, BR0:BR0 + 8192].rearrange("p (a k n) -> p a k n", a=2, k=KC)
        bg_t = [[fv(BR0 + 8192 + 1024 * j + 512 * a, 512) for a in range(2)] for j in range(2)]
        br_t = [[fv(BR0 + 10240 + 1024 * j + 512 * a, 512) for a in range(2)] for j in range(2)]

        def br_sync(sp):
            for h in range(2):
                sp.wait_ge(sem(f"at_out{h}"), 16 * H_B)
            sp.wait_ge(sem("at_wl"), NAU * H_B)
            load_pair(sp, B_BR // 2)
            for h in range(2):
                if h:
                    sp.wait_ge(sem("br_ylo"), 2)
                t = slice(512 * h, 512 * h + 512)
                sp.dma_start(y_raw[:, 0, :, :], s_ya[:, :, t].rearrange("k p n -> p k n")).then_inc(sem("br_yin"), 16)
                sp.dma_start(y_raw[:, 1, :, :], s_yb[:, :, t].rearrange("k p n -> p k n")).then_inc(sem("br_yin"), 16)
                for c in range(KC):
                    n = KC * h + c
                    j = n % 2
                    if n >= 2:
                        sp.wait_ge(sem("br_m"), 3 * (n - 1))
                    for a, tc in ((0, TC_GA), (1, TC_GB)):
                        sp.dma_start(bg_t[j][a], s_t[tc + c][:, t]).then_inc(sem(f"br_gin{j}"), 16)
                    if n < 15:
                        load_pair(sp, B_BR // 2 + n + 1)

        def br_pool(pool):
            pool.wait_ge(sem("br_start"), 1)
            for n in range(2 * KC):
                for a in range(2):
                    if n:
                        pool.wait_ge(sem("br_done"), 2 * n - 1 + a)
                    split_piece(pool, B_BR + 2 * n + a, a, B_BR // 2 + n, *cseg[a])

        def br_tensor(pe):
            pe.wait_ge(sem("at_yev"), 2 * H_B + 2)
            pe.sem_inc(sem("br_start"), 1)
            for n in range(2 * KC):
                h, j = n // KC, n % 2
                if n % KC == 0:
                    pe.wait_ge(sem("br_ylo"), 2 * h + 2)
                for a in range(2):
                    wh, wl = cseg[a]
                    pe.wait_ge(w_split, B_BR + 2 * n + a + 1)
                    if n >= 2:
                        pe.wait_ge(sem("br_m"), 3 * (n - 1))
                    for k in range(KC):
                        c = slice(k * P, k * P + P)
                        last = three(pe, PS[2 * j + a][:, :], wh[:, c], wl[:, c], YH[:, a, k, :], YL[:, a, k, :],
                                     k == 0, k == KC - 1)
                    last.then_inc(sem("br_done"), 1)

        def br_scalar(act):
            def split_y(h):
                act.wait_ge(sem("br_yin"), 32 * h + 32)
                act.wait_ge(sem("at_pv"), NAU * H_B + 2)
                if h:
                    act.wait_ge(sem("br_done"), 2 * KC)
                for a in range(2):
                    nc.scalar.copy(YH[:, a, :, :], y_raw[:, a, :, :]).then_inc(sem("br_yhi"), 1)
            for n in range(2 * KC):
                h, c, j = n // KC, n % KC, n % 2
                if c == 0:
                    split_y(h)
                act.wait_ge(sem(f"br_gin{j}"), 32 * (n // 2) + 32)
                for a in range(2):
                    nc.scalar.activation(bg_t[j][a], bg_t[j][a], ACT.Sigmoid).then_inc(sem("br_sig"), 1)
                act.wait_ge(sem("br_m"), 3 * n + 3)
                nc.scalar.copy(MH[:, c, 512 * h:512 * h + 512], br_t[j][0]).then_inc(sem("br_mhi"), 1)

        def br_vector(dve):
            for n in range(2 * KC):
                h, c, j = n // KC, n % KC, n % 2
                if c == 0:
                    for a in range(2):
                        dve.wait_ge(sem("br_yhi"), 2 * h + a + 1)
                        nc.vector.tensor_tensor(YL[:, a, :, :], y_raw[:, a, :, :], YH[:, a, :, :], ALU.subtract)\
                            .then_inc(sem("br_ylo"), 1)
                dve.wait_ge(sem("br_sig"), 2 * n + 2)
                if n >= 2:
                    dve.wait_ge(sem("br_mlo"), n - 1)
                for a in range(2):
                    dve.wait_ge(sem("br_done"), 2 * n + a + 1)
                    nc.vector.tensor_tensor(br_t[j][a], PS[2 * j + a][:, :], bg_t[j][a], ALU.mult)\
                        .then_inc(sem("br_m"), 1)
                dve.wait_ge(sem("br_m"), 3 * n + 2)
                nc.vector.tensor_tensor(br_t[j][0], br_t[j][0], br_t[j][1], ALU.add).then_inc(sem("br_m"), 1)
                dve.wait_ge(sem("br_mhi"), n + 1)
                nc.vector.tensor_tensor(ML[:, c, 512 * h:512 * h + 512], br_t[j][0],
                                        MH[:, c, 512 * h:512 * h + 512], ALU.subtract).then_inc(sem("br_mlo"), 1)

        def full_pool(pool, base, hi, lo, free):
            for s, v in free:
                pool.wait_ge(s, v)
            for k in range(KC):
                split_piece(pool, base + k, k % 2, base // 2 + k // 2, hi[:, k, :], lo[:, k, :])

        def full_tensor(pe, q, base, lh, ll, rh, rl, ready):
            for s, v in ready:
                pe.wait_ge(s, v)
            for o in range(16):
                tt, dh = o // 2, o % 2
                if o >= 4:
                    pe.wait_ge(sem(q + "evac"), o - 3)
                for k in range(KC):
                    if o == 0:
                        pe.wait_ge(w_split, base + k + 1)
                    t, c = slice(tt * P, tt * P + P), slice(dh * 512, dh * 512 + 512)
                    last = three(pe, PS[4 + o % 4][:, :], lh[:, k, t], ll[:, k, t], rh[:, k, c], rl[:, k, c],
                                 k == 0, k == KC - 1)
                last.then_inc(sem(q + "done"), 1)

        def mix_scalar(act):
            act.wait_ge(sem("br_mlo"), 2 * KC)
            act.dma_start(X, s_x).then_inc(sem("x_back"), 16)
            act.wait_ge(sem("x_back"), 16)
            scale_x(act)

        def mix_vector(dve):
            for o in range(16):
                tt, dh = o // 2, o % 2
                xs = X[:, tt, dh * 512:dh * 512 + 512]
                dve.wait_ge(sem("mx_done"), o + 1)
                dve.wait_ge(sem("x_scaled"), TT + tt + 1)
                nc.vector.tensor_tensor(xs, PS[4 + o % 4][:, :], xs, ALU.add).then_inc(sem("mx_evac"), 1)

        bple_t = fv(G0, D)
        gate_t = [fv(T0 + 512 * j, 512) for j in range(2)]
        pl_t = [fv(T0 + 1024 + 512 * j, 512) for j in range(2)]
        PWH = RP[:, R2:R2 + 8192].rearrange("p (k n) -> p k n", k=KC)
        PWL = RP[:, R2 + 8192:R2 + 16384].rearrange("p (k n) -> p k n", k=KC)

        def ple_scalar(act):
            act.wait_ge(sem("ln_y"), 3 * TT)
            act.dma_start(bple_t, b_ple.partition_broadcast(P)).then_inc(sem("bple_in"), 16)
            act.wait_ge(sem("ln_tr"), 6 * TT)
            scale_x(act)
            act.wait_ge(sem("f_h_lo"), 8 * FI)
            for o in range(16):
                if o < 2:
                    load_ple(act, o)
                act.wait_ge(sem("pg_evac"), o + 1)
                nc.scalar.activation(gate_t[o % 2], gate_t[o % 2], ACT.Sigmoid).then_inc(sem("pg_sig"), 1)
                if o >= 1 and o + 1 < 16:
                    act.wait_ge(sem("pg_mul"), o)
                    load_ple(act, o + 1)

        def load_ple(act, o):
            act.dma_start(pl_t[o % 2], s_ple[o // 2 * P:o // 2 * P + P, o % 2 * 512:o % 2 * 512 + 512])\
                .then_inc(sem(f"pl_in{o % 2}"), 16)

        def ple_vector(dve):
            dve.wait_ge(sem("bple_in"), 16)
            for o in range(16):
                tt, dh = o // 2, o % 2
                xs = X[:, tt, dh * 512:dh * 512 + 512]
                dve.wait_ge(sem("pg_done"), o + 1)
                if o >= 2:
                    dve.wait_ge(sem("pg_mul"), o - 1)
                nc.vector.tensor_tensor(gate_t[o % 2], PS[4 + o % 4][:, :], bple_t[:, dh * 512:dh * 512 + 512], ALU.add)\
                    .then_inc(sem("pg_evac"), 1)
                dve.wait_ge(sem("pg_sig"), o + 1)
                dve.wait_ge(sem(f"pl_in{o % 2}"), 16 * (o // 2) + 16)
                nc.vector.tensor_tensor(gate_t[o % 2], gate_t[o % 2], pl_t[o % 2], ALU.mult).then_inc(sem("pg_mul"), 1)
                dve.wait_ge(sem("pg_mul"), o + 1)
                dve.wait_ge(sem("x_scaled"), 3 * TT + tt + 1)
                nc.vector.tensor_tensor(xs, gate_t[o % 2], xs, ALU.add).then_inc(sem("pg_add"), 1)

        def scale_x_after(act, r):
            act.wait_ge(sem("ln_tr"), 2 * TT * (r + 1))
            scale_x(act)

        @block.sync
        def _(sp):
            sp.dma_start(raw[0], w_all[0]).then_inc(raw_in[0], 16)
            sp.dma_start(raw[1], w_all[1]).then_inc(raw_in[1], 16)
            with sp.Fori(1, B_BR // 2) as j:
                load_pair(sp, j)
            gates_sync(sp)
            ml_sync(sp)
            hn_sync(sp)
            at_sync(sp)
            br_sync(sp)
            with sp.Fori(B_MIX // 2, N_PIECES // 2) as j:
                load_pair(sp, j)
            for tt in range(TT):
                sp.wait_ge(sem("ln_y"), 3 * TT + tt + 1)
                sp.dma_start(out[tt * P:tt * P + P, :], X[:, tt, :]).then_inc(sem("out"), 16)
            sp.wait_ge(sem("out"), 16 * TT)

        @block.gpsimd
        def _(pool):
            start_pool(pool)
            ffn_pool(pool, 0, B_FFN1, [(sem("st_done"), 16)])
            nat_pool(pool, [(sem("f_down_done"), 16 * FI + 16)])
            chunk_pool(pool, "qa_", B_QA, NQA, [])
            chunk_pool(pool, "tc_", B_TC, NTC, [(sem("qa_done"), 2 * NQA + 4)])
            ml_pool(pool)
            at_pool(pool)
            br_pool(pool)
            full_pool(pool, B_MIX, XH, XL, [(sem("br_done"), 4 * KC)])
            ffn_pool(pool, 1, B_FFN2, [(sem("mx_done"), 16)])
            full_pool(pool, B_PLE, PWH, PWL, [(sem("f_down_done"), 32 * FI + 16)])

        @block.tensor
        def _(pe):
            start_tensor(pe)
            ffn_tensor(pe, 0, B_FFN1, [(sem("st_evac"), 16), (w_split, N_START)])
            ln_tensor(pe, 0, [(sem("const"), 5)])
            nat_tensor(pe, [(sem("ln_tr_lo"), 2 * TT)])
            chunk_tensor(pe, "qa_", B_QA, NQA, [(sem("n_evac"), 8 * NG + 8)])
            chunk_tensor(pe, "tc_", B_TC, NTC, [(sem("qa_evac0"), NQA + 2), (sem("qa_evac1"), NQA + 2)])
            gates_tensor(pe)
            ml_tensor(pe)
            hn_tensor(pe)
            at_tensor(pe)
            br_tensor(pe)
            full_tensor(pe, "mx_", B_MIX, MH, ML, XH, XL, [(sem("br_mlo"), 2 * KC)])
            ln_tensor(pe, 1, [])
            ffn_tensor(pe, 1, B_FFN2, [(sem("ln_tr_lo"), 4 * TT)])
            ln_tensor(pe, 2, [])
            full_tensor(pe, "pg_", B_PLE, XH, XL, PWH, PWL, [(sem("ln_tr_lo"), 6 * TT)])

        @block.scalar
        def _(act):
            start_scalar(act)
            ln_loads(act, 0, [(sem("const"), 5)])
            ffn_scalar(act, 0)
            ln_scalar(act, 0, [(sem("f_down_done"), 16 * FI + 16)])
            nat_scalar(act)
            qa_scalar(act)
            tc_scalar(act)
            gates_scalar(act)
            ml_scalar(act)
            hn_scalar(act)
            act.wait_ge(sem("hn_ev"), 2 * TT + 4)
            nc.scalar.preload_act_table_set("natural_log_exp_and_others")
            at_scalar(act)
            br_scalar(act)
            mix_scalar(act)
            ln_loads(act, 1, [])
            ln_scalar(act, 1, [(sem("mx_done"), 16)])
            scale_x_after(act, 1)
            ln_loads(act, 2, [(sem("ln_y"), 2 * TT)])
            ffn_scalar(act, 1)
            ln_scalar(act, 2, [(sem("f_down_done"), 32 * FI + 16)])
            ple_scalar(act)
            ln_loads(act, 3, [(sem("pg_evac"), 16)])
            ln_scalar(act, 3, [], transposed=False)

        @block.vector
        def _(dve):
            ffn_vector(dve, 0, [(sem("x_scaled"), TT), (sem("st_out0"), 64), (sem("st_out1"), 64),
                                   (sem("st_out2"), 64), (sem("st_out3"), 64)])
            ln_vector(dve, 0, [(sem("f_down_evac"), 16 * FI + 4)])
            nat_vector(dve)
            qa_vector(dve)
            tc_vector(dve)
            gates_vector(dve)
            ml_vector(dve)
            hn_vector(dve)
            at_vector(dve)
            br_vector(dve)
            mix_vector(dve)
            ln_vector(dve, 1, [(sem("mx_evac"), 16)])
            ffn_vector(dve, 1, [(sem("x_scaled"), 3 * TT)])
            ln_vector(dve, 2, [(sem("f_down_evac"), 32 * FI + 4)])
            ple_vector(dve)
            ln_vector(dve, 3, [(sem("pg_add"), 16)], transposed=False)


def lay_out(i):
    import numpy as np
    a = {k: np.asarray(v) for k, v in i.items()}

    def columns(w, step=P):
        n = w.shape[1] // step
        return w.reshape(KC, P, n, step).transpose(2, 1, 0, 3).reshape(n, P, KC * step)

    def ffn(l):
        g, u = columns(a["ffn_wg"][0, l]), columns(a["ffn_wu"][0, l])
        d = a["ffn_wd"][0, l].reshape(FC, P, D)
        return np.stack([g[0::2], u[0::2], g[1::2], u[1::2], d[0::2], d[1::2]], axis=1).reshape(6 * FI, P, PC)

    w = a["w_in"][0]
    b = a["b_in"][0]
    qa, va, oa = slice(0, 1024), slice(1024, 2048), slice(2048, 3072)
    ic, fc = slice(3072, 3076), slice(3076, 3080)
    qb, kb, vb = slice(3080, 4104), slice(4104, 5128), slice(5128, 6152)
    ga, gb = slice(6152, 7176), slice(7176, 8200)
    pad = np.zeros((D, P - H_A), w.dtype)
    bpad = np.zeros((P - H_A,), w.dtype)
    nat = np.concatenate([w[:, va], w[:, oa], w[:, vb]], axis=1)
    nat = nat.reshape(4, 2, P, NG, 512).transpose(3, 0, 2, 1, 4).reshape(4 * NG, P, PC)
    tch = np.concatenate([w[:, qb], w[:, kb], w[:, ga], w[:, gb], w[:, ic], pad, w[:, fc], pad], axis=1)
    btc = np.concatenate([b[qb], b[kb], b[ga], b[gb], b[ic], bpad, b[fc], bpad])
    branches = np.stack([columns(a["w_branch_a"][0]), columns(a["w_branch_b"][0])], axis=1).reshape(2 * KC, P, PC)
    w_all = np.concatenate([
        a["p"][0, 0].T.reshape(2, P, T), a["w_ple"][0].reshape(2, P, D), a["x"][0].T.reshape(KC, P, T),
        ffn(0), nat, columns(w[:, qa]), columns(tch), branches, branches,
        a["w_mix_out"][0].reshape(KC, P, D), ffn(1), a["w_ple_gate"][0].reshape(KC, P, D)])
    return {
        "w_all": w_all,
        "x_nat": a["x"][0].reshape(TT, P, D).transpose(1, 0, 2),
        "b_t": btc.reshape(NTC, P).T, "b_qa": b[qa].reshape(NQA, P).T,
        "b_nat": np.concatenate([b[va], b[oa], b[vb]]),
        "b_if": a["b_forget"][0].reshape(H_A, 1),
        "conv_w": a["conv_w"][0].reshape(CONV_W, NQA, P).transpose(2, 1, 0),
        "conv_b": a["conv_b"][0].reshape(NQA, P).T,
        "mh_g": a["mh_norm_g"][0].reshape(-1),
        "ln_g": a["ln_g"][0], "ln_b": a["ln_b"][0], "b_ple": a["b_ple_gate"][0],
    }


_SCRATCH = [("s_ple", (T, D)), ("s_x", (P, TT, D)), ("s_nat", (T, NAT)), ("s_qa", (NQA, P, T)),
            ("s_t", (NTC, P, T)), ("s_m", (H_A, T)), ("s_h", (T, D)), ("s_ya", (KC, P, T)), ("s_yb", (KC, P, T))]


def kernel(**inputs):
    import numpy as _np
    import concourse.bacc as _bacc
    from concourse.bass_utils import run_bass_kernel_spmd as _run

    nc = _bacc.Bacc("TRN2", target_bir_lowering=False, num_devices=1)
    arrays, args = {}, []
    for name, v in lay_out(inputs).items():
        v = _np.ascontiguousarray(v)
        arrays[f"in_{name}"] = v
        args.append(nc.dram_tensor(f"in_{name}", v.shape, F32, kind="ExternalInput").ap())
    args.append(nc.dram_tensor("out_0", (T, D), F32, kind="ExternalOutput").ap())
    for name, shape in _SCRATCH:
        args.append(nc.dram_tensor(name, shape, F32, kind="Internal").ap())
    build(nc, *args)
    r = _run(nc, [arrays], core_ids=[0])
    return r.results[0]["out_0"].reshape(1, T, D)
```

```python
import concourse.bass as bass
from concourse import mybir
from contextlib import ExitStack

F32 = mybir.dt.float32
F32R = mybir.dt.float32r
ACT = mybir.ActivationFunctionType
ALU = mybir.AluOpType

P = 128
D = 1024
T = 1024
KC = D // P
TT = T // P
PC = 1024
FFN_F = 2816
FC = FFN_F // P
FI = FC // 2
H_A, DK_A, DV_A, CONV_W = 4, 128, 256, 4
H_B, DH_B = 8, 128
NAT = 3072
NG = NAT // 512
NQA = 2 * H_A
NTC = 32
TC_Q, TC_K, TC_GA, TC_GB = 0, 8, 16, 24
NTA = 2 * H_B
V_A, V_B, O_A = 0, 1024, 2048
EPS = 1e-5
ALPHA = 2.0 ** 0.25

B_FFN1 = KC
B_NAT = B_FFN1 + 6 * FI
B_PLE0 = B_NAT + 4 * NG
B_IF = B_PLE0 + 4
B_QA = B_IF + 1
B_TA = B_QA + NQA
B_TB = B_TA + NTA
B_BR = B_TB + NTC - NTA
B_MIX = B_BR + 2 * 2 * KC
B_FFN2 = B_MIX + KC
B_PLE = B_FFN2 + 6 * FI
N_PIECES = B_PLE + KC


def triangle_units(descending):
    out = []
    for half in range(2):
        blocks = range(4 * half + 4)
        for sb in (reversed(blocks) if descending else blocks):
            t0 = max(sb * P, 512 * half)
            out.append((half, sb, t0, 512 * (half + 1) - t0, sb >= 4 * half))
    return out


MU = triangle_units(False)
NMU = len(MU)
AU = triangle_units(True)
NAU = len(AU)


def build(nc, w_all, x_nat, b_t, b_if, b_qa, b_nat, b_forget, conv_w, conv_b, mh_g, ln_g, ln_b, b_ple, out,
          s_ple, s_x, s_nat, s_qa, s_t, s_m, s_h, s_ya, s_yb):
    ctx = ExitStack()
    with ctx:
        FP = ctx.enter_context(nc.sbuf_tensor("fp", [P, 16064], F32))
        RP = ctx.enter_context(nc.sbuf_tensor("rp", [P, 37120], F32R))
        PS = [ctx.enter_context(nc.psum_tensor(f"bank{b}", [P, 512], F32)) for b in range(8)]
        made = {}

        def sem(name):
            if name not in made:
                made[name] = ctx.enter_context(nc.semaphore(name))
            return made[name]

        def fv(base, n):
            return FP[:, base:base + n]

        def rv(base, n):
            return RP[:, base:base + n]

        raw = [fv(0, PC), fv(PC, PC)]
        ident = fv(2048, P)
        stats = FP[:, 2176:2176 + 96].rearrange("p (t s) -> p t s", t=TT)
        mv = FP[:, 2272:2288].rearrange("p (t s) -> p t s", t=TT)
        rstd = fv(2288, TT)
        ve = fv(2296, TT)
        bt_col = fv(2304, NTC)
        bif_col = fv(2336, 1)
        bf_col = fv(2337, 1)
        bqa_col = fv(2338, NQA)
        cw_col = FP[:, 2346:2378].rearrange("p (c j) -> p c j", j=CONV_W)
        cb_col = fv(2378, NQA)
        a_col = FP[:, 2386:2418].rearrange("p (h t) -> p h t", h=H_A)
        e_col = FP[:, 2418:2450].rearrange("p (h t) -> p h t", h=H_A)
        a_head = fv(2450, TT)
        e_head = fv(2458, TT)
        small = fv(2466, 64)
        X0 = 2688
        X = FP[:, X0:X0 + 8192].rearrange("p (t n) -> p t n", t=TT)
        G0 = X0 + 8192
        lng_t, lnb_t = fv(G0, D), fv(G0 + D, D)
        T0 = G0 + 2048
        W0 = X0

        XH = RP[:, 0:8192].rearrange("p (k n) -> p k n", k=KC)
        XL = RP[:, 8192:16384].rearrange("p (k n) -> p k n", k=KC)
        R2 = 16384
        R3 = 32768
        TRI = rv(36864, P)
        TRIC = rv(36992, P)

        def seg(base):
            return rv(base, PC), rv(base + PC, PC)

        fseg = [seg(R2 + 2048 * s) for s in range(6)]
        cseg = [seg(R3 + 2048 * s) for s in range(2)]

        raw_in = [sem("raw_in0"), sem("raw_in1")]
        w_hi = sem("w_hi")
        w_split = sem("w_split")
        blk = ctx.enter_context(nc.Block())

        def apart(eng, name):
            eng.sem_inc(sem(name), 1)

        def load_pair(sp, j):
            for s in range(2):
                sp.wait_ge(w_split, 2 * j + s - 1)
                sp.dma_start(raw[s], w_all[2 * j + s]).then_inc(raw_in[s], 16)

        def hi_piece(act, n0, step, hi):
            act.wait_ge(raw_in[n0 % 2], 16 * (n0 // 2) + 8 * step + 16)
            nc.scalar.copy(hi, raw[n0 % 2]).then_inc(w_hi, 1)

        def lo_piece(pool, n0, step, hi, lo):
            pool.wait_ge(w_hi, n0 + step + 1)
            nc.gpsimd.tensor_tensor(lo, raw[n0 % 2], hi, ALU.subtract).then_inc(w_split, 1)

        def three(pe, ps, lh, ll, rh, rl, start, stop, skip=False):
            nc.tensor.matmul(ps, lh, rh, start=start, stop=False, skip_group_check=skip)
            nc.tensor.matmul(ps, lh, rl, start=False, stop=False, skip_group_check=skip)
            return nc.tensor.matmul(ps, ll, rh, start=False, stop=stop, skip_group_check=skip)

        def scale_x(act, tt):
            nc.scalar.mul(X[:, tt, :], X[:, tt, :], ALPHA).then_inc(sem("x_scaled"), 1)

        def start_pool(pool):
            nc.gpsimd.memset(ident, 0.0).then_inc(sem("const"), 1)
            nc.gpsimd.memset(fv(T0, P), 1.0).then_inc(sem("const"), 1)
            pool.wait_ge(sem("const"), 2)
            nc.gpsimd.affine_select(out=ident, in_=ident, compare_op=ALU.not_equal, fill=1.0, base=0,
                                    pattern=[[-1, P]], channel_multiplier=1).then_inc(sem("const"), 1)
            nc.gpsimd.affine_select(out=TRI, in_=fv(T0, P), compare_op=ALU.is_ge, fill=0.0, base=0,
                                    pattern=[[-1, P]], channel_multiplier=1).then_inc(sem("const"), 1)
            nc.gpsimd.affine_select(out=TRIC, in_=fv(T0, P), compare_op=ALU.is_gt, fill=0.0, base=0,
                                    pattern=[[1, P]], channel_multiplier=-1).then_inc(sem("const"), 1)
            for n in range(KC):
                lo_piece(pool, n, 0, XH[:, n, :], XL[:, n, :])

        def start_scalar(act):
            for n in range(KC):
                hi_piece(act, n, 0, XH[:, n, :])
            act.dma_start(X, x_nat).then_inc(sem("x_in"), 16)
            for dst, src in ((bt_col, b_t), (bif_col, b_if), (bqa_col, b_qa), (cw_col, conv_w), (cb_col, conv_b),
                             (bf_col[0:H_A, :], b_forget)):
                act.dma_start(dst, src).then_inc(sem("small_in"), 16)

        HH = RP[:, R2 + 12288:R2 + 14336].rearrange("p (f h n) -> p f h n", f=2, h=2)
        HL = RP[:, R2 + 14336:R2 + 16384].rearrange("p (f h n) -> p f h n", f=2, h=2)
        silu_t = [fv(T0 + 512 * i, 512) for i in range(2)]
        prod_t = [fv(T0 + 1024 + 512 * i, 512) for i in range(2)]
        UNITS = [(0, 0), (1, 0), (0, 1), (1, 1)]
        U4 = [0, 4 * FI]
        U16 = [0, 16 * FI]

        def ffn_pool_first(pool, base):
            for n in range(4):
                lo_piece(pool, base + n, 0, *fseg[n])

        def ffn_pool(pool, base):
            with pool.Fori(0, FI - 1) as i:
                for n in range(4, 10):
                    lo_piece(pool, base + n, 6 * i, *fseg[n % 6])
            for n in range(4, 6):
                lo_piece(pool, base + n, 6 * (FI - 1), *fseg[n])

        def ffn_scalar_first(act, base, free):
            for s, v in free:
                act.wait_ge(s, v)
            for n in range(4):
                hi_piece(act, base + n, 0, fseg[n][0])

        def ffn_scalar(act, r, base, between):
            def gate(i, u):
                f, h = UNITS[u]
                act.wait_ge(sem("f_unit_done"), U4[r] + 4 * i + u + 5)
                act.wait_ge(sem("f_prod"), U4[r] + 4 * i + u + 1)
                nc.scalar.activation(silu_t[u % 2], PS[2 * (u % 2)][:, :], ACT.Silu)\
                    .then_inc(sem("f_silu"), 1)
                act.wait_ge(sem("f_prod"), U4[r] + 4 * i + u + 3)
                act.wait_ge(sem("f_down_done"), U16[r] + 16 * i + 8 + 8 * h)
                nc.scalar.copy(HH[:, f, h, :], prod_t[u % 2]).then_inc(sem("f_h_hi"), 1)

            def down_weights(i):
                act.wait_ge(sem("f_down_done"), U16[r] + 16 * i + 16)
                for n in (4, 5):
                    hi_piece(act, base + n, 6 * i, fseg[n][0])

            with act.Fori(0, FI - 1) as i:
                gate(i, 0)
                gate(i, 1)
                down_weights(i)
                gate(i, 2)
                gate(i, 3)
                for n in range(6, 10):
                    act.wait_ge(sem("f_unit_done"), U4[r] + 4 * i + 7 + (n - 6) // 2)
                    hi_piece(act, base + n, 6 * i, fseg[n - 6][0])
            gate(FI - 1, 0)
            gate(FI - 1, 1)
            down_weights(FI - 1)
            gate(FI - 1, 2)
            between()
            gate(FI - 1, 3)

        def ffn_tensor(pe, r, base, ready, between_first=None):
            def unit(i, u):
                f, h = UNITS[u]
                if h == 0:
                    pe.wait_ge(w_split, base + 6 * i + 2 * f + 2)
                pe.wait_ge(sem("f_prod"), U4[r] + 4 * i + u + 1)
                for g in range(2):
                    wh, wl = fseg[2 * f + g]
                    for k in range(KC):
                        c = slice(k * P, k * P + P)
                        t = slice(h * 512, h * 512 + 512)
                        last = three(pe, PS[2 * (u % 2) + g][:, :], wh[:, c], wl[:, c],
                                     XH[:, k, t], XL[:, k, t], k == 0, k == KC - 1)
                last.then_inc(sem("f_unit_done"), 1)

            def down(i, h):
                pe.wait_ge(w_split, base + 6 * i + 6)
                pe.wait_ge(sem("f_h_lo"), U4[r] + 4 * i + 2 + 2 * h)
                for o in range(8 * h, 8 * h + 8):
                    tl, dh = o // 2 % 4, o % 2
                    pe.wait_ge(sem("f_down_evac"), U16[r] + 16 * i + o + 1)
                    for f in range(2):
                        t = slice(tl * P, tl * P + P)
                        c = slice(dh * 512, dh * 512 + 512)
                        wh, wl = fseg[4 + f]
                        last = three(pe, PS[4 + o % 4][:, :], HH[:, f, h, t], HL[:, f, h, t],
                                     wh[:, c], wl[:, c], f == 0, f == 1)
                    last.then_inc(sem("f_down_done"), 1)

            for s, v in ready:
                pe.wait_ge(s, v)
            if r == 0:
                pe.sem_inc(sem("f_unit_done"), 4)
                pe.sem_inc(sem("f_down_done"), 16)
            if between_first:
                unit(0, 0)
                unit(0, 1)
                between_first()
                unit(0, 2)
                unit(0, 3)
                down(0, 0)
                down(0, 1)
            with pe.Fori(1 if between_first else 0, FI - 1) as i:
                for u in range(4):
                    unit(i, u)
                down(i, 0)
                down(i, 1)
            unit(FI - 1, 0)
            unit(FI - 1, 1)
            unit(FI - 1, 2)
            down(FI - 1, 0)
            unit(FI - 1, 3)
            down(FI - 1, 1)

        def ffn_vector(dve, r, x_ready, evac_hook, half_hook):
            def gate(i, u):
                f, h = UNITS[u]
                dve.wait_ge(sem("f_silu"), U4[r] + 4 * i + u + 1)
                nc.vector.tensor_tensor(prod_t[u % 2], silu_t[u % 2], PS[2 * (u % 2) + 1][:, :], ALU.mult)\
                    .then_inc(sem("f_prod"), 1)
                dve.wait_ge(sem("f_h_hi"), U4[r] + 4 * i + u + 1)
                nc.vector.tensor_tensor(HL[:, f, h, :], prod_t[u % 2], HH[:, f, h, :], ALU.subtract)\
                    .then_inc(sem("f_h_lo"), 1)

            def evac(i, o):
                h, tl, dh = o // 8, o // 2 % 4, o % 2
                xs = X[:, 4 * h + tl, dh * 512:dh * 512 + 512]
                dve.wait_ge(sem("f_down_done"), U16[r] + 16 * i + o + 17)
                nc.vector.scalar_tensor_tensor(out=xs, in0=PS[4 + o % 4][:, :], scalar=0.5, in1=xs,
                                               op0=ALU.mult, op1=ALU.add).then_inc(sem("f_down_evac"), 1)

            if r == 0:
                dve.sem_inc(sem("f_prod"), 2)
                dve.sem_inc(sem("f_down_evac"), 4)
            for s, v in x_ready:
                dve.wait_ge(s, v)
            with dve.Fori(0, FI - 1) as i:
                for u in range(4):
                    gate(i, u)
                for o in range(16):
                    evac(i, o)
            for u in range(3):
                gate(FI - 1, u)
            for h in range(2):
                for tl in range(4):
                    evac(FI - 1, 8 * h + 2 * tl)
                    evac(FI - 1, 8 * h + 2 * tl + 1)
                    if tl:
                        evac_hook(4 * h + tl - 1, U16[r] + 16 * (FI - 1) + 8 * h + 2 * tl + 4)
                evac_hook(4 * h + 3, U16[r] + 16 * (FI - 1) + 8 * h + 12)
                half_hook(h)
                if h == 0:
                    gate(FI - 1, 3)

        def ln_loads(act, r, free):
            for s, v in free:
                act.wait_ge(s, v)
            act.dma_start(lng_t, ln_g[r].partition_broadcast(P)).then_inc(sem("ln_gb_in"), 16)
            act.dma_start(lnb_t, ln_b[r].partition_broadcast(P)).then_inc(sem("ln_gb_in"), 16)

        def ln_stats(dve, r, tt, evac, count):
            dve.wait_ge(evac, count)
            for h in range(2):
                nc.vector.bn_stats(stats[:, tt, 6 * h:6 * h + 6], X[:, tt, 512 * h:512 * h + 512])\
                    .then_inc(sem("ln_st"), 1)
            dve.wait_ge(sem("ln_st"), 16 * r + 2 * tt + 2)
            nc.vector.bn_aggr(mv[:, tt, :], stats[:, tt, :]).then_inc(sem("ln_mv"), 1)

        def ln_centre(dve, r, h):
            t4 = slice(4 * h, 4 * h + 4)
            dve.wait_ge(sem("ln_mv"), 8 * r + 4 * h + 4)
            nc.vector.tensor_scalar(ve[:, t4], mv[:, t4, 1], EPS, None, ALU.add).then_inc(sem("ln_ve"), 1)
            dve.wait_ge(sem("ln_gb_in"), 32 * r + 32)
            for tt in range(4 * h, 4 * h + 4):
                nc.vector.scalar_tensor_tensor(out=X[:, tt, :], in0=X[:, tt, :], scalar=mv[:, tt, 0:1], in1=lng_t,
                                               op0=ALU.subtract, op1=ALU.mult).then_inc(sem("ln_ctr"), 1)
                if tt % 4 == 0:
                    dve.wait_ge(sem("ln_sd"), 2 * r + h + 1)
                    nc.vector.reciprocal(rstd[:, t4], ve[:, t4]).then_inc(sem("ln_rstd"), 1)

        def ln_scale(act, r, h):
            t4 = slice(4 * h, 4 * h + 4)
            act.wait_ge(sem("ln_ve"), 2 * r + h + 1)
            nc.scalar.sqrt(ve[:, t4], ve[:, t4]).then_inc(sem("ln_sd"), 1)
            act.wait_ge(sem("ln_rstd"), 2 * r + h + 1)
            for tt in range(4 * h, 4 * h + 4):
                act.wait_ge(sem("ln_ctr"), 8 * r + tt + 1)
                nc.scalar.mul(X[:, tt, :], X[:, tt, :], rstd[:, tt:tt + 1]).then_inc(sem("ln_n"), 1)

        def ln_offset(pool, r, h):
            for tt in range(4 * h, 4 * h + 4):
                pool.wait_ge(sem("ln_n"), 8 * r + tt + 1)
                nc.gpsimd.tensor_tensor(X[:, tt, :], X[:, tt, :], lnb_t, ALU.add).then_inc(sem("ln_y"), 1)

        def transpose_half(pe, r, h, bank, free):
            for s, v in free:
                pe.wait_ge(s, v)
            for g in range(8 * h, 8 * h + 8):
                tt, j = g // 2, g % 2
                pe.wait_ge(sem("ln_y"), 8 * r + tt + 1)
                if g % 8 >= 4:
                    pe.wait_ge(sem("ln_tr_lo"), 16 * r + g - 3)
                for k in range(4):
                    last = nc.tensor.transpose(PS[bank + g % 4][:, k * P:k * P + P],
                                               X[:, tt, (4 * j + k) * P:(4 * j + k) * P + P], ident)
                last.then_inc(sem("ln_tr"), 1)

        def t_hi(act, r, h, bank):
            for g in range(8 * h, 8 * h + 8):
                tt, j = g // 2, g % 2
                act.wait_ge(sem("ln_tr"), 16 * r + g + 1)
                nc.scalar.copy(XH[:, 4 * j:4 * j + 4, tt * P:tt * P + P],
                               PS[bank + g % 4][:, :].rearrange("p (k n) -> p k n", k=4)).then_inc(sem("ln_tr_hi"), 1)

        def t_lo(dve, r, h, bank):
            for g in range(8 * h, 8 * h + 8):
                tt, j = g // 2, g % 2
                k = slice(4 * j, 4 * j + 4)
                dve.wait_ge(sem("ln_tr_hi"), 16 * r + g + 1)
                nc.vector.tensor_tensor(XL[:, k, tt * P:tt * P + P],
                                        PS[bank + g % 4][:, :].rearrange("p (k n) -> p k n", k=4),
                                        XH[:, k, tt * P:tt * P + P], ALU.subtract).then_inc(sem("ln_tr_lo"), 1)

        def nseg(kh):
            b = R2 + 4096 * kh
            return (RP[:, b:b + 2048].rearrange("p (k n) -> p k n", k=4),
                    RP[:, b + 2048:b + 4096].rearrange("p (k n) -> p k n", k=4))

        def npiece(s, part):
            return nseg(s // 2)[part][:, 2 * (s % 2):2 * (s % 2) + 2, :].rearrange("p k n -> p (k n)")
        bias_nat = fv(G0, NAT)
        stage4 = [fv(14016 + 512 * i, 512) for i in range(4)]

        def nat_pool_first(pool):
            for s in range(4):
                lo_piece(pool, B_NAT + s, 0, npiece(s, 0), npiece(s, 1))

        def nat_pool(pool):
            with pool.Fori(0, NG) as i:
                for s in range(4):
                    lo_piece(pool, B_NAT + 4 + s, 4 * i, npiece(s, 0), npiece(s, 1))

        def nat_scalar_first(act, free):
            for s, v in free:
                act.wait_ge(s, v)
            for s in range(4):
                hi_piece(act, B_NAT + s, 0, npiece(s, 0))

        def nat_tensor(pe, between):
            def group(i, kh, tts):
                wh, wl = nseg(kh)
                for tt in tts:
                    if kh == 0:
                        pe.wait_ge(sem("n_evac"), 8 * i + tt + 1)
                    for k in range(4):
                        t = slice(tt * P, tt * P + P)
                        last = three(pe, PS[tt][:, :], XH[:, 4 * kh + k, t], XL[:, 4 * kh + k, t],
                                     wh[:, k, :], wl[:, k, :], kh == 0 and k == 0, kh == 1 and k == 3)
                    if kh == 1:
                        last.then_inc(sem("n_done"), 1)
                if kh == 0 and tts[-1] == TT - 1:
                    last.then_inc(sem("n_half"), 1)
            pe.wait_ge(w_split, B_NAT + 2)
            pe.wait_ge(sem("ln_tr_lo"), 8)
            group(0, 0, range(0, 4))
            between()
            pe.wait_ge(sem("ln_tr_lo"), 16)
            group(0, 0, range(4, TT))
            pe.wait_ge(w_split, B_NAT + 4)
            group(0, 1, range(TT))
            with pe.Fori(1, NG) as i:
                for kh in range(2):
                    pe.wait_ge(w_split, B_NAT + 4 * i + 2 + 2 * kh)
                    group(i, kh, range(TT))

        def nat_vector(dve):
            dve.wait_ge(sem("f_h_hi"), 4 * FI)
            dve.wait_ge(sem("f_h_lo"), 4 * FI)
            dve.wait_ge(sem("bnat_in"), 16)
            with dve.Fori(0, NG) as i:
                for tt in range(TT):
                    dve.wait_ge(sem("n_done"), 8 * i + tt + 1)
                    dve.wait_ge(sem(f"n_out{tt % 4}"), 32 * i + 16 * (tt // 4) + 16)
                    nc.vector.tensor_tensor(stage4[tt % 4], PS[tt][:, :], bias_nat[:, bass.ts(i, 512)], ALU.add)\
                        .then_inc(sem("n_evac"), 1)

        def nat_scalar(act):
            act.wait_ge(sem("ln_y"), TT)
            act.wait_ge(sem("ln_ctr"), TT)
            act.wait_ge(sem("f_h_lo"), 4 * FI)
            for n in range(4):
                act.sem_inc(sem(f"n_out{n}"), 16)
            act.dma_start(bias_nat, b_nat.partition_broadcast(P)).then_inc(sem("bnat_in"), 16)
            act.dma_start(s_x, X).then_inc(sem("x_out"), 16)

            def round_(i, gated):
                for s in (0, 1):
                    act.wait_ge(sem("n_half"), i + 1)
                    hi_piece(act, B_NAT + 4 + s, 4 * i, npiece(s, 0))
                for tt in range(TT):
                    act.wait_ge(sem("n_evac"), 8 * i + tt + 9)
                    if gated:
                        nc.scalar.activation(stage4[tt % 4], stage4[tt % 4], ACT.Sigmoid).then_inc(sem("n_sig"), 1)
                        act.wait_ge(sem("n_sig"), 8 * i + tt + 1 - 8 * (O_A // 512))
                    act.dma_start(s_nat[tt * P:tt * P + P, bass.ts(i, 512)], stage4[tt % 4])\
                        .then_inc(sem(f"n_out{tt % 4}"), 16)
                for s in (2, 3):
                    act.wait_ge(sem("n_done"), 8 * i + 8)
                    hi_piece(act, B_NAT + 4 + s, 4 * i, npiece(s, 0))
            with act.Fori(0, O_A // 512) as i:
                round_(i, False)
            with act.Fori(O_A // 512, NG) as i:
                round_(i, True)

        GR = W0
        g_i, g_f, g_t, g_u, g_F = (FP[0:H_A, GR + 1024 * n:GR + 1024 * n + 1024] for n in range(5))
        f_raw = FP[32:32 + H_A, GR + 2048:GR + 3072]

        def if_tensor(pe):
            pe.wait_ge(sem("n_evac"), 8 * NG + 8)
            pe.wait_ge(w_split, B_IF + 1)
            wh, wl = cseg[B_IF % 2]
            for h in range(2):
                for k in range(KC):
                    c, t = slice(k * P, k * P + P), slice(h * 512, h * 512 + 512)
                    last = three(pe, PS[4 + h][:, :], wh[:, c], wl[:, c], XH[:, k, t], XL[:, k, t],
                                 k == 0, k == KC - 1)
            last.then_inc(sem("if_done"), 1)

        def if_scalar(act):
            act.wait_ge(sem("if_done"), 1)
            act.wait_ge(sem("x_out"), 16)
            act.wait_ge(sem("ln_tr"), 2 * TT)
            act.wait_ge(sem("small_in"), 96)
            for h in range(2):
                c = slice(512 * h, 512 * h + 512)
                nc.scalar.activation(g_i[:, c], PS[4 + h][0:H_A, :], ACT.Identity, bias=bif_col[0:H_A, :])\
                    .then_inc(sem("if_evac"), 1)
                nc.scalar.activation(f_raw[:, c], PS[4 + h][32:32 + H_A, :], ACT.Identity,
                                     bias=bif_col[32:32 + H_A, :]).then_inc(sem("if_evac"), 1)
            act.wait_ge(sem("if_evac"), 4)
            act.dma_start(g_f, f_raw).then_inc(sem("g_in"), 16)

        def ple0_tensor(pe):
            ph, pl = nseg(0)
            wh, wl = nseg(1)
            ph, pl, wh, wl = (v.rearrange("p k n -> p (k n)").rearrange("p (k n) -> p k n", k=2)
                              for v in (ph, pl, wh, wl))
            for o in range(16):
                tt, dh = o // 2, o % 2
                if o >= 4:
                    pe.wait_ge(sem("st_evac"), o - 3)
                for k in range(2):
                    l, c = slice(tt * P, tt * P + P), slice(dh * 512, dh * 512 + 512)
                    last = three(pe, PS[o % 4][:, :], ph[:, k, l], pl[:, k, l], wh[:, k, c], wl[:, k, c],
                                 k == 0, k == 1)
                last.then_inc(sem("st_done"), 1)

        def ple0_scalar(act):
            for o in range(16):
                act.wait_ge(sem("st_done"), o + 1)
                act.wait_ge(sem(f"n_out{o % 4}"), 16 * (2 * NG + 1 + o // 4))
                nc.scalar.copy(stage4[o % 4], PS[o % 4][:, :]).then_inc(sem("st_evac"), 1)
                act.wait_ge(sem("st_evac"), o + 1)
                act.dma_start(s_ple[o // 2 * P:o // 2 * P + P, o % 2 * 512:o % 2 * 512 + 512],
                              stage4[o % 4]).then_inc(sem(f"n_out{o % 4}"), 16)
        N_OUT = 16 * (2 * NG + 1 + 4)

        def gates_vector(dve):
            n = [0]

            def link(ins):
                n[0] += 1
                ins.then_inc(sem("g_v"), 1)
                dve.wait_ge(sem("g_v"), n[0])
            dve.wait_ge(sem("g_in"), 16)
            dve.wait_ge(sem("if_evac"), 4)
            dve.wait_ge(sem("small_in"), 96)
            link(nc.vector.tensor_scalar(g_f, g_f, bf_col[0:H_A, :], None, ALU.add))
            dve.wait_ge(sem("g_act"), 3)
            link(nc.vector.scalar_tensor_tensor(out=g_u, in0=g_f, scalar=0.0, in1=g_t, op0=ALU.min,
                                                op1=ALU.subtract))
            link(nc.vector.memset(g_t, 0.0))
            link(nc.vector.tensor_tensor_scan(out=g_F, data0=g_u, data1=g_t, initial=0.0, op0=ALU.add, op1=ALU.add))
            link(nc.vector.tensor_tensor(g_i, g_i, g_F, ALU.subtract))
            link(nc.vector.tensor_tensor_scan(out=g_t, data0=g_i, data1=g_i, initial=0.0, op0=ALU.max, op1=ALU.max))
            link(nc.vector.tensor_tensor(g_u, g_F, g_t, ALU.add))

        def gates_columns(dve):
            dve.wait_ge(sem("g_tr"), 1)
            nc.vector.tensor_copy(a_col.rearrange("p h t -> p t h"),
                                  PS[4][:, 0:32].rearrange("p (t h) -> p t h", h=H_A)).then_inc(sem("g_col"), 1)
            nc.vector.tensor_copy(e_col.rearrange("p h t -> p t h"),
                                  PS[4][:, 32:64].rearrange("p (t h) -> p t h", h=H_A)).then_inc(sem("g_col"), 1)

        def gates_scalar(act):
            act.wait_ge(sem("g_v"), 1)
            nc.scalar.activation(g_t, g_f, ACT.Abs).then_inc(sem("g_act"), 1)
            act.wait_ge(sem("g_act"), 1)
            nc.scalar.activation(g_u, g_t, ACT.Exp, scale=-1.0).then_inc(sem("g_act"), 1)
            act.wait_ge(sem("g_act"), 2)
            nc.scalar.activation(g_t, g_u, ACT.Ln, bias=1.0).then_inc(sem("g_act"), 1)
            act.wait_ge(sem("g_v"), 7)
            nc.scalar.activation(g_f, g_u, ACT.Exp, scale=-1.0).then_inc(sem("g_act"), 1)
            act.dma_start(s_m, g_t).then_inc(sem("m_out"), 16)

        def gates_tensor(pe):
            pe.wait_ge(sem("g_act"), 4)
            for n, src in enumerate((g_i, g_f)):
                for tt in range(TT):
                    last = nc.tensor.transpose(PS[4][:, 32 * n + 4 * tt:32 * n + 4 * tt + 4],
                                               src[:, tt * P:tt * P + P], ident[0:H_A, 0:H_A])
            last.then_inc(sem("g_tr"), 1)

        UP = W0 + 5120
        u_pad = [fv(UP + 1028 * j, 1027) for j in range(2)]
        conv_t = [fv(UP + 2056 + 1024 * j, 1024) for j in range(2)]
        conv_o = [fv(UP + 4104 + 1024 * j, 1024) for j in range(2)]

        def half_chunk(pe, wseg, h, bank):
            wh, wl = wseg
            for k in range(KC):
                c, t = slice(k * P, k * P + P), slice(h * 512, h * 512 + 512)
                last = three(pe, PS[bank][:, :], wh[:, c], wl[:, c], XH[:, k, t], XL[:, k, t], k == 0, k == KC - 1)
            return last

        def qa_tensor(pe):
            pe.sem_inc(sem("qa_done"), 4)

            def pair(i):
                for j in range(2):
                    pe.wait_ge(w_split, B_QA + 2 * i + j + 1)
                    for h in range(2):
                        pe.wait_ge(sem(f"qa_evac{h}"), 2 * i + j + 1)
                        half_chunk(pe, cseg[(B_QA + j) % 2], h, 2 * j + h).then_inc(sem("qa_done"), 1)
            pe.wait_ge(sem("st_evac"), 16)
            with pe.Fori(0, NQA // 2 - 1) as i:
                pair(i)
            gates_tensor(pe)
            pair(NQA // 2 - 1)

        def qa_vector(dve):
            dve.wait_ge(sem("n_out3"), N_OUT)
            dve.wait_ge(sem("n_out2"), N_OUT)
            dve.wait_ge(sem("n_out1"), N_OUT)
            dve.wait_ge(sem("n_out0"), N_OUT)
            for j in range(2):
                nc.vector.memset(u_pad[j][:, 0:3], 0.0).then_inc(sem("qa_zero"), 1)
            dve.wait_ge(sem("qa_zero"), 2)
            dve.sem_inc(sem("qa_conv"), 8)

            def pair(i):
                for j in range(2):
                    dve.wait_ge(sem("qa_evac0"), 2 * i + j + 3)
                    dve.wait_ge(sem("qa_evac1"), 2 * i + j + 3)
                    dve.wait_ge(sem("qa_silu"), 2 * i + j + 1)
                    nc.vector.tensor_scalar(conv_t[j], u_pad[j][:, 0:T], cw_col[:, 2 * i + j, 0:1],
                                            cb_col[:, bass.ds(2 * i + j, 1)], ALU.mult, ALU.add)\
                        .then_inc(sem("qa_conv"), 1)
                    for w in range(1, CONV_W):
                        dve.wait_ge(sem("qa_conv"), 8 * i + 4 * j + w + 8)
                        nc.vector.scalar_tensor_tensor(out=conv_t[j], in0=u_pad[j][:, w:w + T],
                                                       scalar=cw_col[:, 2 * i + j, w:w + 1], in1=conv_t[j],
                                                       op0=ALU.mult, op1=ALU.add).then_inc(sem("qa_conv"), 1)
            with dve.Fori(0, NQA // 2 - 1) as i:
                pair(i)
            gates_columns(dve)
            pair(NQA // 2 - 1)

        def qa_scalar(act):
            act.sem_inc(sem("qa_evac0"), 2)
            act.sem_inc(sem("qa_evac1"), 2)
            act.sem_inc(sem("qa_silu"), 2)
            act.sem_inc(sem("qa_out0"), 16)
            act.sem_inc(sem("qa_out1"), 16)
            with act.Fori(0, NQA // 2) as i:
                for j in range(2):
                    for h in range(2):
                        act.wait_ge(sem("qa_done"), 4 * i + 2 * j + h + 5)
                        if h == 0:
                            act.wait_ge(sem("qa_conv"), 8 * i + 4 * j + 4)
                        apart(act, "passed_act")
                        nc.scalar.activation(u_pad[j][:, 3 + 512 * h:515 + 512 * h], PS[2 * j + h][:, :],
                                             ACT.Identity, bias=bqa_col[:, bass.ds(2 * i + j, 1)])\
                            .then_inc(sem(f"qa_evac{h}"), 1)
                    hi_piece(act, B_QA + 2 + j, 2 * i, cseg[(B_QA + j) % 2][0])
                for j in range(2):
                    act.wait_ge(sem("qa_conv"), 8 * i + 4 * j + 12)
                    act.wait_ge(sem(f"qa_out{j}"), 16 * i + 16)
                    nc.scalar.activation(conv_o[j], conv_t[j], ACT.Silu).then_inc(sem("qa_silu"), 1)
                    act.wait_ge(sem("qa_silu"), 2 * i + j + 3)
                    act.dma_start(s_qa[2 * i + j], conv_o[j]).then_inc(sem(f"qa_out{j}"), 16)

        def chunk_pool(pool, n0, count):
            with pool.Fori(0, count // 2) as i:
                for j in range(2):
                    lo_piece(pool, n0 + j, 2 * i, *cseg[(n0 + j) % 2])

        m_q, m_k = fv(W0, 1024), fv(W0 + 1024, 1024)
        m_v = FP[:, W0 + 2048:W0 + 4096].rearrange("p (s n) -> p s n", s=TT)
        m_M = fv(W0 + 4096, 1024)
        m_D = [fv(W0 + 5120 + 512 * j, 512) for j in range(2)]
        m_P = [fv(W0 + 6144 + 512 * j, 512) for j in range(2)]
        m_H = [fv(W0 + 8192 + 256 * j, 256) for j in range(4)]
        ta_stage = [fv(W0 + 9216 + 1024 * j, 1024) for j in range(2)]
        QH, QL, KH, KL = (rv(R2 + 1024 * n, 1024) for n in range(4))
        VW = DV_A + 2
        VH = RP[:, R2 + 4096:R2 + 4096 + TT * VW].rearrange("p (s n) -> p s n", s=TT)
        VL = RP[:, R2 + 4096 + TT * VW:R2 + 4096 + 2 * TT * VW].rearrange("p (s n) -> p s n", s=TT)
        PB = R2 + 4096 + 2 * TT * VW
        PHt = [rv(PB + 512 * j, 512) for j in range(2)]
        PLt = [rv(PB + 1024 + 512 * j, 512) for j in range(2)]
        NCA = NTA // H_A

        def ml_sync(sp):
            sp.wait_ge(sem("g_tr"), 1)
            sp.wait_ge(sem("m_out"), 16)
            with sp.Fori(0, H_A) as i:
                sp.wait_ge(sem("ml_split_v"), i + 1)
                sp.wait_ge(sem("ml_split"), 2 * i + 2)
                for j in range(2):
                    sp.wait_ge(sem(f"qa_out{j}"), 16 * i + 32)
                sp.dma_start(m_q, s_qa[2 * i]).then_inc(sem("ml_in"), 16)
                sp.dma_start(m_k, s_qa[2 * i + 1]).then_inc(sem("ml_in"), 16)
                sp.dma_start(m_v, s_nat[:, bass.ts(i, DV_A)].rearrange("(s p) n -> p s n", p=P))\
                    .then_inc(sem("ml_in"), 16)
                sp.wait_ge(sem("ml_d"), NMU * i + NMU)
                sp.dma_start(m_M, s_m[i].partition_broadcast(P)).then_inc(sem("ml_M_in"), 16)
                load_at(sp, B_TA, 4 * i, 0, 4)

        AHEAD = 2

        def load_at(sp, base, step, a, b):
            for n in range(a, b):
                s = (base + AHEAD + n) % 2
                sp.wait_ge(w_split, base + AHEAD + step + n - 1)
                sp.dma_start(raw[s], w_all[base + AHEAD + step + n]).then_inc(raw_in[s], 16)

        def ml_pool(pool):
            pool.wait_ge(sem("st_done"), 16)
            pool.sem_inc(sem("ml_split"), 2)
            nc.gpsimd.memset(VL[:, :, DV_A:VW].bitcast(F32), 0.0).then_inc(sem("ml_one"), 1)
            nc.gpsimd.memset(VH[:, :, DV_A + 1:VW].bitcast(F32), 0.0).then_inc(sem("ml_one"), 1)
            nc.gpsimd.memset(VH[:, :, DV_A:DV_A + 1].bitcast(F32), 1.0).then_inc(sem("ml_one"), 1)
            with pool.Fori(0, H_A) as i:
                for n, (src, hi, lo) in enumerate([(m_q, QH, QL), (m_k, KH, KL)]):
                    pool.wait_ge(sem("ml_hi"), 3 * i + n + 1)
                    nc.gpsimd.tensor_tensor(lo, src, hi, ALU.subtract).then_inc(sem("ml_split"), 1)
                dg = 0
                for u, (h, sb, t0, n, diag) in enumerate(MU):
                    if diag:
                        pool.wait_ge(sem("ml_d"), NMU * i + u + 1 + NMU)
                        apart(pool, "passed_pool")
                        nc.gpsimd.affine_select(out=m_D[u % 2][:, 0:P], in_=m_D[u % 2][:, 0:P],
                                                compare_op=ALU.is_ge, fill=0.0, base=0, pattern=[[1, P]],
                                                channel_multiplier=-1).then_inc(sem("ml_mask"), 1)
                    if u in (2, 4, 6, 8):
                        lo_piece(pool, B_TA + 1 + u // 2, 4 * i, *cseg[(B_TA + 1 + u // 2) % 2])

        def ml_tensor(pe):
            pe.sem_inc(sem("ml_pv"), 2)
            pe.sem_inc(sem("ml_s"), NMU)
            pe.sem_inc(sem("ta_done"), 2 * NCA)
            pe.wait_ge(sem("g_col"), 2)
            pe.wait_ge(sem("ml_one"), 3)
            pe.wait_ge(sem("qa_evac1"), NQA + 2)
            with pe.Fori(0, H_A) as i:
                def score(u):
                    h, sb, t0, n, diag = MU[u]
                    pe.wait_ge(sem("ml_p"), NMU * i + u + 1)
                    s, t = slice(sb * P, sb * P + P), slice(t0, t0 + n)
                    three(pe, PS[u % 2][:, 0:n], KH[:, s], KL[:, s], QH[:, t], QL[:, t], True, True)\
                        .then_inc(sem("ml_s"), 1)

                def fill(n):
                    j, h = n // 2, n % 2
                    pe.wait_ge(w_split, B_TA + 4 * i + j + 1)
                    pe.wait_ge(sem("ta_evac"), 2 * NCA * i + n + 1)
                    half_chunk(pe, cseg[(B_TA + j) % 2], h, 6 + h).then_inc(sem("ta_done"), 1)

                fill(0)
                fill(1)
                pe.wait_ge(sem("ml_split"), 2 * i + 4)
                score(0)
                for u, (h, sb, t0, n, diag) in enumerate(MU):
                    if u + 1 < NMU:
                        score(u + 1)
                    if 2 <= u + 2 < 2 * NCA:
                        fill(u + 2)
                    if u == 0:
                        pe.wait_ge(sem("ml_split_v"), i + 2)
                    pe.wait_ge(sem("ml_pl"), NMU * i + u + 1)
                    for tl in range((t0 - 512 * h) // P, 4):
                        if sb == 0:
                            pe.wait_ge(sem("ml_nev"), 8 * i + 4 * h + tl + 1)
                        t = slice(512 * h + tl * P - t0, 512 * h + tl * P - t0 + P)
                        last = three(pe, PS[2 + tl][:, 0:VW], PHt[u % 2][:, t], PLt[u % 2][:, t],
                                     VH[:, sb, :], VL[:, sb, :], sb == 0, sb == 4 * h + tl)
                    last.then_inc(sem("ml_pv"), 1)

        def ml_scalar(act):
            act.wait_ge(sem("g_col"), 2)
            act.wait_ge(sem("qa_conv"), 4 * NQA + 8)
            for j in range(2):
                act.wait_ge(sem(f"qa_out{j}"), 8 * NQA + 16)
            act.sem_inc(sem("ml_d"), NMU)
            act.sem_inc(sem("ta_evac"), 2)
            for j in range(2):
                act.sem_inc(sem(f"ta_out{j}"), 16)
            for tl in range(4):
                act.sem_inc(sem(f"ml_out{tl}"), 16)
            with act.Fori(0, H_A) as i:
                def decay(u):
                    h, sb, t0, n, diag = MU[u]
                    act.wait_ge(sem("ml_p"), NMU * i + u + 1)
                    nc.scalar.activation(m_D[u % 2][:, 0:n], m_M[:, t0:t0 + n], ACT.Exp,
                                         bias=a_head[:, sb:sb + 1], scale=-1.0).then_inc(sem("ml_d"), 1)

                def evac(n):
                    j, h = n // 2, n % 2
                    act.wait_ge(sem("ta_done"), 2 * NCA * i + n + 1 + 2 * NCA)
                    act.wait_ge(sem(f"ta_out{h}"), 16 * NCA * i + 16 * j + 16)
                    apart(act, "passed_act")
                    nc.scalar.activation(ta_stage[h][:, 0:512], PS[6 + h][:, :], ACT.Identity,
                                         bias=bt_col[:, bass.ds(4 * i + j, 1)]).then_inc(sem("ta_evac"), 1)
                    act.wait_ge(sem("ta_evac"), 2 * NCA * i + n + 3)
                    act.dma_start(s_t[4 * i + j][:, 512 * h:512 * h + 512], ta_stage[h][:, 0:512])\
                        .then_inc(sem(f"ta_out{h}"), 16)
                    if h:
                        hi_piece(act, B_TA + 2 + j, 4 * i, cseg[(B_TA + j) % 2][0])

                act.wait_ge(sem("ml_in"), 48 * i + 48)
                act.wait_ge(sem("ml_s"), NMU * i + NMU)
                nc.scalar.copy(QH, m_q).then_inc(sem("ml_hi"), 1)
                nc.scalar.copy(KH, m_k).then_inc(sem("ml_hi"), 1)
                act.wait_ge(sem("ml_pv"), NMU * i + 2)
                nc.scalar.copy(VH[:, :, 0:DV_A], m_v).then_inc(sem("ml_hi"), 1)
                act.wait_ge(sem("ml_M_in"), 16 * i + 16)
                act.wait_ge(sem("ml_head"), 2 * i + 2)
                decay(0)
                for u, (h, sb, t0, n, diag) in enumerate(MU):
                    if u + 1 < NMU:
                        decay(u + 1)
                    if u < 2 * NCA:
                        evac(u)
                    act.wait_ge(sem("ml_p"), NMU * i + u + 3)
                    act.wait_ge(sem("ml_pv"), NMU * i + u + 1)
                    nc.scalar.copy(PHt[u % 2][:, 0:n], m_P[u % 2][:, 0:n]).then_inc(sem("ml_ph"), 1)
                    if u and MU[u - 1][4]:
                        store_h(act, i, MU[u - 1])
                store_h(act, i, MU[-1])

        def store_h(act, i, unit):
            h, sb, t0, n, diag = unit
            act.wait_ge(sem("ml_h"), 8 * i + sb + 9)
            act.dma_start(s_h[sb * P:sb * P + P, bass.ts(i, DV_A)], m_H[sb % 4]).then_inc(sem(f"ml_out{sb % 4}"), 16)

        def ml_vector(dve):
            dve.sem_inc(sem("ml_p"), 2)
            dve.sem_inc(sem("ml_nev"), 4)
            dve.sem_inc(sem("ml_h"), 8)
            dve.sem_inc(sem("ml_split_v"), 1)
            dve.wait_ge(sem("g_col"), 2)
            dve.wait_ge(sem("ta_out1"), 16)
            with dve.Fori(0, H_A) as i:
                dve.wait_ge(sem("ml_d"), NMU * i + NMU)
                dve.wait_ge(sem("ml_h"), 8 * i + 8)
                nc.vector.tensor_copy(a_head, a_col[:, i, :]).then_inc(sem("ml_head"), 1)
                nc.vector.tensor_copy(e_head, e_col[:, i, :]).then_inc(sem("ml_head"), 1)
                dve.wait_ge(sem("ml_hi"), 3 * i + 3)
                nc.vector.tensor_tensor(VL[:, :, 0:DV_A], m_v, VH[:, :, 0:DV_A], ALU.subtract)\
                    .then_inc(sem("ml_split_v"), 1)
                dve.wait_ge(sem("ml_head"), 2 * i + 2)

                def tile_out(u):
                    h, sb, t0, n, diag = MU[u]
                    tl = sb - 4 * h
                    dve.wait_ge(sem("ml_pv"), NMU * i + u + 3)
                    bank = PS[2 + tl]
                    nc.vector.tensor_scalar(small[:, 0:1], bank[:, DV_A:DV_A + 1], -1.0, e_head[:, sb:sb + 1],
                                            ALU.mult, ALU.max).then_inc(sem("ml_den"), 1)
                    dve.wait_ge(sem("ml_den"), 24 * i + 3 * sb + 1)
                    nc.vector.tensor_tensor(small[:, 0:1], bank[:, DV_A:DV_A + 1], small[:, 0:1], ALU.max)\
                        .then_inc(sem("ml_den"), 1)
                    dve.wait_ge(sem("ml_den"), 24 * i + 3 * sb + 2)
                    nc.vector.reciprocal(small[:, 1:2], small[:, 0:1]).then_inc(sem("ml_den"), 1)
                    dve.wait_ge(sem("ml_den"), 24 * i + 3 * sb + 3)
                    dve.wait_ge(sem(f"ml_out{tl}"), 32 * i + 16 * h + 16)
                    nc.vector.tensor_scalar(m_H[tl], bank[:, 0:DV_A], small[:, 1:2], None, ALU.mult)\
                        .then_inc(sem("ml_h"), 1)
                    dve.wait_ge(sem("ml_h"), 8 * i + sb + 9)
                    dve.sem_inc(sem("ml_nev"), 1)

                dg = 0
                for u, (h, sb, t0, n, diag) in enumerate(MU):
                    dve.wait_ge(sem("ml_s"), NMU * i + u + 1 + NMU)
                    dve.wait_ge(sem("ml_d"), NMU * i + u + 1 + NMU)
                    if diag:
                        dg += 1
                        dve.wait_ge(sem("ml_mask"), 8 * i + dg)
                    nc.vector.scalar_tensor_tensor(out=m_P[u % 2][:, 0:n], in0=PS[u % 2][:, 0:n],
                                                   scalar=DK_A ** -0.5, in1=m_D[u % 2][:, 0:n],
                                                   op0=ALU.mult, op1=ALU.mult).then_inc(sem("ml_p"), 1)
                    dve.wait_ge(sem("ml_ph"), NMU * i + u + 1)
                    nc.vector.tensor_tensor(PLt[u % 2][:, 0:n], m_P[u % 2][:, 0:n], PHt[u % 2][:, 0:n],
                                            ALU.subtract).then_inc(sem("ml_pl"), 1)
                    if u and MU[u - 1][4]:
                        tile_out(u - 1)
                tile_out(NMU - 1)

        SB_SCALE = DH_B ** -0.5
        A0 = W0
        b_q, b_k = fv(A0, 1024), fv(A0 + 1024, 1024)
        b_v = FP[:, A0 + 2048:A0 + 3072].rearrange("p (s n) -> p s n", s=TT)
        z_t = [fv(A0 + 3072 + 512 * j, 512) for j in range(4)]
        sp_t = [fv(A0 + 5120 + 512 * j, 512) for j in range(4)]
        ag_t = [fv(A0 + 7168 + 512 * j, 512) for j in range(2)]
        yo_t = [fv(A0 + 8192 + 512 * j, 512) for j in range(2)]
        tb_stage = [fv(A0 + 9216 + 512 * j, 512) for j in range(2)]
        hn_h, hn_o, mhg_t = fv(A0 + 10240, 1024), fv(A0 + 11264, 1024), fv(A0 + 12288, 1024)
        BQH, BQL, BKH, BKL, BVH, BVL = (rv(R2 + 1024 * n, 1024) for n in range(6))
        SPH = [rv(R2 + 6144 + 512 * j, 512) for j in range(3)]
        SPL = [rv(R2 + 7680 + 512 * j, 512) for j in range(3)]
        WH = [rv(R2 + 9216 + 512 * j, 512) for j in range(3)]
        WL = [rv(R2 + 10752 + 512 * j, 512) for j in range(3)]
        LAG_TRI, LAG_W, LAG_LOW, LAG_AV = 3, 4, 5, 6
        STEPS = NAU + LAG_AV
        NCB = (NTC - NTA) // H_B
        FS = 4
        FILLED = {FS * n + FS: n for n in range(2 * NCB)}
        TR_AT = 2 * NCB * FS

        def ndiag(n):
            return sum(1 for a in AU[:n] if a[4])

        def at_sync(sp):
            for tl in range(4):
                sp.wait_ge(sem(f"ml_out{tl}"), 16 * 2 * H_A + 16)
            sp.wait_ge(sem("ml_p"), NMU * H_A + 2)
            sp.wait_ge(sem("ml_pl"), NMU * H_A)
            for h in range(2):
                sp.wait_ge(sem(f"ta_out{h}"), 16 * NTA + 16)
            sp.dma_start(mhg_t, mh_g.partition_broadcast(P)).then_inc(sem("hn_g"), 16)
            with sp.Fori(0, H_B) as i:
                sp.wait_ge(sem("at_split"), 3 * i + 3)
                sp.dma_start(b_q, s_t[i + TC_Q]).then_inc(sem("at_in"), 16)
                sp.dma_start(b_k, s_t[i + TC_K]).then_inc(sem("at_in"), 16)
                sp.dma_start(b_v, s_nat[:, bass.ds(i * DH_B + V_B, DH_B)].rearrange("(s p) n -> p s n", p=P))\
                    .then_inc(sem("at_in"), 16)
                load_at(sp, B_TB, 2 * i, 0, 1)
                sp.wait_ge(sem("hn_tr"), i + 1)
                sp.dma_start(hn_h, s_h[bass.ts(i, P), :]).then_inc(sem("hn_in"), 16)
                sp.wait_ge(sem("hn_out"), 16 * i + 16)
                sp.dma_start(hn_o, s_nat[bass.ts(i, P), O_A:O_A + 1024]).then_inc(sem("hn_oin"), 16)
                load_at(sp, B_TB, 2 * i, 1, 2)

        def at_pool(pool):
            def split(i, n):
                src, hi, lo = [(b_q, BQH, BQL), (b_k, BKH, BKL),
                               (b_v, BVH.rearrange("p (s n) -> p s n", s=TT),
                                BVL.rearrange("p (s n) -> p s n", s=TT))][n]
                pool.wait_ge(sem("at_hi"), 3 * i + n + 1)
                nc.gpsimd.tensor_tensor(lo, src, hi, ALU.subtract).then_inc(sem("at_split"), 1)

            def head(i, more):
                for s in range(STEPS):
                    if s < NAU and AU[s][4]:
                        pool.wait_ge(sem("at_z"), NAU * i + s + 3)
                        apart(pool, "passed_pool")
                        nc.gpsimd.affine_select(out=z_t[s % 4][:, 0:P], in_=z_t[s % 4][:, 0:P],
                                                compare_op=ALU.is_gt, fill=-1e30, base=0, pattern=[[1, P]],
                                                channel_multiplier=-1).then_inc(sem("at_mask"), 1)
                    if 0 <= s - 2 < NAU:
                        u = s - 2
                        n = AU[u][3]
                        pool.wait_ge(sem("at_sph"), NAU * i + u + 1)
                        nc.gpsimd.tensor_tensor(SPL[u % 3][:, 0:n], sp_t[u % 4][:, 0:n], SPH[u % 3][:, 0:n],
                                                ALU.subtract).then_inc(sem("at_spl"), 1)
                    if s == 3:
                        split(i, 2)
                    if s == 9:
                        lo_piece(pool, B_TB + 2, 2 * i, *cseg[B_TB % 2])
                    if s in (14, 15) and more:
                        split(i + 1, s - 14)
                lo_piece(pool, B_TB + 3, 2 * i, *cseg[(B_TB + 1) % 2])

            pool.sem_inc(sem("at_split"), 3)
            split(0, 0)
            split(0, 1)
            with pool.Fori(0, H_B - 1) as i:
                head(i, True)
            head(H_B - 1, False)

        def at_tensor(pe):
            pe.sem_inc(sem("at_pv"), NAU)
            pe.sem_inc(sem("at_s"), NAU)
            pe.sem_inc(sem("at_tric"), 3)
            pe.sem_inc(sem("tb_done"), 2 * NCB)
            pe.sem_inc(sem("hn_tr"), 1)
            pe.wait_ge(sem("ml_nev"), 8 * H_A + 4)
            pe.wait_ge(sem("ta_evac"), 2 * NTA + 2)

            def head(i):
                for s in range(STEPS):
                    if s < NAU:
                        h, sb, t0, n, diag = AU[s]
                        if s == 0:
                            pe.wait_ge(sem("at_split"), 3 * i + 5)
                        pe.wait_ge(sem("at_z"), NAU * i + s + 1)
                        ks, t = slice(sb * P, sb * P + P), slice(t0, t0 + n)
                        three(pe, PS[s % 2][:, 0:n], BKH[:, ks], BKL[:, ks], BQH[:, t], BQL[:, t], True, True)\
                            .then_inc(sem("at_s"), 1)
                    if 0 <= s - LAG_TRI < NAU:
                        u = s - LAG_TRI
                        h, sb, t0, n, diag = AU[u]
                        first = sb == 4 * h + 3
                        c = slice(t0 - 512 * h, 512)
                        pe.wait_ge(sem("at_spl"), NAU * i + u + 1)
                        nc.tensor.matmul(PS[2 + h][:, c], TRI, SPH[u % 3][:, 0:n], start=first, stop=False,
                                         skip_group_check=True)
                        nc.tensor.matmul(PS[2 + h][:, c], TRI, SPL[u % 3][:, 0:n], start=False, stop=True,
                                         skip_group_check=True).then_inc(sem("at_tri"), 1)
                    if s < 2 * NCB * FS:
                        n = s // FS
                        j, fh = n // 2, n % 2
                        if s % FS == 0:
                            pe.wait_ge(w_split, B_TB + 2 * i + j + 1)
                            pe.wait_ge(sem("tb_evac"), 6 * i + n + 1)
                        wh, wl = cseg[(B_TB + j) % 2]
                        for k in range(KC // FS * (s % FS), KC // FS * (s % FS + 1)):
                            c, t = slice(k * P, k * P + P), slice(fh * 512, fh * 512 + 512)
                            last = three(pe, PS[6 + fh][:, :], wh[:, c], wl[:, c], XH[:, k, t], XL[:, k, t],
                                         k == 0, k == KC - 1)
                        if s % FS == FS - 1:
                            last.then_inc(sem("tb_done"), 1)
                    if 0 <= s - LAG_AV < NAU:
                        u = s - LAG_AV
                        h, sb, t0, n, diag = AU[u]
                        first = sb == 4 * h + 3
                        if u == 0:
                            pe.wait_ge(sem("at_split"), 3 * i + 6)
                        if first:
                            pe.wait_ge(sem("at_yev"), 2 * i + h + 1)
                        pe.wait_ge(sem("at_wl"), NAU * i + u + 1 + 1)
                        v = slice(sb * P, sb * P + P)
                        three(pe, PS[4 + h][:, t0 - 512 * h:512], BVH[:, v], BVL[:, v], WH[u % 3][:, 0:n],
                              WL[u % 3][:, 0:n], first, sb == 0, skip=True).then_inc(sem("at_pv"), 1)
                    if s >= TR_AT:
                        b = s - TR_AT
                        pe.wait_ge(sem("hn_y"), 4 * i + 2 * b + 2)
                        pe.wait_ge(sem("tb_evac"), 6 * i + 4 + b + 1)
                        for k in range(4):
                            c = (4 * b + k) * P
                            last = nc.tensor.transpose(PS[6 + b][:, k * P:k * P + P], hn_h[:, c:c + P], ident)
                        last.then_inc(sem("hn_tr" if b else "hn_tr0"), 1)
                    if 0 <= s - LAG_TRI < NAU:
                        u = s - LAG_TRI
                        h, sb, t0, n, diag = AU[u]
                        c = slice(t0 - 512 * h, 512)
                        pe.wait_ge(sem("at_arg"), NAU * i + u + 1 + 1)
                        nc.tensor.matmul(PS[2 + h][:, c], TRIC, SPH[u % 3][:, 0:n], start=False, stop=False,
                                         skip_group_check=True)
                        nc.tensor.matmul(PS[2 + h][:, c], TRIC, SPL[u % 3][:, 0:n], start=False, stop=True,
                                         skip_group_check=True).then_inc(sem("at_tric"), 1)

            with pe.Fori(0, H_B) as i:
                head(i)

        def at_scalar(act):
            act.sem_inc(sem("at_z"), 2)
            act.sem_inc(sem("hn_out"), 16)
            for h in range(2):
                act.sem_inc(sem(f"tb_out{h}"), 16)
                act.sem_inc(sem(f"at_out{h}"), 16)

            def round_qk(i, dst, src):
                act.wait_ge(sem("at_in"), 48 * i + 48)
                act.wait_ge(sem("at_s"), NAU * i + NAU)
                nc.scalar.copy(dst, src).then_inc(sem("at_hi"), 1)

            def head(i, more):
                for s in range(STEPS):
                    if s < NAU:
                        n = AU[s][3]
                        act.wait_ge(sem("at_s"), NAU * i + s + 1 + NAU)
                        if s >= 4:
                            act.wait_ge(sem("at_arg"), NAU * i + s - 3 + 1)
                        else:
                            act.wait_ge(sem("at_arg"), NAU * i + 1)
                        nc.scalar.activation(z_t[s % 4][:, 0:n], PS[s % 2][:, 0:n], ACT.Copy, scale=SB_SCALE)\
                            .then_inc(sem("at_z"), 1)
                    if s == 2:
                        act.wait_ge(sem("at_pv"), NAU * i + NAU)
                        nc.scalar.copy(BVH.rearrange("p (s n) -> p s n", s=TT), b_v).then_inc(sem("at_hi"), 1)
                    if s in (13, 14) and more:
                        round_qk(i + 1, *((BQH, b_q), (BKH, b_k))[s - 13])
                    if s == 4:
                        act.wait_ge(sem("hn_ve"), i + 1)
                        nc.scalar.activation(ve[:, 0:4], ve[:, 0:4], ACT.Ln).then_inc(sem("hn_sd"), 1)
                    if s == 5:
                        act.wait_ge(sem("hn_sd"), 2 * i + 1)
                        nc.scalar.activation(rstd[:, 0:4], ve[:, 0:4], ACT.Exp, scale=-0.5).then_inc(sem("hn_sd"), 1)
                    if s == 8:
                        act.wait_ge(sem("tb_done"), 2 * NCB + 4 * i + 2)
                        hi_piece(act, B_TB + 2, 2 * i, cseg[B_TB % 2][0])
                    if 0 <= s - 1 < NAU:
                        u = s - 1
                        n = AU[u][3]
                        act.wait_ge(sem("at_cl"), NAU * i + u + 1)
                        nc.scalar.activation(sp_t[u % 4][:, 0:n], sp_t[u % 4][:, 0:n], ACT.Exp)\
                            .then_inc(sem("at_ex"), 1)
                    if 0 <= s - LAG_W < NAU:
                        u = s - LAG_W
                        n = AU[u][3]
                        act.wait_ge(sem("at_arg"), NAU * i + u + 1 + 1)
                        nc.scalar.activation(ag_t[u % 2][:, 0:n], ag_t[u % 2][:, 0:n], ACT.Exp)\
                            .then_inc(sem("at_w"), 1)
                    if 0 <= s - 1 < NAU:
                        u = s - 1
                        n = AU[u][3]
                        act.wait_ge(sem("at_ex"), NAU * i + u + 1)
                        nc.scalar.activation(sp_t[u % 4][:, 0:n], sp_t[u % 4][:, 0:n], ACT.Ln, bias=1.0)\
                            .then_inc(sem("at_ln"), 1)
                    if 0 <= s - LAG_W < NAU:
                        u = s - LAG_W
                        n = AU[u][3]
                        act.wait_ge(sem("at_w"), NAU * i + u + 1)
                        act.wait_ge(sem("at_pv"), NAU * i + max(u - 2, 0) + NAU)
                        nc.scalar.copy(WH[u % 3][:, 0:n], ag_t[u % 2][:, 0:n]).then_inc(sem("at_wh"), 1)
                    if s - 1 in FILLED:
                        n = FILLED[s - 1]
                        act.wait_ge(sem("tb_evac"), 6 * i + n + 3)
                        act.dma_start(s_t[2 * i + (NTA + n // 2)][:, 512 * (n % 2):512 * (n % 2) + 512], tb_stage[n % 2])\
                            .then_inc(sem(f"tb_out{n % 2}"), 16)
                    if s == 11:
                        act.wait_ge(sem("at_yev"), 2 * i + 3)
                        act.dma_start(s_yb[i][:, 0:512], yo_t[0]).then_inc(sem("at_out0"), 16)
                act.wait_ge(sem("tb_done"), 2 * NCB + 4 * i + 4)
                hi_piece(act, B_TB + 3, 2 * i, cseg[(B_TB + 1) % 2][0])
                act.wait_ge(sem("tb_evac"), 6 * i + 8)
                act.dma_start(s_ya[:, :, bass.ts(i, P)].rearrange("k p n -> p k n"),
                              hn_o.rearrange("p (k n) -> p k n", k=KC)).then_inc(sem("hn_out"), 16)
                act.wait_ge(sem("at_yev"), 2 * i + 4)
                act.dma_start(s_yb[i][:, 512:1024], yo_t[1]).then_inc(sem("at_out1"), 16)

            round_qk(0, BQH, b_q)
            round_qk(0, BKH, b_k)
            with act.Fori(0, H_B - 1) as i:
                head(i, True)
            head(H_B - 1, False)

        def at_vector(dve):
            dve.sem_inc(sem("at_yev"), 2)
            dve.sem_inc(sem("at_arg"), 1)
            dve.sem_inc(sem("at_wl"), 1)
            dve.sem_inc(sem("tb_evac"), 2)
            dve.wait_ge(sem("hn_g"), 16)
            st = small[:, 0:24].rearrange("p (h s) -> p h s", h=H_A)
            m = small[:, 24:32].rearrange("p (h s) -> p h s", h=H_A)
            with dve.Fori(0, H_B) as i:
                def evac(n):
                    j, h = n // 2, n % 2
                    dve.wait_ge(sem("tb_done"), 4 * i + n + 1 + 2 * NCB)
                    dve.wait_ge(sem(f"tb_out{h}"), 32 * i + 16 * j + 16)
                    nc.vector.tensor_scalar(tb_stage[h], PS[6 + h][:, :], bt_col[:, bass.ds(2 * i + (NTA + j), 1)], None,
                                            ALU.add).then_inc(sem("tb_evac"), 1)

                for s in range(STEPS):
                    if s == 3:
                        dve.wait_ge(sem("hn_in"), 16 * i + 16)
                        for h in range(H_A):
                            nc.vector.bn_stats(st[:, h, :], hn_h[:, h * DV_A:(h + 1) * DV_A]).then_inc(sem("hn_st"), 1)
                        dve.wait_ge(sem("hn_st"), 4 * i + 4)
                        apart(dve, "passed_dve")
                        for h in range(H_A):
                            nc.vector.bn_aggr(m[:, h, :], st[:, h, :]).then_inc(sem("hn_mv"), 1)
                        dve.wait_ge(sem("hn_mv"), 4 * i + 4)
                        nc.vector.tensor_scalar(ve[:, 0:4], m[:, :, 1], EPS, None, ALU.add).then_inc(sem("hn_ve"), 1)
                    if 0 <= s - 2 < NAU:
                        u = s - 2
                        n = AU[u][3]
                        dve.wait_ge(sem("at_ln"), NAU * i + u + 1)
                        nc.vector.tensor_tensor(sp_t[u % 4][:, 0:n], sp_t[u % 4][:, 0:n], z_t[u % 4][:, 0:n], ALU.max)\
                            .then_inc(sem("at_sp"), 1)
                    if 0 <= s - LAG_LOW < NAU:
                        u = s - LAG_LOW
                        n = AU[u][3]
                        dve.wait_ge(sem("at_wh"), NAU * i + u + 1)
                        nc.vector.tensor_tensor(WL[u % 3][:, 0:n], ag_t[u % 2][:, 0:n], WH[u % 3][:, 0:n],
                                                ALU.subtract).then_inc(sem("at_wl"), 1)
                    if 0 <= s - 2 < NAU:
                        u = s - 2
                        n = AU[u][3]
                        dve.wait_ge(sem("at_sp"), NAU * i + u + 1)
                        dve.wait_ge(sem("at_tric"), NAU * i + u + 1)
                        nc.vector.tensor_copy(SPH[u % 3][:, 0:n], sp_t[u % 4][:, 0:n]).then_inc(sem("at_sph"), 1)
                    if 0 <= s - LAG_TRI < NAU:
                        u = s - LAG_TRI
                        h, sb, t0, n, diag = AU[u]
                        dve.wait_ge(sem("at_tri"), NAU * i + u + 1)
                        dve.wait_ge(sem("at_wl"), NAU * i + max(u - 1, 0) + 1)
                        nc.vector.tensor_tensor(ag_t[u % 2][:, 0:n], z_t[u % 4][:, 0:n],
                                                PS[2 + h][:, t0 - 512 * h:512], ALU.subtract).then_inc(sem("at_arg"), 1)
                    if s in FILLED:
                        evac(FILLED[s])
                    if s < NAU:
                        n = AU[s][3]
                        dve.wait_ge(sem("at_z"), NAU * i + s + 3)
                        if AU[s][4]:
                            dve.wait_ge(sem("at_mask"), 8 * i + ndiag(s + 1))
                        if s >= 4:
                            dve.wait_ge(sem("at_spl"), NAU * i + s - 3)
                        nc.vector.tensor_scalar(sp_t[s % 4][:, 0:n], z_t[s % 4][:, 0:n], 80.0, None, ALU.min)\
                            .then_inc(sem("at_cl"), 1)
                    if s == 6:
                        for h in range(H_A):
                            c = slice(h * DV_A, (h + 1) * DV_A)
                            nc.vector.scalar_tensor_tensor(out=hn_h[:, c], in0=hn_h[:, c], scalar=m[:, h, 0:1],
                                                           in1=mhg_t[:, c], op0=ALU.subtract, op1=ALU.mult)\
                                .then_inc(sem("hn_c"), 1)
                    if s == 8:
                        dve.wait_ge(sem("hn_sd"), 2 * i + 2)
                        dve.wait_ge(sem("hn_oin"), 16 * i + 16)
                        dve.wait_ge(sem("hn_c"), 4 * i + 4)
                        for h in range(H_A):
                            c = slice(h * DV_A, (h + 1) * DV_A)
                            nc.vector.scalar_tensor_tensor(out=hn_h[:, c], in0=hn_h[:, c], scalar=rstd[:, h:h + 1],
                                                           in1=hn_o[:, c], op0=ALU.mult, op1=ALU.mult)\
                                .then_inc(sem("hn_y"), 1)
                    if s == 10:
                        dve.wait_ge(sem("at_pv"), NAU * i + 4 + NAU)
                        dve.wait_ge(sem("at_out0"), 16 * i + 16)
                        nc.vector.tensor_copy(yo_t[0], PS[4][:, :]).then_inc(sem("at_yev"), 1)
                    if s == TR_AT + 1:
                        dve.wait_ge(sem("hn_tr0"), i + 1)
                        dve.wait_ge(sem("hn_y"), 4 * i + 4)
                        nc.vector.tensor_copy(hn_o[:, 0:512], PS[6][:, :]).then_inc(sem("tb_evac"), 1)
                dve.wait_ge(sem("hn_tr"), i + 2)
                nc.vector.tensor_copy(hn_o[:, 512:1024], PS[7][:, :]).then_inc(sem("tb_evac"), 1)
                dve.wait_ge(sem("at_pv"), NAU * i + NAU + NAU)
                dve.wait_ge(sem("at_out1"), 16 * i + 16)
                nc.vector.tensor_copy(yo_t[1], PS[5][:, :]).then_inc(sem("at_yev"), 1)

        YH = RP[:, 0:8192].rearrange("p (a k n) -> p a k n", a=2, k=KC)
        YL = RP[:, 8192:16384].rearrange("p (a k n) -> p a k n", a=2, k=KC)
        MH = RP[:, R2:R2 + 8192].rearrange("p (k n) -> p k n", k=KC)
        ML = RP[:, R2 + 8192:R2 + 16384].rearrange("p (k n) -> p k n", k=KC)
        BR0 = W0
        y_raw = FP[:, BR0:BR0 + 8192].rearrange("p (a k n) -> p a k n", a=2, k=KC)
        bg_t = [[fv(BR0 + 8192 + 1024 * j + 512 * a, 512) for a in range(2)] for j in range(2)]
        br_t = [[fv(BR0 + 10240 + 1024 * j + 512 * a, 512) for a in range(2)] for j in range(2)]
        Y_PARTS = [(a, slice(4 * kh, 4 * kh + 4)) for a in range(2) for kh in range(2)]

        def br_sync(sp):
            for h in range(2):
                sp.wait_ge(sem(f"at_out{h}"), 16 * H_B + 16)
                sp.wait_ge(sem(f"tb_out{h}"), 16 * (NTC - NTA) + 16)
            sp.wait_ge(sem("hn_out"), 16 * H_B + 16)
            sp.wait_ge(sem("at_wl"), NAU * H_B + 1)
            for h in range(2):
                t = slice(512 * h, 512 * h + 512)
                for n, (a, ks) in enumerate(Y_PARTS):
                    if h:
                        sp.wait_ge(sem("br_ylo"), n + 1)
                    sp.dma_start(y_raw[:, a, ks, :], (s_yb if a else s_ya)[ks, :, t].rearrange("k p n -> p k n"))\
                        .then_inc(sem(f"br_yin{n}"), 16)
                for c in range(KC):
                    m = KC * h + c
                    j = m % 2
                    if m >= 2:
                        sp.wait_ge(sem("br_m"), 3 * (m - 1))
                    for a, tc in ((0, TC_GA), (1, TC_GB)):
                        sp.dma_start(bg_t[j][a], s_t[tc + c][:, t]).then_inc(sem(f"br_gin{j}"), 16)
                    load_at(sp, B_BR, 0, 2 * m, 2 * m + 2)

        def br_pool(pool):
            for n in range(2, 2 * 2 * KC):
                lo_piece(pool, B_BR + n, 0, *cseg[(B_BR + n) % 2])

        def br_tensor(pe):
            pe.wait_ge(sem("at_yev"), 2 * H_B + 2)
            pe.wait_ge(sem("tb_evac"), 6 * H_B + 2)
            for m in range(2 * KC):
                h, j = m // KC, m % 2
                for a in range(2):
                    wh, wl = cseg[(B_BR + a) % 2]
                    pe.wait_ge(w_split, B_BR + 2 * m + a + 1)
                    if m >= 2:
                        pe.wait_ge(sem("br_m"), 3 * (m - 1))
                    for k in range(KC):
                        if m % KC == 0 and k % 4 == 0:
                            pe.wait_ge(sem("br_ylo"), 4 * h + 2 * a + k // 4 + 1)
                        c = slice(k * P, k * P + P)
                        last = three(pe, PS[2 * j + a][:, :], wh[:, c], wl[:, c], YH[:, a, k, :], YL[:, a, k, :],
                                     k == 0, k == KC - 1)
                    last.then_inc(sem("br_done"), 1)

        def br_scalar(act):
            act.wait_ge(sem("at_pv"), NAU * H_B + NAU)
            act.wait_ge(sem("tb_done"), 4 * H_B + 2 * NCB)
            for m in range(2 * KC):
                h, c, j = m // KC, m % KC, m % 2
                if c == 0:
                    for n, (a, ks) in enumerate(Y_PARTS):
                        act.wait_ge(sem(f"br_yin{n}"), 16 * h + 16)
                        if h:
                            act.wait_ge(sem("br_done"), 2 * KC)
                        nc.scalar.copy(YH[:, a, ks, :], y_raw[:, a, ks, :]).then_inc(sem("br_yhi"), 1)
                act.wait_ge(sem(f"br_gin{j}"), 32 * (m // 2) + 32)
                for a in range(2):
                    nc.scalar.activation(bg_t[j][a], bg_t[j][a], ACT.Sigmoid).then_inc(sem("br_sig"), 1)
                    if m < 2 * KC - 1:
                        act.wait_ge(sem("br_done"), 2 * m + a + 1)
                        hi_piece(act, B_BR + 2 + 2 * m + a, 0, cseg[(B_BR + a) % 2][0])
                act.wait_ge(sem("br_m"), 3 * m + 3)
                nc.scalar.copy(MH[:, c, 512 * h:512 * h + 512], br_t[j][0]).then_inc(sem("br_mhi"), 1)

        def br_vector(dve):
            for m in range(2 * KC):
                h, c, j = m // KC, m % KC, m % 2
                if c == 0:
                    for n, (a, ks) in enumerate(Y_PARTS):
                        dve.wait_ge(sem("br_yhi"), 4 * h + n + 1)
                        nc.vector.tensor_tensor(YL[:, a, ks, :], y_raw[:, a, ks, :], YH[:, a, ks, :], ALU.subtract)\
                            .then_inc(sem("br_ylo"), 1)
                if m >= 2:
                    dve.wait_ge(sem("br_mlo"), m - 1)
                for a in range(2):
                    dve.wait_ge(sem("br_sig"), 2 * m + a + 1)
                    dve.wait_ge(sem("br_done"), 2 * m + a + 1)
                    nc.vector.tensor_tensor(br_t[j][a], PS[2 * j + a][:, :], bg_t[j][a], ALU.mult)\
                        .then_inc(sem("br_m"), 1)
                dve.wait_ge(sem("br_m"), 3 * m + 2)
                nc.vector.tensor_tensor(br_t[j][0], br_t[j][0], br_t[j][1], ALU.add).then_inc(sem("br_m"), 1)
                dve.wait_ge(sem("br_mhi"), m + 1)
                nc.vector.tensor_tensor(ML[:, c, 512 * h:512 * h + 512], br_t[j][0],
                                        MH[:, c, 512 * h:512 * h + 512], ALU.subtract).then_inc(sem("br_mlo"), 1)

        def full_pool(pool, base, hi, lo):
            for k in range(KC):
                lo_piece(pool, base + k, 0, hi[:, k, :], lo[:, k, :])

        def full_scalar(act, base, hi, ks):
            for k in ks:
                hi_piece(act, base + k, 0, hi[:, k, :])

        def full_tensor(pe, q, base, left, right, ready, between):
            (lh, ll), (rh, rl) = left, right

            def product(o, k):
                tt, dh = o // 2, o % 2
                t, c = slice(tt * P, tt * P + P), slice(dh * 512, dh * 512 + 512)
                return three(pe, PS[o % 8][:, :], lh[:, k, t], ll[:, k, t], rh[:, k, c], rl[:, k, c],
                             k == 0, k == KC - 1)
            for s, v in ready:
                pe.wait_ge(s, v)
            for k in range(KC):
                pe.wait_ge(w_split, base + k + 1)
                for o in range(8):
                    last = product(o, k)
                    if k == KC - 1:
                        last.then_inc(sem(q + "done"), 1)
            between()
            for o in range(8, 16):
                pe.wait_ge(sem(q + "evac"), o - 7)
                for k in range(KC):
                    last = product(o, k)
                last.then_inc(sem(q + "done"), 1)

        def mix_scalar(act):
            act.wait_ge(sem("br_done"), 4 * KC)
            full_scalar(act, B_MIX, XH, (0, 1))
            act.wait_ge(sem("br_mlo"), 2 * KC)
            for tt in range(TT):
                act.dma_start(X[:, tt, :], s_x[:, tt, :]).then_inc(sem(f"x_back{tt % 2}"), 16)
                full_scalar(act, B_MIX, XH, [tt + 2] if tt + 2 < KC else [])
                if tt >= 1:
                    act.wait_ge(sem(f"x_back{(tt - 1) % 2}"), 16 * ((tt - 1) // 2) + 16)
                    scale_x(act, tt - 1)
            act.wait_ge(sem(f"x_back{(TT - 1) % 2}"), 16 * ((TT - 1) // 2) + 16)
            scale_x(act, TT - 1)

        def mix_vector(dve):
            for o in range(16):
                tt, dh = o // 2, o % 2
                xs = X[:, tt, dh * 512:dh * 512 + 512]
                dve.wait_ge(sem("mx_done"), o + 1)
                dve.wait_ge(sem("x_scaled"), TT + tt + 1)
                nc.vector.tensor_tensor(xs, PS[o % 8][:, :], xs, ALU.add).then_inc(sem("mx_evac"), 1)
                if o % 2:
                    ln_stats(dve, 1, tt, sem("mx_evac"), o + 1)
                if o == 7:
                    ln_centre(dve, 1, 0)
            t_lo(dve, 1, 0, 0)
            ln_centre(dve, 1, 1)
            t_lo(dve, 1, 1, 4)

        bple_t = fv(G0, D)
        gate_t = [fv(T0 + 512 * j, 512) for j in range(4)]
        pl_t = [fv(T0 + 2048 + 512 * j, 512) for j in range(2)]
        PWH = RP[:, R2:R2 + 8192].rearrange("p (k n) -> p k n", k=KC)
        PWL = RP[:, R2 + 8192:R2 + 16384].rearrange("p (k n) -> p k n", k=KC)

        def ple_sigmoid(act, o):
            act.wait_ge(sem("pg_evac"), o + 1)
            nc.scalar.activation(gate_t[o % 4], gate_t[o % 4], ACT.Sigmoid).then_inc(sem("pg_sig"), 1)

        def ple_sync(sp):
            sp.wait_ge(sem("f_h_lo"), 8 * FI)
            for o in range(16):
                if o >= 2:
                    sp.wait_ge(sem("pg_mul"), o - 1)
                sp.dma_start(pl_t[o % 2], s_ple[o // 2 * P:o // 2 * P + P, o % 2 * 512:o % 2 * 512 + 512])\
                    .then_inc(sem(f"pl_in{o % 2}"), 16)

        def ple_evac(dve, o):
            dve.wait_ge(sem("pg_done"), o + 1)
            if o >= 4:
                dve.wait_ge(sem("pg_mul"), o - 3)
            c = slice(o % 2 * 512, o % 2 * 512 + 512)
            nc.vector.tensor_tensor(gate_t[o % 4], PS[o % 8][:, :], bple_t[:, c], ALU.add).then_inc(sem("pg_evac"), 1)

        def ple_add(dve, o):
            tt, dh = o // 2, o % 2
            xs = X[:, tt, dh * 512:dh * 512 + 512]
            dve.wait_ge(sem("pg_sig"), o + 1)
            dve.wait_ge(sem(f"pl_in{o % 2}"), 16 * (o // 2) + 16)
            nc.vector.tensor_tensor(gate_t[o % 4], gate_t[o % 4], pl_t[o % 2], ALU.mult).then_inc(sem("pg_mul"), 1)
            dve.wait_ge(sem("pg_mul"), o + 1)
            dve.wait_ge(sem("x_scaled"), 3 * TT + tt + 1)
            nc.vector.tensor_tensor(xs, gate_t[o % 4], xs, ALU.add).then_inc(sem("pg_add"), 1)
            if dh:
                ln_stats(dve, 3, tt, sem("pg_add"), o + 1)

        @blk.sync
        def _(sp):
            for s in range(2):
                sp.dma_start(raw[s], w_all[s]).then_inc(raw_in[s], 16)
            with sp.Fori(1, (B_TA + 1) // 2) as j:
                load_pair(sp, j)
            load_at(sp, B_TA, 0, -1, 0)
            ml_sync(sp)
            at_sync(sp)
            br_sync(sp)
            load_at(sp, B_MIX, 0, 0, 1)
            with sp.Fori((B_MIX + AHEAD + 1) // 2, N_PIECES // 2) as j:
                load_pair(sp, j)
            sp.wait_ge(w_split, N_PIECES - 2)
            sp.dma_start(raw[0], w_all[N_PIECES - 1]).then_inc(raw_in[0], 16)
            ple_sync(sp)
            for tt in range(TT):
                sp.wait_ge(sem("ln_y"), 3 * TT + tt + 1)
                sp.dma_start(out[tt * P:tt * P + P, :], X[:, tt, :]).then_inc(sem("out"), 16)
            sp.wait_ge(sem("out"), 16 * TT)

        @blk.gpsimd
        def _(pool):
            start_pool(pool)
            ffn_pool_first(pool, B_FFN1)
            ffn_pool(pool, B_FFN1)
            ln_offset(pool, 0, 0)
            nat_pool_first(pool)
            ln_offset(pool, 0, 1)
            nat_pool(pool)
            for n in (B_IF, B_QA, B_QA + 1):
                lo_piece(pool, n, 0, *cseg[n % 2])
            chunk_pool(pool, B_QA + 2, NQA)
            ml_pool(pool)
            at_pool(pool)
            br_pool(pool)
            full_pool(pool, B_MIX, XH, XL)
            ln_offset(pool, 1, 0)
            ffn_pool_first(pool, B_FFN2)
            ln_offset(pool, 1, 1)
            ffn_pool(pool, B_FFN2)
            ln_offset(pool, 2, 0)
            for k in range(2):
                lo_piece(pool, B_PLE + k, 0, PWH[:, k, :], PWL[:, k, :])
            ln_offset(pool, 2, 1)
            for k in range(2, KC):
                lo_piece(pool, B_PLE + k, 0, PWH[:, k, :], PWL[:, k, :])
            ln_offset(pool, 3, 0)
            ln_offset(pool, 3, 1)

        @blk.tensor
        def _(pe):
            pe.wait_ge(sem("const"), 5)
            ffn_tensor(pe, 0, B_FFN1, [(w_split, B_FFN1)])
            transpose_half(pe, 0, 0, 0, [(sem("f_prod"), 4 * FI + 2)])
            nat_tensor(pe, lambda: transpose_half(pe, 0, 1, 4, [(sem("f_down_evac"), 16 * FI + 4)]))
            if_tensor(pe)
            ple0_tensor(pe)
            qa_tensor(pe)
            ml_tensor(pe)
            at_tensor(pe)
            br_tensor(pe)
            full_tensor(pe, "mx_", B_MIX, (MH, ML), (XH, XL), [(sem("br_mlo"), 2 * KC)], lambda: None)
            transpose_half(pe, 1, 0, 0, [(sem("mx_evac"), 12)])
            ffn_tensor(pe, 1, B_FFN2, [(sem("ln_tr_lo"), 16 + 8)], lambda: (
                transpose_half(pe, 1, 1, 4, [(sem("mx_evac"), 16)]), pe.wait_ge(sem("ln_tr_lo"), 2 * 16)))
            transpose_half(pe, 2, 0, 0, [(sem("f_prod"), 8 * FI + 2)])
            full_tensor(pe, "pg_", B_PLE, (XH, XL), (PWH, PWL),
                        [(sem("ln_tr_lo"), 32 + 8), (sem("f_down_evac"), 32 * FI + 4)],
                        lambda: (transpose_half(pe, 2, 1, 0, [(sem("pg_evac"), 4)]),
                                 pe.wait_ge(sem("ln_tr_lo"), 3 * 16)))

        @blk.scalar
        def _(act):
            start_scalar(act)
            ffn_scalar_first(act, B_FFN1, [])
            ln_loads(act, 0, [(sem("const"), 5)])
            act.wait_ge(sem("x_in"), 16)
            for tt in range(TT):
                scale_x(act, tt)
            ffn_scalar(act, 0, B_FFN1, lambda: ln_scale(act, 0, 0))
            nat_scalar_first(act, [(sem("f_unit_done"), 4 * FI + 4)])
            t_hi(act, 0, 0, 0)
            ln_scale(act, 0, 1)
            t_hi(act, 0, 1, 4)
            nat_scalar(act)
            for n in (B_IF, B_QA):
                hi_piece(act, n, 0, cseg[n % 2][0])
            if_scalar(act)
            hi_piece(act, B_QA + 1, 0, cseg[(B_QA + 1) % 2][0])
            ple0_scalar(act)
            gates_scalar(act)
            qa_scalar(act)
            nc.scalar.preload_act_table_set("natural_log_exp_and_others")
            ml_scalar(act)
            at_scalar(act)
            br_scalar(act)
            mix_scalar(act)
            ln_loads(act, 1, [])
            ln_scale(act, 1, 0)
            ffn_scalar_first(act, B_FFN2, [(sem("mx_done"), 16)])
            t_hi(act, 1, 0, 0)
            for tt in range(4):
                scale_x(act, tt)
            ln_scale(act, 1, 1)
            t_hi(act, 1, 1, 4)
            for tt in range(4, TT):
                scale_x(act, tt)
            ln_loads(act, 2, [(sem("ln_y"), 2 * TT), (sem("ln_ctr"), 2 * TT)])
            ffn_scalar(act, 1, B_FFN2, lambda: ln_scale(act, 2, 0))
            act.wait_ge(sem("f_down_done"), 32 * FI + 16)
            full_scalar(act, B_PLE, PWH, (0, 1))
            t_hi(act, 2, 0, 0)
            ln_scale(act, 2, 1)
            full_scalar(act, B_PLE, PWH, range(2, KC))
            for tt in range(4):
                scale_x(act, tt)
            act.wait_ge(sem("ln_y"), 3 * TT)
            act.wait_ge(sem("ln_ctr"), 3 * TT)
            act.dma_start(bple_t, b_ple.partition_broadcast(P)).then_inc(sem("bple_in"), 16)
            for o in range(8):
                ple_sigmoid(act, o)
            t_hi(act, 2, 1, 0)
            for tt in range(4, TT):
                scale_x(act, tt)
            for o in range(8, 16):
                ple_sigmoid(act, o)
            ln_loads(act, 3, [(sem("pg_evac"), 16)])
            ln_scale(act, 3, 0)
            ln_scale(act, 3, 1)

        @blk.vector
        def _(dve):
            dve.sem_inc(sem("n_evac"), 8)
            ffn_vector(dve, 0, [(sem("x_scaled"), TT)],
                       lambda tt, v: ln_stats(dve, 0, tt, sem("f_down_evac"), v),
                       lambda h: ln_centre(dve, 0, 0) if h == 0 else None)
            t_lo(dve, 0, 0, 0)
            ln_centre(dve, 0, 1)
            t_lo(dve, 0, 1, 4)
            nat_vector(dve)
            gates_vector(dve)
            qa_vector(dve)
            ml_vector(dve)
            at_vector(dve)
            br_vector(dve)
            mix_vector(dve)
            ffn_vector(dve, 1, [(sem("x_scaled"), 3 * TT)],
                       lambda tt, v: ln_stats(dve, 2, tt, sem("f_down_evac"), v),
                       lambda h: ln_centre(dve, 2, 0) if h == 0 else None)
            t_lo(dve, 2, 0, 0)
            ln_centre(dve, 2, 1)
            dve.wait_ge(sem("bple_in"), 16)
            ple_evac(dve, 0)
            ple_evac(dve, 1)
            for o in range(8):
                if o + 2 < 8:
                    ple_evac(dve, o + 2)
                ple_add(dve, o)
            t_lo(dve, 2, 1, 0)
            ple_evac(dve, 8)
            ple_evac(dve, 9)
            for o in range(8, 16):
                if o + 2 < 16:
                    ple_evac(dve, o + 2)
                ple_add(dve, o)
            ln_centre(dve, 3, 0)
            ln_centre(dve, 3, 1)


def lay_out(i):
    import numpy as np
    a = {k: np.asarray(v) for k, v in i.items()}

    def columns(w, step=P):
        n = w.shape[1] // step
        return w.reshape(KC, P, n, step).transpose(2, 1, 0, 3).reshape(n, P, KC * step)

    def ffn(l):
        g, u = columns(a["ffn_wg"][0, l]), columns(a["ffn_wu"][0, l])
        d = a["ffn_wd"][0, l].reshape(FC, P, D)
        return np.stack([g[0::2], u[0::2], g[1::2], u[1::2], d[0::2], d[1::2]], axis=1).reshape(6 * FI, P, PC)

    w = a["w_in"][0]
    b = a["b_in"][0]
    qa, va, oa = slice(0, 1024), slice(1024, 2048), slice(2048, 3072)
    ic, fc = slice(3072, 3076), slice(3076, 3080)
    qb, kb, vb = slice(3080, 4104), slice(4104, 5128), slice(5128, 6152)
    ga, gb = slice(6152, 7176), slice(7176, 8200)
    pair = np.arange(NQA).reshape(2, H_A).T.reshape(-1)
    wif, bif = np.zeros((D, P), w.dtype), np.zeros((P, 1), w.dtype)
    wif[:, 0:H_A], wif[:, 32:32 + H_A] = w[:, ic], w[:, fc]
    bif[0:H_A, 0], bif[32:32 + H_A, 0] = b[ic], b[fc]
    nat = np.concatenate([w[:, va], w[:, vb], w[:, oa]], axis=1)
    nat = nat.reshape(4, 2, P, NG, 512).transpose(3, 0, 2, 1, 4).reshape(4 * NG, P, PC)
    tch = np.concatenate([w[:, qb], w[:, kb], w[:, ga], w[:, gb]], axis=1)
    btc = np.concatenate([b[qb], b[kb], b[ga], b[gb]])
    branches = np.stack([columns(a["w_branch_a"][0]), columns(a["w_branch_b"][0])], axis=1).reshape(2 * KC, P, PC)
    w_all = np.concatenate([
        a["x"][0].T.reshape(KC, P, T), ffn(0), nat, a["p"][0, 0].T.reshape(2, P, T),
        a["w_ple"][0].reshape(2, P, D), columns(wif), columns(w[:, qa])[pair], columns(tch), branches, branches,
        a["w_mix_out"][0].reshape(KC, P, D), ffn(1), a["w_ple_gate"][0].reshape(KC, P, D)])
    return {
        "w_all": w_all,
        "x_nat": a["x"][0].reshape(TT, P, D).transpose(1, 0, 2),
        "b_t": btc.reshape(NTC, P).T, "b_if": bif, "b_qa": b[qa].reshape(NQA, P)[pair].T,
        "b_nat": np.concatenate([b[va], b[vb], b[oa]]),
        "b_forget": a["b_forget"][0].reshape(H_A, 1),
        "conv_w": a["conv_w"][0].reshape(CONV_W, NQA, P)[:, pair].transpose(2, 1, 0),
        "conv_b": a["conv_b"][0].reshape(NQA, P)[pair].T,
        "mh_g": a["mh_norm_g"][0].reshape(-1),
        "ln_g": a["ln_g"][0], "ln_b": a["ln_b"][0], "b_ple": a["b_ple_gate"][0],
    }


_SCRATCH = [("s_ple", (T, D)), ("s_x", (P, TT, D)), ("s_nat", (T, NAT)), ("s_qa", (NQA, P, T)),
            ("s_t", (NTC, P, T)), ("s_m", (H_A, T)), ("s_h", (T, D)), ("s_ya", (KC, P, T)), ("s_yb", (KC, P, T))]


def kernel(**inputs):
    import numpy as _np
    import concourse.bacc as _bacc
    from concourse.bass_utils import run_bass_kernel_spmd as _run

    nc = _bacc.Bacc("TRN2", target_bir_lowering=False, num_devices=1)
    arrays, args = {}, []
    for name, v in lay_out(inputs).items():
        v = _np.ascontiguousarray(v)
        arrays[f"in_{name}"] = v
        args.append(nc.dram_tensor(f"in_{name}", v.shape, F32, kind="ExternalInput").ap())
    args.append(nc.dram_tensor("out_0", (T, D), F32, kind="ExternalOutput").ap())
    for name, shape in _SCRATCH:
        args.append(nc.dram_tensor(name, shape, F32, kind="Internal").ap())
    build(nc, *args)
    r = _run(nc, [arrays], core_ids=[0])
    return r.results[0]["out_0"].reshape(1, T, D)
```

```python
import concourse.bass as bass
from concourse import mybir
from contextlib import ExitStack

F32 = mybir.dt.float32
F32R = mybir.dt.float32r
ACT = mybir.ActivationFunctionType
ALU = mybir.AluOpType

P = 128
D = 1024
T = 1024
KC = D // P
TT = T // P
PC = 1024
FFN_F = 2816
FC = FFN_F // P
FI = FC // 2
H_A, DK_A, DV_A, CONV_W = 4, 128, 256, 4
H_B, DH_B = 8, 128
NAT = 3072
NG = NAT // 512
NQA = 2 * H_A
NTC = 32
TC_Q, TC_K, TC_GA, TC_GB = 0, 8, 16, 24
NTA = 2 * H_B
V_A, V_B, O_A = 0, 1024, 2048
EPS = 1e-5
ALPHA = 2.0 ** 0.25

B_FFN1 = 0
B_NAT = B_FFN1 + 6 * FI
B_PLE0 = B_NAT + 4 * NG
B_IF = B_PLE0 + 4
B_QA = B_IF + 1
B_TA = B_QA + NQA
B_TB = B_TA + NTA
B_BR = B_TB + NTC - NTA
B_MIX = B_BR + 2 * 2 * KC
B_FFN2 = B_MIX + KC
B_PLE = B_FFN2 + 6 * FI
N_PIECES = B_PLE + KC


def triangle_units(descending):
    out = []
    for half in range(2):
        blocks = range(4 * half + 4)
        for sb in (reversed(blocks) if descending else blocks):
            t0 = max(sb * P, 512 * half)
            out.append((half, sb, t0, 512 * (half + 1) - t0, sb >= 4 * half))
    return out


MU = triangle_units(False)
NMU = len(MU)
AU = triangle_units(True)
NAU = len(AU)


def build(nc, w_all, x_t, x_nat, b_t, b_if, b_qa, b_nat, b_forget, conv_w, conv_b, mh_g, ln_g, ln_b, b_ple, out,
          s_ple, s_x, s_nat, s_qa, s_t, s_m, s_h, s_ya, s_yb):
    ctx = ExitStack()
    with ctx:
        FP = ctx.enter_context(nc.sbuf_tensor("fp", [P, 16064], F32))
        RP = ctx.enter_context(nc.sbuf_tensor("rp", [P, 37120], F32R))
        PS = [ctx.enter_context(nc.psum_tensor(f"bank{b}", [P, 512], F32)) for b in range(8)]
        made = {}

        def sem(name):
            if name not in made:
                made[name] = ctx.enter_context(nc.semaphore(name))
            return made[name]

        def fv(base, n):
            return FP[:, base:base + n]

        def rv(base, n):
            return RP[:, base:base + n]

        raw = [fv(0, PC), fv(PC, PC)]
        ident = fv(2048, P)
        stats = FP[:, 2176:2176 + 96].rearrange("p (t s) -> p t s", t=TT)
        mv = FP[:, 2272:2288].rearrange("p (t s) -> p t s", t=TT)
        rstd = fv(2288, TT)
        ve = fv(2296, TT)
        bt_col = fv(2304, NTC)
        bif_col = fv(2336, 1)
        bf_col = fv(2337, 1)
        bqa_col = fv(2338, NQA)
        cw_col = FP[:, 2346:2378].rearrange("p (c j) -> p c j", j=CONV_W)
        cb_col = fv(2378, NQA)
        a_col = FP[:, 2386:2418].rearrange("p (h t) -> p h t", h=H_A)
        e_col = FP[:, 2418:2450].rearrange("p (h t) -> p h t", h=H_A)
        a_head = fv(2450, TT)
        e_head = fv(2458, TT)
        small = fv(2466, 64)
        X0 = 2688
        X = FP[:, X0:X0 + 8192].rearrange("p (t n) -> p t n", t=TT)
        G0 = X0 + 8192
        lng_t, lnb_t = fv(G0, D), fv(G0 + D, D)
        T0 = G0 + 2048
        W0 = X0

        XH = RP[:, 0:8192].rearrange("p (k n) -> p k n", k=KC)
        XL = RP[:, 8192:16384].rearrange("p (k n) -> p k n", k=KC)
        R2 = 16384
        R3 = 32768
        TRI = rv(36864, P)
        TRIC = rv(36992, P)

        def seg(base):
            return rv(base, PC), rv(base + PC, PC)

        cseg = [seg(R3 + 2048 * s) for s in range(2)]
        fseg = cseg + [seg(R2 + 2048 * s) for s in range(4)]

        raw_in = [sem("raw_in0"), sem("raw_in1")]
        w_hi = sem("w_hi")
        w_split = sem("w_split")
        blk = ctx.enter_context(nc.Block())

        def apart(eng, name):
            eng.sem_inc(sem(name), 1)

        def load_pair(sp, j):
            for s in range(2):
                sp.wait_ge(w_split, 2 * j + s - 1)
                sp.dma_start(raw[s], w_all[2 * j + s]).then_inc(raw_in[s], 16)

        def hi_piece(act, n0, step, hi):
            act.wait_ge(raw_in[n0 % 2], 16 * (n0 // 2) + 8 * step + 16)
            nc.scalar.copy(hi, raw[n0 % 2]).then_inc(w_hi, 1)

        def lo_piece(pool, n0, step, hi, lo):
            pool.wait_ge(w_hi, n0 + step + 1)
            nc.gpsimd.tensor_tensor(lo, raw[n0 % 2], hi, ALU.subtract).then_inc(w_split, 1)

        def three(pe, ps, lh, ll, rh, rl, start, stop, skip=False):
            nc.tensor.matmul(ps, lh, rh, start=start, stop=False, skip_group_check=skip)
            nc.tensor.matmul(ps, lh, rl, start=False, stop=False, skip_group_check=skip)
            return nc.tensor.matmul(ps, ll, rh, start=False, stop=stop, skip_group_check=skip)

        def scale_x(act, tt):
            nc.scalar.mul(X[:, tt, :], X[:, tt, :], ALPHA).then_inc(sem("x_scaled"), 1)

        def start_pool(pool):
            nc.gpsimd.memset(ident, 0.0).then_inc(sem("const"), 1)
            nc.gpsimd.memset(fv(G0, P), 1.0).then_inc(sem("const"), 1)
            pool.wait_ge(sem("const"), 2)
            nc.gpsimd.affine_select(out=ident, in_=ident, compare_op=ALU.not_equal, fill=1.0, base=0,
                                    pattern=[[-1, P]], channel_multiplier=1).then_inc(sem("const"), 1)
            nc.gpsimd.affine_select(out=TRI, in_=fv(G0, P), compare_op=ALU.is_ge, fill=0.0, base=0,
                                    pattern=[[-1, P]], channel_multiplier=1).then_inc(sem("const"), 1)
            nc.gpsimd.affine_select(out=TRIC, in_=fv(G0, P), compare_op=ALU.is_gt, fill=0.0, base=0,
                                    pattern=[[1, P]], channel_multiplier=-1).then_inc(sem("const"), 1)

        XT_PARTS = [(slice(k, k + 2), slice(512 * h, 512 * h + 512)) for h in range(2) for k in range(0, KC, 2)]

        def start_sync(sp):
            for s in range(2):
                sp.dma_start(raw[s], w_all[s]).then_inc(raw_in[s], 16)
            for n, (ks, t) in enumerate(XT_PARTS[::2]):
                if n == 2:
                    load_pair(sp, 1)
                ks = slice(ks.start, ks.start + 4)
                sp.dma_start(X[:, ks, t], x_t[ks, :, t].rearrange("k p n -> p k n")).then_inc(sem(f"xt_in{n}"), 16)

        def start_scalar(act):
            for n in range(2):
                hi_piece(act, B_FFN1 + n, 0, fseg[n][0])
            for n, (ks, t) in enumerate(XT_PARTS):
                act.wait_ge(sem(f"xt_in{n // 2}"), 16)
                nc.scalar.copy(XH[:, ks, t], X[:, ks, t]).then_inc(sem("xt_hi"), 1)
                if n in (1, 3):
                    m = (n + 3) // 2
                    hi_piece(act, B_FFN1 + m, 0, fseg[m][0])
            for dst, src in ((bt_col, b_t), (bif_col, b_if), (bqa_col, b_qa), (cw_col, conv_w), (cb_col, conv_b),
                             (bf_col[0:H_A, :], b_forget)):
                act.dma_start(dst, src).then_inc(sem("small_in"), 16)
            act.wait_ge(sem("xt_lo"), len(XT_PARTS))
            act.dma_start(X, x_nat).then_inc(sem("x_in"), 16)

        def start_vector(dve):
            for n, (ks, t) in enumerate(XT_PARTS):
                dve.wait_ge(sem("xt_hi"), n + 1)
                nc.vector.tensor_tensor(XL[:, ks, t], X[:, ks, t], XH[:, ks, t], ALU.subtract)\
                    .then_inc(sem("xt_lo"), 1)

        HH = RP[:, R2 + 8192:R2 + 10240].rearrange("p (f h n) -> p f h n", f=2, h=2)
        HL = RP[:, R2 + 10240:R2 + 12288].rearrange("p (f h n) -> p f h n", f=2, h=2)
        silu_t = [fv(T0 + 512 * i, 512) for i in range(2)]
        prod_t = [fv(T0 + 1024 + 512 * i, 512) for i in range(2)]
        UNITS = [(0, 0), (1, 0), (0, 1), (1, 1)]
        U4 = [0, 4 * FI]
        U16 = [0, 16 * FI]

        def ffn_pool_first(pool, base, ns):
            for n in ns:
                lo_piece(pool, base + n, 0, *fseg[n])

        def ffn_pool(pool, base):
            with pool.Fori(0, FI - 1) as i:
                for n in range(4, 10):
                    lo_piece(pool, base + n, 6 * i, *fseg[n % 6])
            for n in range(4, 6):
                lo_piece(pool, base + n, 6 * (FI - 1), *fseg[n])

        def ffn_scalar(act, r, base, between, beside_first=None):
            def gate(i, u):
                f, h = UNITS[u]
                act.wait_ge(sem("f_unit_done"), U4[r] + 4 * i + u + 5)
                act.wait_ge(sem("f_prod"), U4[r] + 4 * i + u + 1)
                nc.scalar.activation(silu_t[u % 2], PS[2 * (u % 2)][:, :], ACT.Silu)\
                    .then_inc(sem("f_silu"), 1)
                act.wait_ge(sem("f_prod"), U4[r] + 4 * i + u + 3)
                act.wait_ge(sem("f_down_done"), U16[r] + 16 * i + 8 + 8 * h)
                nc.scalar.copy(HH[:, f, h, :], prod_t[u % 2]).then_inc(sem("f_h_hi"), 1)

            def down_weights(i):
                act.wait_ge(sem("f_down_done"), U16[r] + 16 * i + 16)
                for n in (4, 5):
                    hi_piece(act, base + n, 6 * i, fseg[n][0])

            def round_(i, beside):
                gate(i, 0)
                gate(i, 1)
                down_weights(i)
                gate(i, 2)
                gate(i, 3)
                for n in range(6, 10):
                    beside(n - 6)
                    act.wait_ge(sem("f_unit_done"), U4[r] + 4 * i + 7 + (n - 6) // 2)
                    hi_piece(act, base + n, 6 * i, fseg[n - 6][0])

            if beside_first:
                round_(0, beside_first)
            with act.Fori(1 if beside_first else 0, FI - 1) as i:
                round_(i, lambda n: None)
            gate(FI - 1, 0)
            gate(FI - 1, 1)
            down_weights(FI - 1)
            gate(FI - 1, 2)
            between()
            gate(FI - 1, 3)

        def ffn_tensor(pe, r, base, ready, between_first=None):
            def unit(i, u, arriving=False):
                f, h = UNITS[u]
                if h == 0:
                    pe.wait_ge(w_split, base + 6 * i + 2 * f + 2)
                pe.wait_ge(sem("f_prod"), U4[r] + 4 * i + u + 1)
                for g in range(2):
                    wh, wl = fseg[2 * f + g]
                    for k in range(KC):
                        if arriving and k % 2 == 0:
                            pe.wait_ge(sem("xt_lo"), 4 * h + k // 2 + 1)
                        c = slice(k * P, k * P + P)
                        t = slice(h * 512, h * 512 + 512)
                        last = three(pe, PS[2 * (u % 2) + g][:, :], wh[:, c], wl[:, c],
                                     XH[:, k, t], XL[:, k, t], k == 0, k == KC - 1)
                last.then_inc(sem("f_unit_done"), 1)

            def down(i, h):
                pe.wait_ge(w_split, base + 6 * i + 6)
                pe.wait_ge(sem("f_h_lo"), U4[r] + 4 * i + 2 + 2 * h)
                for o in range(8 * h, 8 * h + 8):
                    tl, dh = o // 2 % 4, o % 2
                    pe.wait_ge(sem("f_down_evac"), U16[r] + 16 * i + o + 1)
                    for f in range(2):
                        t = slice(tl * P, tl * P + P)
                        c = slice(dh * 512, dh * 512 + 512)
                        wh, wl = fseg[4 + f]
                        last = three(pe, PS[4 + o % 4][:, :], HH[:, f, h, t], HL[:, f, h, t],
                                     wh[:, c], wl[:, c], f == 0, f == 1)
                    last.then_inc(sem("f_down_done"), 1)

            for s, v in ready:
                pe.wait_ge(s, v)
            if r == 0:
                pe.sem_inc(sem("f_unit_done"), 4)
                pe.sem_inc(sem("f_down_done"), 16)
            if r == 0:
                unit(0, 0, True)
                unit(0, 1)
            else:
                unit(0, 0)
                between_first(0)
                unit(0, 1)
                between_first(1)
            unit(0, 2, r == 0)
            unit(0, 3)
            down(0, 0)
            down(0, 1)
            with pe.Fori(1, FI - 1) as i:
                for u in range(4):
                    unit(i, u)
                down(i, 0)
                down(i, 1)
            unit(FI - 1, 0)
            unit(FI - 1, 1)
            unit(FI - 1, 2)
            down(FI - 1, 0)
            unit(FI - 1, 3)
            down(FI - 1, 1)

        def ffn_vector(dve, r, evac_hook, half_hook):
            def gate(i, u):
                f, h = UNITS[u]
                dve.wait_ge(sem("f_silu"), U4[r] + 4 * i + u + 1)
                nc.vector.tensor_tensor(prod_t[u % 2], silu_t[u % 2], PS[2 * (u % 2) + 1][:, :], ALU.mult)\
                    .then_inc(sem("f_prod"), 1)
                dve.wait_ge(sem("f_h_hi"), U4[r] + 4 * i + u + 1)
                nc.vector.tensor_tensor(HL[:, f, h, :], prod_t[u % 2], HH[:, f, h, :], ALU.subtract)\
                    .then_inc(sem("f_h_lo"), 1)

            def evac(i, o):
                h, tl, dh = o // 8, o // 2 % 4, o % 2
                xs = X[:, 4 * h + tl, dh * 512:dh * 512 + 512]
                dve.wait_ge(sem("f_down_done"), U16[r] + 16 * i + o + 17)
                nc.vector.scalar_tensor_tensor(out=xs, in0=PS[4 + o % 4][:, :], scalar=0.5, in1=xs,
                                               op0=ALU.mult, op1=ALU.add).then_inc(sem("f_down_evac"), 1)

            if r == 0:
                dve.sem_inc(sem("f_prod"), 2)
                dve.sem_inc(sem("f_down_evac"), 4)
            for u in range(4):
                gate(0, u)
            for o in range(16):
                if o % 2 == 0:
                    dve.wait_ge(sem("x_scaled"), 2 * TT * r + o // 2 + 1)
                evac(0, o)
            with dve.Fori(1, FI - 1) as i:
                for u in range(4):
                    gate(i, u)
                for o in range(16):
                    evac(i, o)
            for u in range(3):
                gate(FI - 1, u)
            for h in range(2):
                for tl in range(4):
                    evac(FI - 1, 8 * h + 2 * tl)
                    evac(FI - 1, 8 * h + 2 * tl + 1)
                    if tl:
                        evac_hook(4 * h + tl - 1, U16[r] + 16 * (FI - 1) + 8 * h + 2 * tl + 4)
                evac_hook(4 * h + 3, U16[r] + 16 * (FI - 1) + 8 * h + 12)
                half_hook(h)
                if h == 0:
                    gate(FI - 1, 3)

        def ln_loads(act, r, free):
            for s, v in free:
                act.wait_ge(s, v)
            act.dma_start(lng_t, ln_g[r].partition_broadcast(P)).then_inc(sem("ln_gb_in"), 16)
            act.dma_start(lnb_t, ln_b[r].partition_broadcast(P)).then_inc(sem("ln_gb_in"), 16)

        def ln_stats(dve, r, tt, evac, count):
            dve.wait_ge(evac, count)
            for h in range(2):
                nc.vector.bn_stats(stats[:, tt, 6 * h:6 * h + 6], X[:, tt, 512 * h:512 * h + 512])\
                    .then_inc(sem("ln_st"), 1)
            dve.wait_ge(sem("ln_st"), 16 * r + 2 * tt + 2)
            nc.vector.bn_aggr(mv[:, tt, :], stats[:, tt, :]).then_inc(sem("ln_mv"), 1)

        def ln_half(r, h):
            return r, range(4 * h, 4 * h + 4), 2 * r + h

        LAST = [(3, range(4, 6), 7), (3, range(6, 8), 8)]

        def ln_centre(dve, part):
            r, tiles, n = part
            t4 = slice(tiles[0], tiles[-1] + 1)
            dve.wait_ge(sem("ln_mv"), 8 * r + tiles[-1] + 1)
            nc.vector.tensor_scalar(ve[:, t4], mv[:, t4, 1], EPS, None, ALU.add).then_inc(sem("ln_ve"), 1)
            dve.wait_ge(sem("ln_gb_in"), 32 * r + 32)
            for tt in tiles:
                nc.vector.scalar_tensor_tensor(out=X[:, tt, :], in0=X[:, tt, :], scalar=mv[:, tt, 0:1], in1=lng_t,
                                               op0=ALU.subtract, op1=ALU.mult).then_inc(sem("ln_ctr"), 1)
                if tt == tiles[0]:
                    dve.wait_ge(sem("ln_sd"), n + 1)
                    nc.vector.reciprocal(rstd[:, t4], ve[:, t4]).then_inc(sem("ln_rstd"), 1)

        def ln_scale(act, part):
            r, tiles, n = part
            t4 = slice(tiles[0], tiles[-1] + 1)
            act.wait_ge(sem("ln_ve"), n + 1)
            nc.scalar.sqrt(ve[:, t4], ve[:, t4]).then_inc(sem("ln_sd"), 1)
            act.wait_ge(sem("ln_rstd"), n + 1)
            for tt in tiles:
                act.wait_ge(sem("ln_ctr"), 8 * r + tt + 1)
                nc.scalar.mul(X[:, tt, :], X[:, tt, :], rstd[:, tt:tt + 1]).then_inc(sem("ln_n"), 1)

        def ln_offset(pool, r, tiles):
            for tt in tiles:
                pool.wait_ge(sem("ln_n"), 8 * r + tt + 1)
                nc.gpsimd.tensor_tensor(X[:, tt, :], X[:, tt, :], lnb_t, ALU.add).then_inc(sem("ln_y"), 1)

        def transpose_half(pe, r, h, bank, free):
            for s, v in free:
                pe.wait_ge(s, v)
            transpose(pe, r, range(8 * h, 8 * h + 8), bank)

        def transpose(pe, r, groups, bank):
            for g in groups:
                tt, j = g // 2, g % 2
                pe.wait_ge(sem("ln_y"), 8 * r + tt + 1)
                if g % 8 >= 4:
                    pe.wait_ge(sem("ln_tr_lo"), 16 * r + g - 3)
                for k in range(4):
                    last = nc.tensor.transpose(PS[bank + g % 4][:, k * P:k * P + P],
                                               X[:, tt, (4 * j + k) * P:(4 * j + k) * P + P], ident)
                last.then_inc(sem("ln_tr"), 1)

        def t_hi(act, r, h, bank):
            for g in range(8 * h, 8 * h + 8):
                tt, j = g // 2, g % 2
                act.wait_ge(sem("ln_tr"), 16 * r + g + 1)
                nc.scalar.copy(XH[:, 4 * j:4 * j + 4, tt * P:tt * P + P],
                               PS[bank + g % 4][:, :].rearrange("p (k n) -> p k n", k=4)).then_inc(sem("ln_tr_hi"), 1)

        def t_lo(dve, r, h, bank):
            for g in range(8 * h, 8 * h + 8):
                tt, j = g // 2, g % 2
                k = slice(4 * j, 4 * j + 4)
                dve.wait_ge(sem("ln_tr_hi"), 16 * r + g + 1)
                nc.vector.tensor_tensor(XL[:, k, tt * P:tt * P + P],
                                        PS[bank + g % 4][:, :].rearrange("p (k n) -> p k n", k=4),
                                        XH[:, k, tt * P:tt * P + P], ALU.subtract).then_inc(sem("ln_tr_lo"), 1)

        def nseg(kh):
            b = (R3, R2)[kh]
            return (RP[:, b:b + 2048].rearrange("p (k n) -> p k n", k=4),
                    RP[:, b + 2048:b + 4096].rearrange("p (k n) -> p k n", k=4))

        def npiece(s, part):
            return nseg(s // 2)[part][:, 2 * (s % 2):2 * (s % 2) + 2, :].rearrange("p k n -> p (k n)")
        p_seg, wp_seg = ([rv(R2 + 8192 + 4096 * a + 2048 * b, 2048) for b in range(2)] for a in range(2))
        bias_nat = fv(G0, NAT)
        stage4 = [fv(14016 + 512 * i, 512) for i in range(4)]

        def ple_piece(n):
            return [v[:, PC * (n % 2):PC * (n % 2) + PC] for v in (p_seg, wp_seg)[n // 2]]

        def nat_pool_first(pool):
            for s in range(4):
                lo_piece(pool, B_NAT + s, 0, npiece(s, 0), npiece(s, 1))

        def nat_pool(pool):
            with pool.Fori(0, NG - 1) as i:
                for s in range(4):
                    lo_piece(pool, B_NAT + 4 + s, 4 * i, npiece(s, 0), npiece(s, 1))
            for n in range(4):
                lo_piece(pool, B_PLE0 + n, 0, *ple_piece(n))

        def nat_scalar_first(act, free):
            for s, v in free:
                act.wait_ge(s, v)
            for s in range(4):
                hi_piece(act, B_NAT + s, 0, npiece(s, 0))

        def nat_tensor(pe, between):
            def group(i, kh, tts):
                wh, wl = nseg(kh)
                for tt in tts:
                    if kh == 0:
                        pe.wait_ge(sem("n_evac"), 8 * i + tt + 1)
                    for k in range(4):
                        t = slice(tt * P, tt * P + P)
                        last = three(pe, PS[tt][:, :], XH[:, 4 * kh + k, t], XL[:, 4 * kh + k, t],
                                     wh[:, k, :], wl[:, k, :], kh == 0 and k == 0, kh == 1 and k == 3)
                    if kh == 1:
                        last.then_inc(sem("n_done"), 1)
                if kh == 0 and tts[-1] == TT - 1:
                    last.then_inc(sem("n_half"), 1)
            pe.wait_ge(w_split, B_NAT + 2)
            pe.wait_ge(sem("ln_tr_lo"), 8)
            group(0, 0, range(0, 4))
            between()
            pe.wait_ge(sem("ln_tr_lo"), 16)
            group(0, 0, range(4, TT))
            pe.wait_ge(w_split, B_NAT + 4)
            group(0, 1, range(TT))
            with pe.Fori(1, NG) as i:
                for kh in range(2):
                    pe.wait_ge(w_split, B_NAT + 4 * i + 2 + 2 * kh)
                    group(i, kh, range(TT))

        def nat_vector(dve):
            dve.wait_ge(sem("f_h_hi"), 4 * FI)
            dve.wait_ge(sem("f_h_lo"), 4 * FI)
            dve.wait_ge(sem("bnat_in"), 16)
            with dve.Fori(0, NG) as i:
                for tt in range(TT):
                    dve.wait_ge(sem("n_done"), 8 * i + tt + 1)
                    dve.wait_ge(sem(f"n_out{tt % 4}"), 32 * i + 16 * (tt // 4) + 16)
                    nc.vector.tensor_tensor(stage4[tt % 4], PS[tt][:, :], bias_nat[:, bass.ts(i, 512)], ALU.add)\
                        .then_inc(sem("n_evac"), 1)

        def nat_scalar(act):
            act.wait_ge(sem("ln_y"), TT)
            act.wait_ge(sem("ln_ctr"), TT)
            act.wait_ge(sem("f_h_lo"), 4 * FI)
            for n in range(4):
                act.sem_inc(sem(f"n_out{n}"), 16)
            act.dma_start(bias_nat, b_nat.partition_broadcast(P)).then_inc(sem("bnat_in"), 16)
            act.dma_start(s_x, X).then_inc(sem("x_out"), 16)

            def store(i, tt, gated):
                act.wait_ge(sem("n_evac"), 8 * i + tt + 9)
                if gated:
                    nc.scalar.activation(stage4[tt % 4], stage4[tt % 4], ACT.Sigmoid).then_inc(sem("n_sig"), 1)
                    act.wait_ge(sem("n_sig"), 8 * i + tt + 1 - 8 * (O_A // 512))
                act.dma_start(s_nat[tt * P:tt * P + P, bass.ts(i, 512)], stage4[tt % 4])\
                    .then_inc(sem(f"n_out{tt % 4}"), 16)

            def round_(i, gated):
                for s in (0, 1):
                    act.wait_ge(sem("n_half"), i + 1)
                    hi_piece(act, B_NAT + 4 + s, 4 * i, npiece(s, 0))
                for tt in range(TT):
                    store(i, tt, gated)
                for s in (2, 3):
                    act.wait_ge(sem("n_done"), 8 * i + 8)
                    hi_piece(act, B_NAT + 4 + s, 4 * i, npiece(s, 0))
            with act.Fori(0, O_A // 512) as i:
                round_(i, False)
            with act.Fori(O_A // 512, NG - 1) as i:
                round_(i, True)
            for n in range(4):
                hi_piece(act, B_PLE0 + n, 0, ple_piece(n)[0])
            act.wait_ge(sem("n_half"), NG)
            for n in (B_IF, B_QA):
                hi_piece(act, n, 0, cseg[n % 2][0])
            for tt in range(TT):
                store(NG - 1, tt, True)

        GR = W0
        g_i, g_f, g_t, g_u, g_F = (FP[0:H_A, GR + 1024 * n:GR + 1024 * n + 1024] for n in range(5))
        f_raw = FP[32:32 + H_A, GR + 2048:GR + 3072]

        def if_tensor(pe):
            pe.wait_ge(sem("n_evac"), 8 * NG + 8)
            pe.wait_ge(w_split, B_IF + 1)
            wh, wl = cseg[B_IF % 2]
            for h in range(2):
                for k in range(KC):
                    c, t = slice(k * P, k * P + P), slice(h * 512, h * 512 + 512)
                    last = three(pe, PS[4 + h][:, :], wh[:, c], wl[:, c], XH[:, k, t], XL[:, k, t],
                                 k == 0, k == KC - 1)
            last.then_inc(sem("if_done"), 1)

        def if_scalar(act):
            act.wait_ge(sem("if_done"), 1)
            act.wait_ge(sem("x_out"), 16)
            act.wait_ge(sem("ln_tr"), 2 * TT)
            act.wait_ge(sem("small_in"), 96)
            for h in range(2):
                c = slice(512 * h, 512 * h + 512)
                nc.scalar.activation(g_i[:, c], PS[4 + h][0:H_A, :], ACT.Identity, bias=bif_col[0:H_A, :])\
                    .then_inc(sem("if_evac"), 1)
                nc.scalar.activation(f_raw[:, c], PS[4 + h][32:32 + H_A, :], ACT.Identity,
                                     bias=bif_col[32:32 + H_A, :]).then_inc(sem("if_evac"), 1)
            act.wait_ge(sem("if_evac"), 4)
            act.dma_start(g_f, f_raw).then_inc(sem("g_in"), 16)

        def ple0_tensor(pe):
            ph, pl, wh, wl = (v.rearrange("p (k n) -> p k n", k=2) for v in (*p_seg, *wp_seg))
            for o in range(16):
                tt, dh = o // 2, o % 2
                if o >= 4:
                    pe.wait_ge(sem("st_evac"), o - 3)
                for k in range(2):
                    l, c = slice(tt * P, tt * P + P), slice(dh * 512, dh * 512 + 512)
                    last = three(pe, PS[o % 4][:, :], ph[:, k, l], pl[:, k, l], wh[:, k, c], wl[:, k, c],
                                 k == 0, k == 1)
                last.then_inc(sem("st_done"), 1)

        def ple0_scalar(act):
            for o in range(16):
                act.wait_ge(sem("st_done"), o + 1)
                act.wait_ge(sem(f"n_out{o % 4}"), 16 * (2 * NG + 1 + o // 4))
                nc.scalar.copy(stage4[o % 4], PS[o % 4][:, :]).then_inc(sem("st_evac"), 1)
                act.wait_ge(sem("st_evac"), o + 1)
                act.dma_start(s_ple[o // 2 * P:o // 2 * P + P, o % 2 * 512:o % 2 * 512 + 512],
                              stage4[o % 4]).then_inc(sem(f"n_out{o % 4}"), 16)
        N_OUT = 16 * (2 * NG + 1 + 4)

        def gates_vector(dve):
            n = [0]

            def link(ins):
                n[0] += 1
                ins.then_inc(sem("g_v"), 1)
                dve.wait_ge(sem("g_v"), n[0])
            dve.wait_ge(sem("g_in"), 16)
            dve.wait_ge(sem("if_evac"), 4)
            dve.wait_ge(sem("small_in"), 96)
            link(nc.vector.tensor_scalar(g_f, g_f, bf_col[0:H_A, :], None, ALU.add))
            dve.wait_ge(sem("g_act"), 3)
            link(nc.vector.scalar_tensor_tensor(out=g_u, in0=g_f, scalar=0.0, in1=g_t, op0=ALU.min,
                                                op1=ALU.subtract))
            link(nc.vector.memset(g_t, 0.0))
            link(nc.vector.tensor_tensor_scan(out=g_F, data0=g_u, data1=g_t, initial=0.0, op0=ALU.add, op1=ALU.add))
            link(nc.vector.tensor_tensor(g_i, g_i, g_F, ALU.subtract))
            link(nc.vector.tensor_tensor_scan(out=g_t, data0=g_i, data1=g_i, initial=0.0, op0=ALU.max, op1=ALU.max))
            link(nc.vector.tensor_tensor(g_u, g_F, g_t, ALU.add))

        def gates_columns(dve):
            dve.wait_ge(sem("g_tr"), 1)
            nc.vector.tensor_copy(a_col.rearrange("p h t -> p t h"),
                                  PS[4][:, 0:32].rearrange("p (t h) -> p t h", h=H_A)).then_inc(sem("g_col"), 1)
            nc.vector.tensor_copy(e_col.rearrange("p h t -> p t h"),
                                  PS[4][:, 32:64].rearrange("p (t h) -> p t h", h=H_A)).then_inc(sem("g_col"), 1)

        def gates_scalar(act):
            act.wait_ge(sem("g_v"), 1)
            nc.scalar.activation(g_t, g_f, ACT.Abs).then_inc(sem("g_act"), 1)
            act.wait_ge(sem("g_act"), 1)
            nc.scalar.activation(g_u, g_t, ACT.Exp, scale=-1.0).then_inc(sem("g_act"), 1)
            act.wait_ge(sem("g_act"), 2)
            nc.scalar.activation(g_t, g_u, ACT.Ln, bias=1.0).then_inc(sem("g_act"), 1)
            act.wait_ge(sem("g_v"), 7)
            nc.scalar.activation(g_f, g_u, ACT.Exp, scale=-1.0).then_inc(sem("g_act"), 1)
            act.dma_start(s_m, g_t).then_inc(sem("m_out"), 16)

        def gates_tensor(pe):
            pe.wait_ge(sem("g_act"), 4)
            for n, src in enumerate((g_i, g_f)):
                for tt in range(TT):
                    last = nc.tensor.transpose(PS[4][:, 32 * n + 4 * tt:32 * n + 4 * tt + 4],
                                               src[:, tt * P:tt * P + P], ident[0:H_A, 0:H_A])
            last.then_inc(sem("g_tr"), 1)

        UP = W0 + 5120
        u_pad = [fv(UP + 1028 * j, 1027) for j in range(2)]
        conv_t = [fv(UP + 2056 + 1024 * j, 1024) for j in range(2)]
        conv_o = [fv(UP + 4104 + 1024 * j, 1024) for j in range(2)]

        def half_chunk(pe, wseg, h, bank):
            wh, wl = wseg
            for k in range(KC):
                c, t = slice(k * P, k * P + P), slice(h * 512, h * 512 + 512)
                last = three(pe, PS[bank][:, :], wh[:, c], wl[:, c], XH[:, k, t], XL[:, k, t], k == 0, k == KC - 1)
            return last

        def qa_tensor(pe):
            pe.sem_inc(sem("qa_done"), 4)

            def pair(i):
                for j in range(2):
                    pe.wait_ge(w_split, B_QA + 2 * i + j + 1)
                    for h in range(2):
                        pe.wait_ge(sem(f"qa_evac{h}"), 2 * i + j + 1)
                        half_chunk(pe, cseg[(B_QA + j) % 2], h, 2 * j + h).then_inc(sem("qa_done"), 1)
            pe.wait_ge(sem("st_evac"), 16)
            with pe.Fori(0, NQA // 2 - 1) as i:
                pair(i)
            gates_tensor(pe)
            pair(NQA // 2 - 1)

        def qa_vector(dve):
            dve.wait_ge(sem("n_out3"), N_OUT)
            dve.wait_ge(sem("n_out2"), N_OUT)
            dve.wait_ge(sem("n_out1"), N_OUT)
            dve.wait_ge(sem("n_out0"), N_OUT)
            for j in range(2):
                nc.vector.memset(u_pad[j][:, 0:3], 0.0).then_inc(sem("qa_zero"), 1)
            dve.wait_ge(sem("qa_zero"), 2)
            dve.sem_inc(sem("qa_conv"), 8)

            def pair(i):
                for j in range(2):
                    dve.wait_ge(sem("qa_evac0"), 2 * i + j + 3)
                    dve.wait_ge(sem("qa_evac1"), 2 * i + j + 3)
                    dve.wait_ge(sem("qa_silu"), 2 * i + j + 1)
                    nc.vector.tensor_scalar(conv_t[j], u_pad[j][:, 0:T], cw_col[:, 2 * i + j, 0:1],
                                            cb_col[:, bass.ds(2 * i + j, 1)], ALU.mult, ALU.add)\
                        .then_inc(sem("qa_conv"), 1)
                    for w in range(1, CONV_W):
                        dve.wait_ge(sem("qa_conv"), 8 * i + 4 * j + w + 8)
                        nc.vector.scalar_tensor_tensor(out=conv_t[j], in0=u_pad[j][:, w:w + T],
                                                       scalar=cw_col[:, 2 * i + j, w:w + 1], in1=conv_t[j],
                                                       op0=ALU.mult, op1=ALU.add).then_inc(sem("qa_conv"), 1)
            with dve.Fori(0, NQA // 2 - 1) as i:
                pair(i)
            gates_columns(dve)
            pair(NQA // 2 - 1)

        def qa_scalar(act):
            act.sem_inc(sem("qa_silu"), 2)
            act.sem_inc(sem("qa_out0"), 16)
            act.sem_inc(sem("qa_out1"), 16)
            with act.Fori(0, NQA // 2) as i:
                for j in range(2):
                    for h in range(2):
                        act.wait_ge(sem("qa_done"), 4 * i + 2 * j + h + 5)
                        if h == 0:
                            act.wait_ge(sem("qa_conv"), 8 * i + 4 * j + 4)
                        apart(act, "passed_act")
                        nc.scalar.activation(u_pad[j][:, 3 + 512 * h:515 + 512 * h], PS[2 * j + h][:, :],
                                             ACT.Identity, bias=bqa_col[:, bass.ds(2 * i + j, 1)])\
                            .then_inc(sem(f"qa_evac{h}"), 1)
                    hi_piece(act, B_QA + 2 + j, 2 * i, cseg[(B_QA + j) % 2][0])
                for j in range(2):
                    act.wait_ge(sem("qa_conv"), 8 * i + 4 * j + 12)
                    act.wait_ge(sem(f"qa_out{j}"), 16 * i + 16)
                    nc.scalar.activation(conv_o[j], conv_t[j], ACT.Silu).then_inc(sem("qa_silu"), 1)
                    act.wait_ge(sem("qa_silu"), 2 * i + j + 3)
                    act.dma_start(s_qa[2 * i + j], conv_o[j]).then_inc(sem(f"qa_out{j}"), 16)

        def chunk_pool(pool, n0, count):
            with pool.Fori(0, count // 2) as i:
                for j in range(2):
                    lo_piece(pool, n0 + j, 2 * i, *cseg[(n0 + j) % 2])

        m_q, m_k = fv(W0, 1024), fv(W0 + 1024, 1024)
        m_v = FP[:, W0 + 2048:W0 + 4096].rearrange("p (s n) -> p s n", s=TT)
        m_M = fv(W0 + 4096, 1024)
        m_D = [fv(W0 + 5120 + 512 * j, 512) for j in range(2)]
        m_P = [fv(W0 + 6144 + 512 * j, 512) for j in range(2)]
        m_H = [fv(W0 + 8192 + 256 * j, 256) for j in range(4)]
        ta_stage = [fv(W0 + 9216 + 1024 * j, 1024) for j in range(2)]
        QH, QL, KH, KL = (rv(R2 + 1024 * n, 1024) for n in range(4))
        VW = DV_A + 2
        VH = RP[:, R2 + 4096:R2 + 4096 + TT * VW].rearrange("p (s n) -> p s n", s=TT)
        VL = RP[:, R2 + 4096 + TT * VW:R2 + 4096 + 2 * TT * VW].rearrange("p (s n) -> p s n", s=TT)
        PB = R2 + 4096 + 2 * TT * VW
        PHt = [rv(PB + 512 * j, 512) for j in range(2)]
        PLt = [rv(PB + 1024 + 512 * j, 512) for j in range(2)]
        NCA = NTA // H_A

        def ml_sync(sp):
            sp.wait_ge(sem("g_tr"), 1)
            sp.wait_ge(sem("m_out"), 16)
            with sp.Fori(0, H_A) as i:
                sp.wait_ge(sem("ml_split_v"), i + 1)
                sp.wait_ge(sem("ml_split"), 2 * i + 2)
                for j in range(2):
                    sp.wait_ge(sem(f"qa_out{j}"), 16 * i + 32)
                sp.dma_start(m_q, s_qa[2 * i]).then_inc(sem("ml_in"), 16)
                sp.dma_start(m_k, s_qa[2 * i + 1]).then_inc(sem("ml_in"), 16)
                sp.dma_start(m_v, s_nat[:, bass.ts(i, DV_A)].rearrange("(s p) n -> p s n", p=P))\
                    .then_inc(sem("ml_in"), 16)
                sp.wait_ge(sem("ml_d"), NMU * i + NMU)
                sp.dma_start(m_M, s_m[i].partition_broadcast(P)).then_inc(sem("ml_M_in"), 16)
                load_at(sp, B_TA, 4 * i, 0, 4)

        AHEAD = 2

        def load_at(sp, base, step, a, b):
            for n in range(a, b):
                s = (base + AHEAD + n) % 2
                sp.wait_ge(w_split, base + AHEAD + step + n - 1)
                sp.dma_start(raw[s], w_all[base + AHEAD + step + n]).then_inc(raw_in[s], 16)

        def ml_ones(pool):
            pool.wait_ge(sem("st_done"), 16)
            nc.gpsimd.memset(VL[:, :, DV_A:VW].bitcast(F32), 0.0).then_inc(sem("ml_one"), 1)
            nc.gpsimd.memset(VH[:, :, DV_A + 1:VW].bitcast(F32), 0.0).then_inc(sem("ml_one"), 1)
            nc.gpsimd.memset(VH[:, :, DV_A:DV_A + 1].bitcast(F32), 1.0).then_inc(sem("ml_one"), 1)

        def ml_pool(pool):
            with pool.Fori(0, H_A) as i:
                for n, (src, hi, lo) in enumerate([(m_q, QH, QL), (m_k, KH, KL)]):
                    pool.wait_ge(sem("ml_hi"), 3 * i + n + 1)
                    nc.gpsimd.tensor_tensor(lo, src, hi, ALU.subtract).then_inc(sem("ml_split"), 1)
                for u, (h, sb, t0, n, diag) in enumerate(MU):
                    if diag:
                        pool.wait_ge(sem("ml_d"), NMU * i + u + 1 + NMU)
                        apart(pool, "passed_pool")
                        nc.gpsimd.affine_select(out=m_D[u % 2][:, 0:P], in_=m_D[u % 2][:, 0:P],
                                                compare_op=ALU.is_ge, fill=0.0, base=0, pattern=[[1, P]],
                                                channel_multiplier=-1).then_inc(sem("ml_mask"), 1)
                    if u in (2, 4, 6, 8):
                        lo_piece(pool, B_TA + 1 + u // 2, 4 * i, *cseg[(B_TA + 1 + u // 2) % 2])

        def ml_tensor(pe):
            pe.sem_inc(sem("ml_pv"), 2)
            pe.sem_inc(sem("ml_s"), NMU)
            pe.sem_inc(sem("ta_done"), 2 * NCA)
            pe.wait_ge(sem("g_col"), 2)
            pe.wait_ge(sem("ml_one"), 3)
            pe.wait_ge(sem("qa_evac1"), NQA + 2)
            with pe.Fori(0, H_A) as i:
                def score(u):
                    h, sb, t0, n, diag = MU[u]
                    pe.wait_ge(sem("ml_p"), NMU * i + u + 1)
                    s, t = slice(sb * P, sb * P + P), slice(t0, t0 + n)
                    three(pe, PS[u % 2][:, 0:n], KH[:, s], KL[:, s], QH[:, t], QL[:, t], True, True)\
                        .then_inc(sem("ml_s"), 1)

                def fill(n):
                    j, h = n // 2, n % 2
                    pe.wait_ge(w_split, B_TA + 4 * i + j + 1)
                    pe.wait_ge(sem("ta_evac"), 2 * NCA * i + n + 1)
                    half_chunk(pe, cseg[(B_TA + j) % 2], h, 6 + h).then_inc(sem("ta_done"), 1)

                fill(0)
                fill(1)
                pe.wait_ge(sem("ml_split"), 2 * i + 4)
                score(0)
                for u, (h, sb, t0, n, diag) in enumerate(MU):
                    if u + 1 < NMU:
                        score(u + 1)
                    if 2 <= u + 2 < 2 * NCA:
                        fill(u + 2)
                    if u == 0:
                        pe.wait_ge(sem("ml_split_v"), i + 2)
                    pe.wait_ge(sem("ml_pl"), NMU * i + u + 1)
                    for tl in range((t0 - 512 * h) // P, 4):
                        if sb == 0:
                            pe.wait_ge(sem("ml_nev"), 8 * i + 4 * h + tl + 1)
                        t = slice(512 * h + tl * P - t0, 512 * h + tl * P - t0 + P)
                        last = three(pe, PS[2 + tl][:, 0:VW], PHt[u % 2][:, t], PLt[u % 2][:, t],
                                     VH[:, sb, :], VL[:, sb, :], sb == 0, sb == 4 * h + tl)
                    last.then_inc(sem("ml_pv"), 1)

        def ml_scalar(act):
            act.wait_ge(sem("g_col"), 2)
            act.wait_ge(sem("qa_conv"), 4 * NQA + 8)
            for j in range(2):
                act.wait_ge(sem(f"qa_out{j}"), 8 * NQA + 16)
            for j in range(2):
                act.sem_inc(sem(f"ta_out{j}"), 16)
            for tl in range(4):
                act.sem_inc(sem(f"ml_out{tl}"), 16)
            with act.Fori(0, H_A) as i:
                def decay(u):
                    h, sb, t0, n, diag = MU[u]
                    act.wait_ge(sem("ml_p"), NMU * i + u + 1)
                    nc.scalar.activation(m_D[u % 2][:, 0:n], m_M[:, t0:t0 + n], ACT.Exp,
                                         bias=a_head[:, sb:sb + 1], scale=-1.0).then_inc(sem("ml_d"), 1)

                def evac(n):
                    j, h = n // 2, n % 2
                    act.wait_ge(sem("ta_done"), 2 * NCA * i + n + 1 + 2 * NCA)
                    act.wait_ge(sem(f"ta_out{h}"), 16 * NCA * i + 16 * j + 16)
                    apart(act, "passed_act")
                    nc.scalar.activation(ta_stage[h][:, 0:512], PS[6 + h][:, :], ACT.Identity,
                                         bias=bt_col[:, bass.ds(4 * i + j, 1)]).then_inc(sem("ta_evac"), 1)
                    act.wait_ge(sem("ta_evac"), 2 * NCA * i + n + 3)
                    act.dma_start(s_t[4 * i + j][:, 512 * h:512 * h + 512], ta_stage[h][:, 0:512])\
                        .then_inc(sem(f"ta_out{h}"), 16)
                    if h:
                        hi_piece(act, B_TA + 2 + j, 4 * i, cseg[(B_TA + j) % 2][0])

                act.wait_ge(sem("ml_in"), 48 * i + 48)
                act.wait_ge(sem("ml_s"), NMU * i + NMU)
                nc.scalar.copy(QH, m_q).then_inc(sem("ml_hi"), 1)
                nc.scalar.copy(KH, m_k).then_inc(sem("ml_hi"), 1)
                act.wait_ge(sem("ml_pv"), NMU * i + 2)
                nc.scalar.copy(VH[:, :, 0:DV_A], m_v).then_inc(sem("ml_hi"), 1)
                act.wait_ge(sem("ml_M_in"), 16 * i + 16)
                act.wait_ge(sem("ml_head"), 2 * i + 2)
                decay(0)
                for u, (h, sb, t0, n, diag) in enumerate(MU):
                    if u + 1 < NMU:
                        decay(u + 1)
                    if u < 2 * NCA:
                        evac(u)
                    act.wait_ge(sem("ml_p"), NMU * i + u + 3)
                    act.wait_ge(sem("ml_pv"), NMU * i + u + 1)
                    nc.scalar.copy(PHt[u % 2][:, 0:n], m_P[u % 2][:, 0:n]).then_inc(sem("ml_ph"), 1)
                    if u and MU[u - 1][4]:
                        store_h(act, i, MU[u - 1])
                store_h(act, i, MU[-1])

        def store_h(act, i, unit):
            h, sb, t0, n, diag = unit
            act.wait_ge(sem("ml_h"), 8 * i + sb + 9)
            act.dma_start(s_h[sb * P:sb * P + P, bass.ts(i, DV_A)], m_H[sb % 4]).then_inc(sem(f"ml_out{sb % 4}"), 16)

        def ml_vector(dve):
            dve.sem_inc(sem("ml_p"), 2)
            dve.sem_inc(sem("ml_nev"), 4)
            dve.sem_inc(sem("ml_h"), 8)
            dve.wait_ge(sem("g_col"), 2)
            dve.wait_ge(sem("ta_out1"), 16)
            with dve.Fori(0, H_A) as i:
                dve.wait_ge(sem("ml_d"), NMU * i + NMU)
                dve.wait_ge(sem("ml_h"), 8 * i + 8)
                nc.vector.tensor_copy(a_head, a_col[:, i, :]).then_inc(sem("ml_head"), 1)
                nc.vector.tensor_copy(e_head, e_col[:, i, :]).then_inc(sem("ml_head"), 1)
                dve.wait_ge(sem("ml_hi"), 3 * i + 3)
                nc.vector.tensor_tensor(VL[:, :, 0:DV_A], m_v, VH[:, :, 0:DV_A], ALU.subtract)\
                    .then_inc(sem("ml_split_v"), 1)
                dve.wait_ge(sem("ml_head"), 2 * i + 2)

                def tile_out(u):
                    h, sb, t0, n, diag = MU[u]
                    tl = sb - 4 * h
                    dve.wait_ge(sem("ml_pv"), NMU * i + u + 3)
                    bank = PS[2 + tl]
                    nc.vector.tensor_scalar(small[:, 0:1], bank[:, DV_A:DV_A + 1], -1.0, e_head[:, sb:sb + 1],
                                            ALU.mult, ALU.max).then_inc(sem("ml_den"), 1)
                    dve.wait_ge(sem("ml_den"), 24 * i + 3 * sb + 1)
                    nc.vector.tensor_tensor(small[:, 0:1], bank[:, DV_A:DV_A + 1], small[:, 0:1], ALU.max)\
                        .then_inc(sem("ml_den"), 1)
                    dve.wait_ge(sem("ml_den"), 24 * i + 3 * sb + 2)
                    nc.vector.reciprocal(small[:, 1:2], small[:, 0:1]).then_inc(sem("ml_den"), 1)
                    dve.wait_ge(sem("ml_den"), 24 * i + 3 * sb + 3)
                    dve.wait_ge(sem(f"ml_out{tl}"), 32 * i + 16 * h + 16)
                    nc.vector.tensor_scalar(m_H[tl], bank[:, 0:DV_A], small[:, 1:2], None, ALU.mult)\
                        .then_inc(sem("ml_h"), 1)
                    dve.wait_ge(sem("ml_h"), 8 * i + sb + 9)
                    dve.sem_inc(sem("ml_nev"), 1)

                dg = 0
                for u, (h, sb, t0, n, diag) in enumerate(MU):
                    dve.wait_ge(sem("ml_s"), NMU * i + u + 1 + NMU)
                    dve.wait_ge(sem("ml_d"), NMU * i + u + 1 + NMU)
                    if diag:
                        dg += 1
                        dve.wait_ge(sem("ml_mask"), 8 * i + dg)
                    nc.vector.scalar_tensor_tensor(out=m_P[u % 2][:, 0:n], in0=PS[u % 2][:, 0:n],
                                                   scalar=DK_A ** -0.5, in1=m_D[u % 2][:, 0:n],
                                                   op0=ALU.mult, op1=ALU.mult).then_inc(sem("ml_p"), 1)
                    dve.wait_ge(sem("ml_ph"), NMU * i + u + 1)
                    nc.vector.tensor_tensor(PLt[u % 2][:, 0:n], m_P[u % 2][:, 0:n], PHt[u % 2][:, 0:n],
                                            ALU.subtract).then_inc(sem("ml_pl"), 1)
                    if u and MU[u - 1][4]:
                        tile_out(u - 1)
                tile_out(NMU - 1)

        SB_SCALE = DH_B ** -0.5
        A0 = W0
        b_q, b_k = fv(A0 + 11264, 1024), fv(A0 + 12288, 1024)
        b_v = FP[:, A0 + 2048:A0 + 3072].rearrange("p (s n) -> p s n", s=TT)
        z_t = [fv(A0 + 3072 + 512 * j, 512) for j in range(4)]
        sp_t = [fv(A0 + 5120 + 512 * j, 512) for j in range(4)]
        ag_t = [fv(A0 + 7168 + 512 * j, 512) for j in range(2)]
        yo_t = [fv(A0 + 8192 + 512 * j, 512) for j in range(2)]
        tb_stage = [fv(A0 + 9216 + 512 * j, 512) for j in range(2)]
        hn_h, hn_o, mhg_t = fv(A0 + 10240, 1024), fv(A0, 1024), fv(A0 + 1024, 1024)
        BQH, BQL, BKH, BKL = (rv(R2 + 12288 + 1024 * n, 1024) for n in range(4))
        BVH, BVL = (rv(R2 + 1024 * n, 1024) for n in range(2))
        SPH = [rv(R2 + 6144 + 512 * j, 512) for j in range(3)]
        SPL = [rv(R2 + 7680 + 512 * j, 512) for j in range(3)]
        WH = [rv(R2 + 9216 + 512 * j, 512) for j in range(3)]
        WL = [rv(R2 + 10752 + 512 * j, 512) for j in range(3)]
        LAG_TRI, LAG_W, LAG_LOW, LAG_AV = 3, 4, 5, 6
        STEPS = NAU + LAG_AV
        NCB = (NTC - NTA) // H_B
        FS = 4
        FILLED = {FS * n + FS: n for n in range(2 * NCB)}
        TR_AT = 2 * NCB * FS

        def ndiag(n):
            return sum(1 for a in AU[:n] if a[4])

        def at_sync(sp):
            def qkv(i):
                sp.dma_start(b_q, s_t[i + TC_Q]).then_inc(sem("at_in"), 16)
                sp.dma_start(b_k, s_t[i + TC_K]).then_inc(sem("at_in"), 16)
                sp.dma_start(b_v, s_nat[:, bass.ds(i * DH_B + V_B, DH_B)].rearrange("(s p) n -> p s n", p=P))\
                    .then_inc(sem("at_in"), 16)

            def beside(i):
                load_at(sp, B_TB, 2 * i, 0, 1)
                sp.wait_ge(sem("hn_tr"), i + 1)
                sp.dma_start(hn_h, s_h[bass.ts(i, P), :]).then_inc(sem("hn_in"), 16)
                sp.wait_ge(sem("hn_out"), 16 * i + 16)
                sp.dma_start(hn_o, s_nat[bass.ts(i, P), O_A:O_A + 1024]).then_inc(sem("hn_oin"), 16)
                load_at(sp, B_TB, 2 * i, 1, 2)

            sp.wait_ge(sem("ml_split_v"), H_A + 1)
            for h in range(2):
                sp.wait_ge(sem(f"ta_out{h}"), 16 * (TC_K + 1) + 16)
            qkv(0)
            for tl in range(4):
                sp.wait_ge(sem(f"ml_out{tl}"), 16 * 2 * H_A + 16)
            sp.wait_ge(sem("ml_p"), NMU * H_A + 2)
            sp.wait_ge(sem("ml_pl"), NMU * H_A)
            for h in range(2):
                sp.wait_ge(sem(f"ta_out{h}"), 16 * NTA + 16)
            sp.dma_start(mhg_t, mh_g.partition_broadcast(P)).then_inc(sem("hn_g"), 16)
            with sp.Fori(0, H_B - 1) as i:
                beside(i)
                sp.wait_ge(sem("at_split"), 3 * i + 6)
                qkv(i + 1)
            beside(H_B - 1)

        def at_pool(pool):
            def split(i, n):
                src, hi, lo = [(b_q, BQH, BQL), (b_k, BKH, BKL),
                               (b_v, BVH.rearrange("p (s n) -> p s n", s=TT),
                                BVL.rearrange("p (s n) -> p s n", s=TT))][n]
                pool.wait_ge(sem("at_hi"), 3 * i + n + 1)
                nc.gpsimd.tensor_tensor(lo, src, hi, ALU.subtract).then_inc(sem("at_split"), 1)

            def head(i, more):
                for s in range(STEPS):
                    if s < NAU and AU[s][4]:
                        pool.wait_ge(sem("at_z"), NAU * i + s + 3)
                        apart(pool, "passed_pool")
                        nc.gpsimd.affine_select(out=z_t[s % 4][:, 0:P], in_=z_t[s % 4][:, 0:P],
                                                compare_op=ALU.is_gt, fill=-1e30, base=0, pattern=[[1, P]],
                                                channel_multiplier=-1).then_inc(sem("at_mask"), 1)
                    if 0 <= s - 2 < NAU:
                        u = s - 2
                        n = AU[u][3]
                        pool.wait_ge(sem("at_sph"), NAU * i + u + 1)
                        nc.gpsimd.tensor_tensor(SPL[u % 3][:, 0:n], sp_t[u % 4][:, 0:n], SPH[u % 3][:, 0:n],
                                                ALU.subtract).then_inc(sem("at_spl"), 1)
                    if s == 3:
                        split(i, 2)
                    if s == 9:
                        lo_piece(pool, B_TB + 2, 2 * i, *cseg[B_TB % 2])
                    if s in (14, 15) and more:
                        split(i + 1, s - 14)
                lo_piece(pool, B_TB + 3, 2 * i, *cseg[(B_TB + 1) % 2])

            pool.sem_inc(sem("at_split"), 3)
            split(0, 0)
            split(0, 1)
            with pool.Fori(0, H_B - 1) as i:
                head(i, True)
            head(H_B - 1, False)

        def at_tensor(pe):
            pe.sem_inc(sem("at_pv"), NAU)
            pe.sem_inc(sem("at_s"), NAU)
            pe.sem_inc(sem("at_tric"), 3)
            pe.sem_inc(sem("tb_done"), 2 * NCB)
            pe.sem_inc(sem("hn_tr"), 1)
            pe.wait_ge(sem("ml_nev"), 8 * H_A + 4)
            pe.wait_ge(sem("ta_evac"), 2 * NTA + 2)

            def head(i):
                for s in range(STEPS):
                    if s < NAU:
                        h, sb, t0, n, diag = AU[s]
                        if s == 0:
                            pe.wait_ge(sem("at_split"), 3 * i + 5)
                        pe.wait_ge(sem("at_z"), NAU * i + s + 1)
                        ks, t = slice(sb * P, sb * P + P), slice(t0, t0 + n)
                        three(pe, PS[s % 2][:, 0:n], BKH[:, ks], BKL[:, ks], BQH[:, t], BQL[:, t], True, True)\
                            .then_inc(sem("at_s"), 1)
                    if 0 <= s - LAG_TRI < NAU:
                        u = s - LAG_TRI
                        h, sb, t0, n, diag = AU[u]
                        first = sb == 4 * h + 3
                        c = slice(t0 - 512 * h, 512)
                        pe.wait_ge(sem("at_spl"), NAU * i + u + 1)
                        nc.tensor.matmul(PS[2 + h][:, c], TRI, SPH[u % 3][:, 0:n], start=first, stop=False,
                                         skip_group_check=True)
                        nc.tensor.matmul(PS[2 + h][:, c], TRI, SPL[u % 3][:, 0:n], start=False, stop=True,
                                         skip_group_check=True).then_inc(sem("at_tri"), 1)
                    if s < 2 * NCB * FS:
                        n = s // FS
                        j, fh = n // 2, n % 2
                        if s % FS == 0:
                            pe.wait_ge(w_split, B_TB + 2 * i + j + 1)
                            pe.wait_ge(sem("tb_evac"), 6 * i + n + 1)
                        wh, wl = cseg[(B_TB + j) % 2]
                        for k in range(KC // FS * (s % FS), KC // FS * (s % FS + 1)):
                            c, t = slice(k * P, k * P + P), slice(fh * 512, fh * 512 + 512)
                            last = three(pe, PS[6 + fh][:, :], wh[:, c], wl[:, c], XH[:, k, t], XL[:, k, t],
                                         k == 0, k == KC - 1)
                        if s % FS == FS - 1:
                            last.then_inc(sem("tb_done"), 1)
                    if 0 <= s - LAG_AV < NAU:
                        u = s - LAG_AV
                        h, sb, t0, n, diag = AU[u]
                        first = sb == 4 * h + 3
                        if u == 0:
                            pe.wait_ge(sem("at_split"), 3 * i + 6)
                        if first:
                            pe.wait_ge(sem("at_yev"), 2 * i + h + 1)
                        pe.wait_ge(sem("at_wl"), NAU * i + u + 1 + 1)
                        v = slice(sb * P, sb * P + P)
                        three(pe, PS[4 + h][:, t0 - 512 * h:512], BVH[:, v], BVL[:, v], WH[u % 3][:, 0:n],
                              WL[u % 3][:, 0:n], first, sb == 0, skip=True).then_inc(sem("at_pv"), 1)
                    if s >= TR_AT:
                        b = s - TR_AT
                        pe.wait_ge(sem("hn_y"), 4 * i + 2 * b + 2)
                        pe.wait_ge(sem("tb_evac"), 6 * i + 4 + b + 1)
                        for k in range(4):
                            c = (4 * b + k) * P
                            last = nc.tensor.transpose(PS[6 + b][:, k * P:k * P + P], hn_h[:, c:c + P], ident)
                        last.then_inc(sem("hn_tr" if b else "hn_tr0"), 1)
                    if 0 <= s - LAG_TRI < NAU:
                        u = s - LAG_TRI
                        h, sb, t0, n, diag = AU[u]
                        c = slice(t0 - 512 * h, 512)
                        pe.wait_ge(sem("at_arg"), NAU * i + u + 1 + 1)
                        nc.tensor.matmul(PS[2 + h][:, c], TRIC, SPH[u % 3][:, 0:n], start=False, stop=False,
                                         skip_group_check=True)
                        nc.tensor.matmul(PS[2 + h][:, c], TRIC, SPL[u % 3][:, 0:n], start=False, stop=True,
                                         skip_group_check=True).then_inc(sem("at_tric"), 1)

            with pe.Fori(0, H_B) as i:
                head(i)

        def at_scalar(act):
            act.sem_inc(sem("at_z"), 2)
            act.sem_inc(sem("hn_out"), 16)
            for h in range(2):
                act.sem_inc(sem(f"tb_out{h}"), 16)
                act.sem_inc(sem(f"at_out{h}"), 16)

            def round_qk(i, dst, src):
                act.wait_ge(sem("at_in"), 48 * i + 48)
                act.wait_ge(sem("at_s"), NAU * i + NAU)
                nc.scalar.copy(dst, src).then_inc(sem("at_hi"), 1)

            def head(i, more):
                for s in range(STEPS):
                    if s < NAU:
                        n = AU[s][3]
                        act.wait_ge(sem("at_s"), NAU * i + s + 1 + NAU)
                        if s >= 4:
                            act.wait_ge(sem("at_arg"), NAU * i + s - 3 + 1)
                        else:
                            act.wait_ge(sem("at_arg"), NAU * i + 1)
                        nc.scalar.activation(z_t[s % 4][:, 0:n], PS[s % 2][:, 0:n], ACT.Copy, scale=SB_SCALE)\
                            .then_inc(sem("at_z"), 1)
                    if s == 2:
                        act.wait_ge(sem("at_pv"), NAU * i + NAU)
                        nc.scalar.copy(BVH.rearrange("p (s n) -> p s n", s=TT), b_v).then_inc(sem("at_hi"), 1)
                    if s in (13, 14) and more:
                        round_qk(i + 1, *((BQH, b_q), (BKH, b_k))[s - 13])
                    if s == 4:
                        act.wait_ge(sem("hn_ve"), i + 1)
                        nc.scalar.activation(ve[:, 0:4], ve[:, 0:4], ACT.Ln).then_inc(sem("hn_sd"), 1)
                    if s == 5:
                        act.wait_ge(sem("hn_sd"), 2 * i + 1)
                        nc.scalar.activation(rstd[:, 0:4], ve[:, 0:4], ACT.Exp, scale=-0.5).then_inc(sem("hn_sd"), 1)
                    if s == 8:
                        act.wait_ge(sem("tb_done"), 2 * NCB + 4 * i + 2)
                        hi_piece(act, B_TB + 2, 2 * i, cseg[B_TB % 2][0])
                    if 0 <= s - 1 < NAU:
                        u = s - 1
                        n = AU[u][3]
                        act.wait_ge(sem("at_cl"), NAU * i + u + 1)
                        nc.scalar.activation(sp_t[u % 4][:, 0:n], sp_t[u % 4][:, 0:n], ACT.Exp)\
                            .then_inc(sem("at_ex"), 1)
                    if 0 <= s - LAG_W < NAU:
                        u = s - LAG_W
                        n = AU[u][3]
                        act.wait_ge(sem("at_arg"), NAU * i + u + 1 + 1)
                        nc.scalar.activation(ag_t[u % 2][:, 0:n], ag_t[u % 2][:, 0:n], ACT.Exp)\
                            .then_inc(sem("at_w"), 1)
                    if 0 <= s - 1 < NAU:
                        u = s - 1
                        n = AU[u][3]
                        act.wait_ge(sem("at_ex"), NAU * i + u + 1)
                        nc.scalar.activation(sp_t[u % 4][:, 0:n], sp_t[u % 4][:, 0:n], ACT.Ln, bias=1.0)\
                            .then_inc(sem("at_ln"), 1)
                    if 0 <= s - LAG_W < NAU:
                        u = s - LAG_W
                        n = AU[u][3]
                        act.wait_ge(sem("at_w"), NAU * i + u + 1)
                        act.wait_ge(sem("at_pv"), NAU * i + max(u - 2, 0) + NAU)
                        nc.scalar.copy(WH[u % 3][:, 0:n], ag_t[u % 2][:, 0:n]).then_inc(sem("at_wh"), 1)
                    if s - 1 in FILLED:
                        n = FILLED[s - 1]
                        act.wait_ge(sem("tb_evac"), 6 * i + n + 3)
                        act.dma_start(s_t[2 * i + (NTA + n // 2)][:, 512 * (n % 2):512 * (n % 2) + 512], tb_stage[n % 2])\
                            .then_inc(sem(f"tb_out{n % 2}"), 16)
                    if s == 11:
                        act.wait_ge(sem("at_yev"), 2 * i + 3)
                        act.dma_start(s_yb[i][:, 0:512], yo_t[0]).then_inc(sem("at_out0"), 16)
                act.wait_ge(sem("tb_done"), 2 * NCB + 4 * i + 4)
                hi_piece(act, B_TB + 3, 2 * i, cseg[(B_TB + 1) % 2][0])
                act.wait_ge(sem("tb_evac"), 6 * i + 8)
                act.dma_start(s_ya[:, :, bass.ts(i, P)].rearrange("k p n -> p k n"),
                              hn_o.rearrange("p (k n) -> p k n", k=KC)).then_inc(sem("hn_out"), 16)
                act.wait_ge(sem("at_yev"), 2 * i + 4)
                act.dma_start(s_yb[i][:, 512:1024], yo_t[1]).then_inc(sem("at_out1"), 16)

            round_qk(0, BQH, b_q)
            round_qk(0, BKH, b_k)
            with act.Fori(0, H_B - 1) as i:
                head(i, True)
            head(H_B - 1, False)

        def at_vector(dve):
            dve.sem_inc(sem("at_yev"), 2)
            dve.sem_inc(sem("at_arg"), 1)
            dve.sem_inc(sem("at_wl"), 1)
            dve.sem_inc(sem("tb_evac"), 2)
            st = small[:, 0:24].rearrange("p (h s) -> p h s", h=H_A)
            m = small[:, 24:32].rearrange("p (h s) -> p h s", h=H_A)
            with dve.Fori(0, H_B) as i:
                def evac(n):
                    j, h = n // 2, n % 2
                    dve.wait_ge(sem("tb_done"), 4 * i + n + 1 + 2 * NCB)
                    dve.wait_ge(sem(f"tb_out{h}"), 32 * i + 16 * j + 16)
                    nc.vector.tensor_scalar(tb_stage[h], PS[6 + h][:, :], bt_col[:, bass.ds(2 * i + (NTA + j), 1)], None,
                                            ALU.add).then_inc(sem("tb_evac"), 1)

                for s in range(STEPS):
                    if s == 3:
                        dve.wait_ge(sem("hn_in"), 16 * i + 16)
                        for h in range(H_A):
                            nc.vector.bn_stats(st[:, h, :], hn_h[:, h * DV_A:(h + 1) * DV_A]).then_inc(sem("hn_st"), 1)
                        dve.wait_ge(sem("hn_st"), 4 * i + 4)
                        apart(dve, "passed_dve")
                        for h in range(H_A):
                            nc.vector.bn_aggr(m[:, h, :], st[:, h, :]).then_inc(sem("hn_mv"), 1)
                        dve.wait_ge(sem("hn_mv"), 4 * i + 4)
                        nc.vector.tensor_scalar(ve[:, 0:4], m[:, :, 1], EPS, None, ALU.add).then_inc(sem("hn_ve"), 1)
                    if 0 <= s - 2 < NAU:
                        u = s - 2
                        n = AU[u][3]
                        dve.wait_ge(sem("at_ln"), NAU * i + u + 1)
                        nc.vector.tensor_tensor(sp_t[u % 4][:, 0:n], sp_t[u % 4][:, 0:n], z_t[u % 4][:, 0:n], ALU.max)\
                            .then_inc(sem("at_sp"), 1)
                    if 0 <= s - LAG_LOW < NAU:
                        u = s - LAG_LOW
                        n = AU[u][3]
                        dve.wait_ge(sem("at_wh"), NAU * i + u + 1)
                        nc.vector.tensor_tensor(WL[u % 3][:, 0:n], ag_t[u % 2][:, 0:n], WH[u % 3][:, 0:n],
                                                ALU.subtract).then_inc(sem("at_wl"), 1)
                    if 0 <= s - 2 < NAU:
                        u = s - 2
                        n = AU[u][3]
                        dve.wait_ge(sem("at_sp"), NAU * i + u + 1)
                        dve.wait_ge(sem("at_tric"), NAU * i + u + 1)
                        nc.vector.tensor_copy(SPH[u % 3][:, 0:n], sp_t[u % 4][:, 0:n]).then_inc(sem("at_sph"), 1)
                    if 0 <= s - LAG_TRI < NAU:
                        u = s - LAG_TRI
                        h, sb, t0, n, diag = AU[u]
                        dve.wait_ge(sem("at_tri"), NAU * i + u + 1)
                        dve.wait_ge(sem("at_wl"), NAU * i + max(u - 1, 0) + 1)
                        nc.vector.tensor_tensor(ag_t[u % 2][:, 0:n], z_t[u % 4][:, 0:n],
                                                PS[2 + h][:, t0 - 512 * h:512], ALU.subtract).then_inc(sem("at_arg"), 1)
                    if s in FILLED:
                        evac(FILLED[s])
                    if s < NAU:
                        n = AU[s][3]
                        dve.wait_ge(sem("at_z"), NAU * i + s + 3)
                        if AU[s][4]:
                            dve.wait_ge(sem("at_mask"), 8 * i + ndiag(s + 1))
                        if s >= 4:
                            dve.wait_ge(sem("at_spl"), NAU * i + s - 3)
                        nc.vector.tensor_scalar(sp_t[s % 4][:, 0:n], z_t[s % 4][:, 0:n], 80.0, None, ALU.min)\
                            .then_inc(sem("at_cl"), 1)
                    if s == 6:
                        dve.wait_ge(sem("hn_g"), 16)
                        for h in range(H_A):
                            c = slice(h * DV_A, (h + 1) * DV_A)
                            nc.vector.scalar_tensor_tensor(out=hn_h[:, c], in0=hn_h[:, c], scalar=m[:, h, 0:1],
                                                           in1=mhg_t[:, c], op0=ALU.subtract, op1=ALU.mult)\
                                .then_inc(sem("hn_c"), 1)
                    if s == 8:
                        dve.wait_ge(sem("hn_sd"), 2 * i + 2)
                        dve.wait_ge(sem("hn_oin"), 16 * i + 16)
                        dve.wait_ge(sem("hn_c"), 4 * i + 4)
                        for h in range(H_A):
                            c = slice(h * DV_A, (h + 1) * DV_A)
                            nc.vector.scalar_tensor_tensor(out=hn_h[:, c], in0=hn_h[:, c], scalar=rstd[:, h:h + 1],
                                                           in1=hn_o[:, c], op0=ALU.mult, op1=ALU.mult)\
                                .then_inc(sem("hn_y"), 1)
                    if s == 10:
                        dve.wait_ge(sem("at_pv"), NAU * i + 4 + NAU)
                        dve.wait_ge(sem("at_out0"), 16 * i + 16)
                        nc.vector.tensor_copy(yo_t[0], PS[4][:, :]).then_inc(sem("at_yev"), 1)
                    if s == TR_AT + 1:
                        dve.wait_ge(sem("hn_tr0"), i + 1)
                        dve.wait_ge(sem("hn_y"), 4 * i + 4)
                        nc.vector.tensor_copy(hn_o[:, 0:512], PS[6][:, :]).then_inc(sem("tb_evac"), 1)
                dve.wait_ge(sem("hn_tr"), i + 2)
                nc.vector.tensor_copy(hn_o[:, 512:1024], PS[7][:, :]).then_inc(sem("tb_evac"), 1)
                dve.wait_ge(sem("at_pv"), NAU * i + NAU + NAU)
                dve.wait_ge(sem("at_out1"), 16 * i + 16)
                nc.vector.tensor_copy(yo_t[1], PS[5][:, :]).then_inc(sem("at_yev"), 1)

        YH = RP[:, 0:8192].rearrange("p (a k n) -> p a k n", a=2, k=KC)
        YL = RP[:, 8192:16384].rearrange("p (a k n) -> p a k n", a=2, k=KC)
        MH = RP[:, R2:R2 + 8192].rearrange("p (k n) -> p k n", k=KC)
        ML = RP[:, R2 + 8192:R2 + 16384].rearrange("p (k n) -> p k n", k=KC)
        BR0 = W0
        y_raw = FP[:, BR0:BR0 + 8192].rearrange("p (a k n) -> p a k n", a=2, k=KC)
        bg_t = [[fv(BR0 + 8192 + 1024 * j + 512 * a, 512) for a in range(2)] for j in range(2)]
        br_t = [[fv(BR0 + 10240 + 1024 * j + 512 * a, 512) for a in range(2)] for j in range(2)]
        Y_PARTS = [(a, slice(4 * kh, 4 * kh + 4)) for a in range(2) for kh in range(2)]

        def br_sync(sp):
            for h in range(2):
                sp.wait_ge(sem(f"at_out{h}"), 16 * H_B + 16)
                sp.wait_ge(sem(f"tb_out{h}"), 16 * (NTC - NTA) + 16)
            sp.wait_ge(sem("hn_out"), 16 * H_B + 16)
            sp.wait_ge(sem("at_wl"), NAU * H_B + 1)
            for h in range(2):
                t = slice(512 * h, 512 * h + 512)
                for n, (a, ks) in enumerate(Y_PARTS):
                    if h:
                        sp.wait_ge(sem("br_ylo"), 2 * n + 2)
                    sp.dma_start(y_raw[:, a, ks, :], (s_yb if a else s_ya)[ks, :, t].rearrange("k p n -> p k n"))\
                        .then_inc(sem(f"br_yin{n}"), 16)
                for c in range(KC):
                    m = KC * h + c
                    j = m % 2
                    if m >= 2:
                        sp.wait_ge(sem("br_m"), 3 * (m - 1))
                    for a, tc in ((0, TC_GA), (1, TC_GB)):
                        sp.dma_start(bg_t[j][a], s_t[tc + c][:, t]).then_inc(sem(f"br_gin{j}"), 16)
                    load_at(sp, B_BR, 0, 2 * m, 2 * m + 2)

        def br_pool(pool):
            for n in range(2, 2 * 2 * KC):
                lo_piece(pool, B_BR + n, 0, *cseg[(B_BR + n) % 2])

        def br_tensor(pe):
            pe.wait_ge(sem("at_yev"), 2 * H_B + 2)
            pe.wait_ge(sem("tb_evac"), 6 * H_B + 2)
            for m in range(2 * KC):
                h, j = m // KC, m % 2
                for a in range(2):
                    wh, wl = cseg[(B_BR + a) % 2]
                    pe.wait_ge(w_split, B_BR + 2 * m + a + 1)
                    if m >= 2:
                        pe.wait_ge(sem("br_m"), 3 * (m - 1))
                    for k in range(KC):
                        if m % KC == 0 and k % 2 == 0:
                            pe.wait_ge(sem("br_ylo"), 8 * h + 4 * a + k // 2 + 1)
                        c = slice(k * P, k * P + P)
                        last = three(pe, PS[2 * j + a][:, :], wh[:, c], wl[:, c], YH[:, a, k, :], YL[:, a, k, :],
                                     k == 0, k == KC - 1)
                    last.then_inc(sem("br_done"), 1)

        def br_scalar(act):
            act.wait_ge(sem("at_pv"), NAU * H_B + NAU)
            act.wait_ge(sem("tb_done"), 4 * H_B + 2 * NCB)

            def round_y(h, a):
                if h:
                    act.wait_ge(sem("br_done"), 2 * KC - 1 + a)
                for k in range(0, KC, 2):
                    act.wait_ge(sem(f"br_yin{2 * a + k // 4}"), 16 * h + 16)
                    nc.scalar.copy(YH[:, a, k:k + 2, :], y_raw[:, a, k:k + 2, :]).then_inc(sem("br_yhi"), 1)
            for m in range(2 * KC):
                h, c, j = m // KC, m % KC, m % 2
                if c == 0:
                    if h == 0:
                        round_y(h, 0)
                    round_y(h, 1)
                act.wait_ge(sem(f"br_gin{j}"), 32 * (m // 2) + 32)
                for a in range(2):
                    nc.scalar.activation(bg_t[j][a], bg_t[j][a], ACT.Sigmoid).then_inc(sem("br_sig"), 1)
                    if m < 2 * KC - 1:
                        act.wait_ge(sem("br_done"), 2 * m + a + 1)
                        hi_piece(act, B_BR + 2 + 2 * m + a, 0, cseg[(B_BR + a) % 2][0])
                    if m == KC - 1 and a == 0:
                        round_y(1, 0)
                if m == 2 * KC - 1:
                    act.wait_ge(sem("br_done"), 4 * KC)
                    full_scalar(act, B_MIX, XH, (0, 1))
                act.wait_ge(sem("br_m"), 3 * m + 3)
                nc.scalar.copy(MH[:, c, 512 * h:512 * h + 512], br_t[j][0]).then_inc(sem("br_mhi"), 1)

        def br_vector(dve):
            def split_y(h, a):
                for k in range(0, KC, 2):
                    dve.wait_ge(sem("br_yhi"), 8 * h + 4 * a + k // 2 + 1)
                    nc.vector.tensor_tensor(YL[:, a, k:k + 2, :], y_raw[:, a, k:k + 2, :], YH[:, a, k:k + 2, :],
                                            ALU.subtract).then_inc(sem("br_ylo"), 1)
            for m in range(2 * KC):
                h, c, j = m // KC, m % KC, m % 2
                if c == 0:
                    if h == 0:
                        split_y(h, 0)
                    split_y(h, 1)
                if m >= 2:
                    dve.wait_ge(sem("br_mlo"), m - 1)
                for a in range(2):
                    dve.wait_ge(sem("br_sig"), 2 * m + a + 1)
                    dve.wait_ge(sem("br_done"), 2 * m + a + 1)
                    nc.vector.tensor_tensor(br_t[j][a], PS[2 * j + a][:, :], bg_t[j][a], ALU.mult)\
                        .then_inc(sem("br_m"), 1)
                    if m == KC - 1 and a == 0:
                        split_y(1, 0)
                dve.wait_ge(sem("br_m"), 3 * m + 2)
                nc.vector.tensor_tensor(br_t[j][0], br_t[j][0], br_t[j][1], ALU.add).then_inc(sem("br_m"), 1)
                dve.wait_ge(sem("br_mhi"), m + 1)
                nc.vector.tensor_tensor(ML[:, c, 512 * h:512 * h + 512], br_t[j][0],
                                        MH[:, c, 512 * h:512 * h + 512], ALU.subtract).then_inc(sem("br_mlo"), 1)

        def full_pool(pool, base, hi, lo):
            for k in range(KC):
                lo_piece(pool, base + k, 0, hi[:, k, :], lo[:, k, :])

        def full_scalar(act, base, hi, ks):
            for k in ks:
                hi_piece(act, base + k, 0, hi[:, k, :])

        def full_tensor(pe, q, base, left, right, ready, between):
            (lh, ll), (rh, rl) = left, right

            def product(o, k):
                tt, dh = o // 2, o % 2
                t, c = slice(tt * P, tt * P + P), slice(dh * 512, dh * 512 + 512)
                return three(pe, PS[o % 8][:, :], lh[:, k, t], ll[:, k, t], rh[:, k, c], rl[:, k, c],
                             k == 0, k == KC - 1)
            for s, v in ready:
                pe.wait_ge(s, v)
            for k in range(KC):
                pe.wait_ge(w_split, base + k + 1)
                for o in range(8):
                    last = product(o, k)
                    if k == KC - 1:
                        last.then_inc(sem(q + "done"), 1)
            between()
            for o in range(8, 16):
                pe.wait_ge(sem(q + "evac"), o - 7)
                for k in range(KC):
                    last = product(o, k)
                last.then_inc(sem(q + "done"), 1)

        def mix_scalar(act):
            act.wait_ge(sem("br_mlo"), 2 * KC)
            for tt in range(TT):
                act.dma_start(X[:, tt, :], s_x[:, tt, :]).then_inc(sem(f"x_back{tt % 2}"), 16)
                full_scalar(act, B_MIX, XH, [tt + 2] if tt + 2 < KC else [])
                if tt >= 1:
                    act.wait_ge(sem(f"x_back{(tt - 1) % 2}"), 16 * ((tt - 1) // 2) + 16)
                    scale_x(act, tt - 1)
            act.wait_ge(sem(f"x_back{(TT - 1) % 2}"), 16 * ((TT - 1) // 2) + 16)
            scale_x(act, TT - 1)

        def mix_vector(dve):
            for o in range(16):
                tt, dh = o // 2, o % 2
                xs = X[:, tt, dh * 512:dh * 512 + 512]
                dve.wait_ge(sem("mx_done"), o + 1)
                dve.wait_ge(sem("x_scaled"), TT + tt + 1)
                nc.vector.tensor_tensor(xs, PS[o % 8][:, :], xs, ALU.add).then_inc(sem("mx_evac"), 1)
                if o % 2:
                    ln_stats(dve, 1, tt, sem("mx_evac"), o + 1)
                if o == 7:
                    ln_centre(dve, ln_half(1, 0))
            t_lo(dve, 1, 0, 0)
            ln_centre(dve, ln_half(1, 1))
            t_lo(dve, 1, 1, 4)

        bple_t = raw[1]
        gate_t = [fv(T0 + 512 * j, 512) for j in range(4)]
        pl_t = [fv(T0 + 2048 + 512 * j, 512) for j in range(2)]
        PWH = RP[:, R2:R2 + 8192].rearrange("p (k n) -> p k n", k=KC)
        PWL = RP[:, R2 + 8192:R2 + 16384].rearrange("p (k n) -> p k n", k=KC)

        def ple_sigmoid(act, o):
            act.wait_ge(sem("pg_evac"), o + 1)
            nc.scalar.activation(gate_t[o % 4], gate_t[o % 4], ACT.Sigmoid).then_inc(sem("pg_sig"), 1)

        def ple_sync(sp):
            sp.wait_ge(sem("f_h_lo"), 8 * FI)
            for o in range(16):
                if o >= 2:
                    sp.wait_ge(sem("pg_mul"), o - 1)
                sp.dma_start(pl_t[o % 2], s_ple[o // 2 * P:o // 2 * P + P, o % 2 * 512:o % 2 * 512 + 512])\
                    .then_inc(sem(f"pl_in{o % 2}"), 16)

        def ple_evac(dve, o):
            dve.wait_ge(sem("pg_done"), o + 1)
            if o >= 4:
                dve.wait_ge(sem("pg_add"), o - 3)
            c = slice(o % 2 * 512, o % 2 * 512 + 512)
            nc.vector.tensor_tensor(gate_t[o % 4], PS[o % 8][:, :], bple_t[:, c], ALU.add).then_inc(sem("pg_evac"), 1)

        def ple_multiply(pool, outputs):
            for o in outputs:
                pool.wait_ge(sem("pg_sig"), o + 1)
                pool.wait_ge(sem(f"pl_in{o % 2}"), 16 * (o // 2) + 16)
                nc.gpsimd.tensor_tensor(gate_t[o % 4], gate_t[o % 4], pl_t[o % 2], ALU.mult)\
                    .then_inc(sem("pg_mul"), 1)

        def ple_add(dve, o):
            tt, dh = o // 2, o % 2
            xs = X[:, tt, dh * 512:dh * 512 + 512]
            dve.wait_ge(sem("pg_mul"), o + 1)
            dve.wait_ge(sem("x_scaled"), 3 * TT + tt + 1)
            nc.vector.tensor_tensor(xs, gate_t[o % 4], xs, ALU.add).then_inc(sem("pg_add"), 1)
            if dh:
                ln_stats(dve, 3, tt, sem("pg_add"), o + 1)

        @blk.sync
        def _(sp):
            start_sync(sp)
            with sp.Fori(2, (B_TA + 1) // 2) as j:
                load_pair(sp, j)
            load_at(sp, B_TA, 0, -1, 0)
            ml_sync(sp)
            at_sync(sp)
            br_sync(sp)
            load_at(sp, B_MIX, 0, 0, 1)
            with sp.Fori((B_MIX + AHEAD + 1) // 2, N_PIECES // 2) as j:
                load_pair(sp, j)
            sp.wait_ge(w_split, N_PIECES - 2)
            sp.dma_start(raw[0], w_all[N_PIECES - 1]).then_inc(raw_in[0], 16)
            ple_sync(sp)
            for tt in range(TT):
                if tt == TT - 1:
                    sp.wait_ge(sem("ln_y_v"), 1)
                else:
                    sp.wait_ge(sem("ln_y"), 3 * TT + tt + 1)
                sp.dma_start(out[tt * P:tt * P + P, :], X[:, tt, :]).then_inc(sem("out"), 16)
            sp.wait_ge(sem("out"), 16 * TT)

        @blk.gpsimd
        def _(pool):
            ffn_pool_first(pool, B_FFN1, (0, 1))
            start_pool(pool)
            ffn_pool_first(pool, B_FFN1, (2, 3))
            ffn_pool(pool, B_FFN1)
            ln_offset(pool, 0, range(4))
            nat_pool_first(pool)
            ln_offset(pool, 0, range(4, TT))
            nat_pool(pool)
            for n in (B_IF, B_QA, B_QA + 1):
                lo_piece(pool, n, 0, *cseg[n % 2])
            ml_ones(pool)
            pool.sem_inc(sem("ml_split"), 2)
            chunk_pool(pool, B_QA + 2, NQA)
            ml_pool(pool)
            at_pool(pool)
            br_pool(pool)
            full_pool(pool, B_MIX, XH, XL)
            ffn_pool_first(pool, B_FFN2, (0, 1))
            ln_offset(pool, 1, range(4))
            ffn_pool_first(pool, B_FFN2, (2, 3))
            ln_offset(pool, 1, range(4, TT))
            ffn_pool(pool, B_FFN2)
            ln_offset(pool, 2, range(4))
            for k in range(2):
                lo_piece(pool, B_PLE + k, 0, PWH[:, k, :], PWL[:, k, :])
            ln_offset(pool, 2, range(4, TT))
            for k in range(2, KC):
                lo_piece(pool, B_PLE + k, 0, PWH[:, k, :], PWL[:, k, :])
            ple_multiply(pool, range(8))
            ple_multiply(pool, range(8, 12))
            ln_offset(pool, 3, range(0, 2))
            ple_multiply(pool, range(12, 14))
            ln_offset(pool, 3, range(2, 4))
            ple_multiply(pool, range(14, 16))
            ln_offset(pool, 3, range(4, 6))
            ln_offset(pool, 3, range(6, 7))

        @blk.tensor
        def _(pe):
            ffn_tensor(pe, 0, B_FFN1, [])
            transpose_half(pe, 0, 0, 0, [(sem("const"), 5), (sem("f_prod"), 4 * FI + 2)])
            nat_tensor(pe, lambda: transpose_half(pe, 0, 1, 4, [(sem("f_down_evac"), 16 * FI + 4)]))
            if_tensor(pe)
            ple0_tensor(pe)
            qa_tensor(pe)
            ml_tensor(pe)
            at_tensor(pe)
            br_tensor(pe)
            full_tensor(pe, "mx_", B_MIX, (MH, ML), (XH, XL), [(sem("br_m"), 6 * KC)],
                        lambda: pe.wait_ge(sem("br_mlo"), 2 * KC))
            transpose_half(pe, 1, 0, 0, [(sem("mx_evac"), 12)])

            def rest_of_x(n):
                pe.wait_ge(sem("mx_evac"), 16)
                transpose(pe, 1, range(8 + 4 * n, 12 + 4 * n), 4)
                if n == 1:
                    pe.wait_ge(sem("ln_tr_lo"), 2 * 16)
            ffn_tensor(pe, 1, B_FFN2, [(sem("ln_tr_lo"), 16 + 8)], rest_of_x)
            transpose_half(pe, 2, 0, 0, [(sem("f_prod"), 8 * FI + 2)])
            full_tensor(pe, "pg_", B_PLE, (XH, XL), (PWH, PWL),
                        [(sem("ln_tr_lo"), 32 + 8), (sem("f_down_evac"), 32 * FI + 4)],
                        lambda: (transpose_half(pe, 2, 1, 0, [(sem("pg_evac"), 4)]),
                                 pe.wait_ge(sem("ln_tr_lo"), 3 * 16)))

        @blk.scalar
        def _(act):
            start_scalar(act)
            ln_loads(act, 0, [(sem("const"), 5)])

            def two_tiles(n):
                act.wait_ge(sem("x_in"), 16)
                scale_x(act, 2 * n)
                scale_x(act, 2 * n + 1)
            ffn_scalar(act, 0, B_FFN1, lambda: ln_scale(act, ln_half(0, 0)), two_tiles)
            nat_scalar_first(act, [(sem("f_unit_done"), 4 * FI + 4)])
            t_hi(act, 0, 0, 0)
            ln_scale(act, ln_half(0, 1))
            t_hi(act, 0, 1, 4)
            nat_scalar(act)
            if_scalar(act)
            hi_piece(act, B_QA + 1, 0, cseg[(B_QA + 1) % 2][0])
            ple0_scalar(act)
            act.sem_inc(sem("qa_evac0"), 2)
            act.sem_inc(sem("qa_evac1"), 2)
            act.sem_inc(sem("ta_evac"), 2)
            act.sem_inc(sem("ml_d"), NMU)
            gates_scalar(act)
            qa_scalar(act)
            nc.scalar.preload_act_table_set("natural_log_exp_and_others")
            ml_scalar(act)
            at_scalar(act)
            br_scalar(act)
            mix_scalar(act)
            ln_loads(act, 1, [])
            for n in range(2):
                hi_piece(act, B_FFN2 + n, 0, fseg[n][0])
            ln_scale(act, ln_half(1, 0))
            t_hi(act, 1, 0, 0)
            act.wait_ge(sem("mx_done"), 16)
            for n in range(2, 4):
                hi_piece(act, B_FFN2 + n, 0, fseg[n][0])
            ln_scale(act, ln_half(1, 1))
            for tt in range(4):
                scale_x(act, tt)
            t_hi(act, 1, 1, 4)
            for tt in range(4, TT):
                scale_x(act, tt)
            ln_loads(act, 2, [(sem("ln_y"), 2 * TT), (sem("ln_ctr"), 2 * TT)])
            ffn_scalar(act, 1, B_FFN2, lambda: ln_scale(act, ln_half(2, 0)))
            act.wait_ge(sem("f_down_done"), 32 * FI + 16)
            full_scalar(act, B_PLE, PWH, (0, 1))
            t_hi(act, 2, 0, 0)
            ln_scale(act, ln_half(2, 1))
            full_scalar(act, B_PLE, PWH, range(2, KC))
            for tt in range(4):
                scale_x(act, tt)
            act.wait_ge(w_split, N_PIECES - 1)
            act.dma_start(bple_t, b_ple.partition_broadcast(P)).then_inc(sem("bple_in"), 16)
            ln_loads(act, 3, [(sem("ln_y"), 3 * TT), (sem("ln_ctr"), 3 * TT)])
            t_hi(act, 2, 1, 0)
            for o in range(8):
                ple_sigmoid(act, o)
            for tt in range(4, TT):
                scale_x(act, tt)
            ln_scale(act, ln_half(3, 0))
            for o in range(8, 12):
                ple_sigmoid(act, o)
            ln_scale(act, LAST[0])
            for o in range(12, 16):
                ple_sigmoid(act, o)
            ln_scale(act, LAST[1])

        @blk.vector
        def _(dve):
            dve.sem_inc(sem("n_evac"), 8)
            start_vector(dve)
            ffn_vector(dve, 0,
                       lambda tt, v: ln_stats(dve, 0, tt, sem("f_down_evac"), v),
                       lambda h: ln_centre(dve, ln_half(0, 0)) if h == 0 else None)
            t_lo(dve, 0, 0, 0)
            ln_centre(dve, ln_half(0, 1))
            t_lo(dve, 0, 1, 4)
            nat_vector(dve)
            gates_vector(dve)
            dve.sem_inc(sem("ml_split_v"), 1)
            qa_vector(dve)
            ml_vector(dve)
            at_vector(dve)
            br_vector(dve)
            mix_vector(dve)
            ffn_vector(dve, 1,
                       lambda tt, v: ln_stats(dve, 2, tt, sem("f_down_evac"), v),
                       lambda h: ln_centre(dve, ln_half(2, 0)) if h == 0 else None)
            t_lo(dve, 2, 0, 0)
            ln_centre(dve, ln_half(2, 1))
            dve.wait_ge(sem("bple_in"), 16)
            for o in range(4):
                ple_evac(dve, o)
            t_lo(dve, 2, 1, 0)
            for o in range(8):
                ple_add(dve, o)
                if o + 4 < 8:
                    ple_evac(dve, o + 4)
            ln_centre(dve, ln_half(3, 0))
            ple_evac(dve, 8)
            for o in range(8, 16):
                if o + 1 < 16:
                    ple_evac(dve, o + 1)
                ple_add(dve, o)
                if o == 11:
                    ln_centre(dve, LAST[0])
            ln_centre(dve, LAST[1])
            dve.wait_ge(sem("ln_n"), 4 * TT)
            nc.vector.tensor_tensor(X[:, TT - 1, :], X[:, TT - 1, :], lnb_t, ALU.add).then_inc(sem("ln_y_v"), 1)


def lay_out(i):
    import numpy as np
    a = {k: np.asarray(v) for k, v in i.items()}

    def columns(w, step=P):
        n = w.shape[1] // step
        return w.reshape(KC, P, n, step).transpose(2, 1, 0, 3).reshape(n, P, KC * step)

    def ffn(l):
        g, u = columns(a["ffn_wg"][0, l]), columns(a["ffn_wu"][0, l])
        d = a["ffn_wd"][0, l].reshape(FC, P, D)
        return np.stack([g[0::2], u[0::2], g[1::2], u[1::2], d[0::2], d[1::2]], axis=1).reshape(6 * FI, P, PC)

    w = a["w_in"][0]
    b = a["b_in"][0]
    qa, va, oa = slice(0, 1024), slice(1024, 2048), slice(2048, 3072)
    ic, fc = slice(3072, 3076), slice(3076, 3080)
    qb, kb, vb = slice(3080, 4104), slice(4104, 5128), slice(5128, 6152)
    ga, gb = slice(6152, 7176), slice(7176, 8200)
    pair = np.arange(NQA).reshape(2, H_A).T.reshape(-1)
    wif, bif = np.zeros((D, P), w.dtype), np.zeros((P, 1), w.dtype)
    wif[:, 0:H_A], wif[:, 32:32 + H_A] = w[:, ic], w[:, fc]
    bif[0:H_A, 0], bif[32:32 + H_A, 0] = b[ic], b[fc]
    nat = np.concatenate([w[:, va], w[:, vb], w[:, oa]], axis=1)
    nat = nat.reshape(4, 2, P, NG, 512).transpose(3, 0, 2, 1, 4).reshape(4 * NG, P, PC)
    tch = np.concatenate([w[:, qb], w[:, kb], w[:, ga], w[:, gb]], axis=1)
    btc = np.concatenate([b[qb], b[kb], b[ga], b[gb]])
    branches = np.stack([columns(a["w_branch_a"][0]), columns(a["w_branch_b"][0])], axis=1).reshape(2 * KC, P, PC)
    w_all = np.concatenate([
        ffn(0), nat, a["p"][0, 0].T.reshape(2, P, T),
        a["w_ple"][0].reshape(2, P, D), columns(wif), columns(w[:, qa])[pair], columns(tch), branches, branches,
        a["w_mix_out"][0].reshape(KC, P, D), ffn(1), a["w_ple_gate"][0].reshape(KC, P, D)])
    return {
        "w_all": w_all,
        "x_t": a["x"][0].T.reshape(KC, P, T),
        "x_nat": a["x"][0].reshape(TT, P, D).transpose(1, 0, 2),
        "b_t": btc.reshape(NTC, P).T, "b_if": bif, "b_qa": b[qa].reshape(NQA, P)[pair].T,
        "b_nat": np.concatenate([b[va], b[vb], b[oa]]),
        "b_forget": a["b_forget"][0].reshape(H_A, 1),
        "conv_w": a["conv_w"][0].reshape(CONV_W, NQA, P)[:, pair].transpose(2, 1, 0),
        "conv_b": a["conv_b"][0].reshape(NQA, P)[pair].T,
        "mh_g": a["mh_norm_g"][0].reshape(-1),
        "ln_g": a["ln_g"][0], "ln_b": a["ln_b"][0], "b_ple": a["b_ple_gate"][0],
    }


_SCRATCH = [("s_ple", (T, D)), ("s_x", (P, TT, D)), ("s_nat", (T, NAT)), ("s_qa", (NQA, P, T)),
            ("s_t", (NTC, P, T)), ("s_m", (H_A, T)), ("s_h", (T, D)), ("s_ya", (KC, P, T)), ("s_yb", (KC, P, T))]


def kernel(**inputs):
    import numpy as _np
    import concourse.bacc as _bacc
    from concourse.bass_utils import run_bass_kernel_spmd as _run

    nc = _bacc.Bacc("TRN2", target_bir_lowering=False, num_devices=1)
    arrays, args = {}, []
    for name, v in lay_out(inputs).items():
        v = _np.ascontiguousarray(v)
        arrays[f"in_{name}"] = v
        args.append(nc.dram_tensor(f"in_{name}", v.shape, F32, kind="ExternalInput").ap())
    args.append(nc.dram_tensor("out_0", (T, D), F32, kind="ExternalOutput").ap())
    for name, shape in _SCRATCH:
        args.append(nc.dram_tensor(name, shape, F32, kind="Internal").ap())
    build(nc, *args)
    r = _run(nc, [arrays], core_ids=[0])
    return r.results[0]["out_0"].reshape(1, T, D)
```
